# Optimizing a Trainium2 kernel written in Bass

```python
import math
import jax
import jax.numpy as jnp
from jax import lax
import numpy as np

D_MODEL = 2048
BATCH = 1
SEQ = 512
DEPTH = 2

D_MIX = D_MODEL
N_GROUPS = 4
GROUP_W = D_MIX // N_GROUPS
ROPE_THETA = 500000.0
NORM_EPS = 1e-6
Q_BLOCK = 128

RW_HEAD = 64
RW_HEADS = GROUP_W // RW_HEAD
RW_DECAY_LORA = 32
RW_A_LORA = 32
RW_V_LORA = 32
RW_GN_EPS = 64e-5
RW_COLS = 3 * GROUP_W + RW_DECAY_LORA + RW_A_LORA

ML_HEADS = 4
ML_HEAD = GROUP_W // ML_HEADS
ML_CONV = 4
ML_CHUNK = 64
ML_COLS = 4 * GROUP_W + 2 * ML_HEADS

MLA_HEADS = 4
MLA_V = GROUP_W // MLA_HEADS
MLA_NOPE = 128
MLA_ROPE = 64
MLA_QK = MLA_NOPE + MLA_ROPE
MLA_Q_LORA = 384
MLA_KV_LORA = 256
MLA_COLS = MLA_Q_LORA + MLA_KV_LORA + MLA_ROPE

DA_HEADS = 4
DA_V = GROUP_W // DA_HEADS
DA_QK = DA_V // 2
DA_ROT = DA_QK // 4
DA_COLS = 3 * GROUP_W

IN_WIDTHS = (D_MIX, RW_COLS, ML_COLS, MLA_COLS, DA_COLS)
N_IN = sum(IN_WIDTHS)

kernel_name = 'hybrid_rwkv7_mlstm_mla_diffattn_parallel_heads'

def _split(a, widths):
    idx = [int(i) for i in np.cumsum(widths)[:-1]]
    return jnp.split(a, idx, axis=-1)

def rms_norm(x, g, eps=NORM_EPS):
    xf = x.astype(jnp.float32)
    return xf * lax.rsqrt(jnp.mean(xf * xf, -1, keepdims=True) + eps) * g.astype(jnp.float32)

def rope_tables(T, rot_dim):
    inv = ROPE_THETA ** (-jnp.arange(0, rot_dim, 2, dtype=jnp.float32) / rot_dim)
    ang = jnp.arange(T, dtype=jnp.float32)[:, None] * inv[None, :]
    return jnp.cos(ang), jnp.sin(ang)

def apply_rope(x, cos, sin):
    half = x.shape[-1] // 2
    extra = x.ndim - 3
    c = cos.reshape((cos.shape[0],) + (1,) * extra + (half,))
    s = sin.reshape((sin.shape[0],) + (1,) * extra + (half,))
    x1, x2 = x[..., :half], x[..., half:]
    return jnp.concatenate([x1 * c - x2 * s, x2 * c + x1 * s], axis=-1)

def _token_shift(p, mu):
    prev = jnp.pad(p, ((0, 0), (1, 0), (0, 0)))[:, :-1]
    return p + (prev - p) * mu

def _causal_dwconv(x, w, b):
    K, C = w.shape
    out = lax.conv_general_dilated(x, w.astype(x.dtype)[:, None, :], window_strides=(1,),
                                   padding=[(K - 1, 0)], dimension_numbers=('NWC', 'WIO', 'NWC'),
                                   feature_group_count=C)
    return out + b.astype(x.dtype)

def causal_attention_blocks(q, k, v, coeffs, scale):
    B, T, H, M, dk = q.shape
    nb = T // Q_BLOCK
    qb = jnp.moveaxis(q.astype(jnp.float32).reshape(B, nb, Q_BLOCK, H, M, dk), 1, 0)
    kf = k.astype(jnp.float32)
    vf = v.astype(jnp.float32)
    kpos = jnp.arange(T)
    neg = jnp.finfo(jnp.float32).min

    def one_block(args):
        q_blk, start = args
        qpos = start + jnp.arange(Q_BLOCK)
        s = jnp.einsum('bqhmd,bkhmd->bhmqk', q_blk, kf) * scale
        s = jnp.where(kpos[None, :] <= qpos[:, None], s, neg)
        p = jax.nn.softmax(s, axis=-1)
        attn = jnp.einsum('m,bhmqk->bhqk', coeffs, p)
        return jnp.einsum('bhqk,bkhv->bqhv', attn, vf)

    out = lax.map(one_block, (qb, jnp.arange(nb) * Q_BLOCK))
    return jnp.moveaxis(out, 0, 1).reshape(B, T, H, v.shape[-1])

def _group_norm(y, w, b, eps):
    H, N = y.shape[-2:]
    mu = jnp.mean(y, -1, keepdims=True)
    var = jnp.mean(jnp.square(y - mu), -1, keepdims=True)
    return (y - mu) * lax.rsqrt(var + eps) * w.reshape(H, N) + b.reshape(H, N)

def _wkv7_scan(r, w, k, v, kk, a):
    B, T, H, N = r.shape

    def step(S, inp):
        r_t, w_t, k_t, v_t, kk_t, a_t = inp
        sa = jnp.einsum('bhvk,bhk->bhv', S, -kk_t)
        S = S * w_t[:, :, None, :] + sa[..., None] * (kk_t * a_t)[:, :, None, :] + v_t[..., None] * k_t[:, :, None, :]
        return S, jnp.einsum('bhvk,bhk->bhv', S, r_t)

    xs = tuple(jnp.moveaxis(t, 1, 0) for t in (r, w, k, v, kk, a))
    _, y = lax.scan(step, jnp.zeros((B, H, N, N), jnp.float32), xs)
    return jnp.moveaxis(y, 0, 1)

def rwkv7_group(p, v_first, mu, w0, w_up, a0, a_up, v_res, k_k, k_a, r_k, ln_w, ln_b):
    B, T, _ = p.shape
    p = _token_shift(p.astype(jnp.float32), mu)
    r, k, v, wd, ad = _split(p, (GROUP_W, GROUP_W, GROUP_W, RW_DECAY_LORA, RW_A_LORA))
    decay = jnp.exp(-jnp.exp(-jax.nn.softplus(-(w0 + jnp.tanh(wd) @ w_up)) - 0.5))
    a = jax.nn.sigmoid(a0 + ad @ a_up)
    if v_res is None:
        v_first = v
    else:
        v0, v_dn, v_up = v_res
        v = v + (v_first - v) * jax.nn.sigmoid(v0 + (v @ v_dn) @ v_up)

    def hd(t):
        return t.reshape(B, T, RW_HEADS, RW_HEAD)

    kk = hd(k * k_k)
    kk = kk / jnp.maximum(jnp.sqrt(jnp.sum(kk * kk, -1, keepdims=True)), 1e-12)
    k = k * (1.0 + (a - 1.0) * k_a)
    r, k, v, decay, a = hd(r), hd(k), hd(v), hd(decay), hd(a)
    y = _wkv7_scan(r, decay, k, v, kk, a)
    y = _group_norm(y, ln_w, ln_b, RW_GN_EPS) + jnp.sum(r * k * r_k, -1, keepdims=True) * v
    return y.reshape(B, T, GROUP_W), v_first

def _mlstm_chunkwise(q, k, v, i_pre, log_f):
    B, H, T, dk = q.shape
    dv = v.shape[-1]
    L = ML_CHUNK
    NC = T // L
    q = q.reshape(B, H, NC, L, dk)
    k = k.reshape(B, H, NC, L, dk)
    v = v.reshape(B, H, NC, L, dv)
    ig = i_pre.reshape(B, H, NC, L)
    b = jnp.cumsum(log_f.reshape(B, H, NC, L), axis=-1)
    b_last = b[..., -1]
    g = b_last[..., None] - b + ig
    g_max = jnp.max(g, axis=-1)
    wgt = jnp.exp(g - g_max[..., None])
    C_chunk = jnp.einsum('bhcs,bhcsv,bhcsk->bhcvk', wgt, v, k)
    n_chunk = jnp.einsum('bhcs,bhcsk->bhck', wgt, k)

    def step(carry, inp):
        C, n, m = carry
        bl, gm, Cc, nc = inp
        m_new = jnp.maximum(bl + m, gm)
        a_old = jnp.exp(bl + m - m_new)
        a_new = jnp.exp(gm - m_new)
        C_new = a_old[..., None, None] * C + a_new[..., None, None] * Cc
        n_new = a_old[..., None] * n + a_new[..., None] * nc
        return (C_new, n_new, m_new), (C, n, m)

    init = (jnp.zeros((B, H, dv, dk), jnp.float32), jnp.zeros((B, H, dk), jnp.float32),
            jnp.zeros((B, H), jnp.float32))
    xs = (jnp.moveaxis(b_last, 2, 0), jnp.moveaxis(g_max, 2, 0),
          jnp.moveaxis(C_chunk, 2, 0), jnp.moveaxis(n_chunk, 2, 0))
    _, (C_prev, n_prev, m_prev) = lax.scan(step, init, xs)
    C_prev = jnp.moveaxis(C_prev, 0, 2)
    n_prev = jnp.moveaxis(n_prev, 0, 2)
    m_prev = jnp.moveaxis(m_prev, 0, 2)

    mask = jnp.tril(jnp.ones((L, L), dtype=bool))
    D = b[..., :, None] - b[..., None, :] + ig[..., None, :]
    D = jnp.where(mask, D, -jnp.inf)
    inter_log = b + m_prev[..., None]
    m_j = jnp.maximum(inter_log, jnp.max(D, axis=-1))
    s = jnp.einsum('bhcjd,bhcsd->bhcjs', q, k) * jnp.exp(D - m_j[..., None])
    inter_w = jnp.exp(inter_log - m_j)
    num = jnp.einsum('bhcjs,bhcsv->bhcjv', s, v) + inter_w[..., None] * jnp.einsum('bhcvk,bhcjk->bhcjv', C_prev, q)
    den = jnp.sum(s, axis=-1) + inter_w * jnp.einsum('bhck,bhcjk->bhcj', n_prev, q)
    h = num / jnp.maximum(jnp.abs(den), jnp.exp(-m_j))[..., None]
    return h.reshape(B, H, T, dv)

def mlstm_group(p, conv_w, conv_b, i_b, f_b, norm_g):
    B, T, _ = p.shape
    qk, v, o, ig, fg = _split(p.astype(jnp.float32), (2 * GROUP_W, GROUP_W, GROUP_W, ML_HEADS, ML_HEADS))
    qk = jax.nn.silu(_causal_dwconv(qk, conv_w, conv_b))
    q, k = _split(qk, (GROUP_W, GROUP_W))

    def hd(t):
        return t.reshape(B, T, ML_HEADS, ML_HEAD).transpose(0, 2, 1, 3)

    i_pre = jnp.transpose(ig + i_b, (0, 2, 1))
    log_f = jnp.transpose(jax.nn.log_sigmoid(fg + f_b), (0, 2, 1))
    h = _mlstm_chunkwise(hd(q), hd(k) * ML_HEAD ** -0.5, hd(v), i_pre, log_f)
    h = rms_norm(h.transpose(0, 2, 1, 3), norm_g.reshape(ML_HEADS, ML_HEAD))
    h = jax.nn.sigmoid(o).reshape(B, T, ML_HEADS, ML_HEAD) * h
    return h.reshape(B, T, GROUP_W)

def mla_group(p, cos, sin, q_norm_g, kv_norm_g, w_q_b, w_kv_b, q_g, k_g):
    B, T, _ = p.shape
    q_lat, kv_lat, k_pe = _split(p.astype(jnp.float32), (MLA_Q_LORA, MLA_KV_LORA, MLA_ROPE))
    q = (rms_norm(q_lat, q_norm_g) @ w_q_b).reshape(B, T, MLA_HEADS, MLA_QK)
    kv = (rms_norm(kv_lat, kv_norm_g) @ w_kv_b).reshape(B, T, MLA_HEADS, MLA_NOPE + MLA_V)
    k_nope, v = kv[..., :MLA_NOPE], kv[..., MLA_NOPE:]
    k = jnp.concatenate([k_nope, jnp.broadcast_to(k_pe[:, :, None, :], (B, T, MLA_HEADS, MLA_ROPE))], -1)
    q = rms_norm(q, q_g)
    k = rms_norm(k, k_g)
    q = jnp.concatenate([q[..., :MLA_NOPE], apply_rope(q[..., MLA_NOPE:], cos, sin)], -1)
    k = jnp.concatenate([k[..., :MLA_NOPE], apply_rope(k[..., MLA_NOPE:], cos, sin)], -1)
    o = causal_attention_blocks(q[:, :, :, None, :], k[:, :, :, None, :], v,
                                jnp.ones((1,), jnp.float32), MLA_QK ** -0.5)
    return o.reshape(B, T, GROUP_W)

def diff_attn_group(p, layer, cos, sin, q_g, k_g, lq1, lk1, lq2, lk2, sub_g):
    B, T, _ = p.shape
    q, k, v = _split(p.astype(jnp.float32), (GROUP_W, GROUP_W, GROUP_W))
    q = rms_norm(q.reshape(B, T, DA_HEADS, 2, DA_QK), q_g)
    k = rms_norm(k.reshape(B, T, DA_HEADS, 2, DA_QK), k_g)
    q = jnp.concatenate([apply_rope(q[..., :DA_ROT], cos, sin), q[..., DA_ROT:]], -1)
    k = jnp.concatenate([apply_rope(k[..., :DA_ROT], cos, sin), k[..., DA_ROT:]], -1)
    v = v.reshape(B, T, DA_HEADS, DA_V)
    lam_init = 0.8 - 0.6 * math.exp(-0.3 * layer)
    lam = (jnp.exp(jnp.sum(lq1.astype(jnp.float32) * lk1.astype(jnp.float32)))
           - jnp.exp(jnp.sum(lq2.astype(jnp.float32) * lk2.astype(jnp.float32))) + lam_init)
    coeffs = jnp.stack([jnp.ones((), jnp.float32), -lam])
    o = causal_attention_blocks(q, k, v, coeffs, DA_QK ** -0.5)
    o = rms_norm(o, sub_g) * (1.0 - lam_init)
    return o.reshape(B, T, GROUP_W)

def setup_inputs(seed: int = 0) -> dict:
    key = jax.random.key(seed)
    ks = iter(jax.random.split(key, 48))
    f32 = jnp.float32
    L = DEPTH
    G = GROUP_W

    def nrm(shape, scale):
        return scale * jax.random.normal(next(ks), shape, f32)

    def gain(shape):
        return 1.0 + nrm(shape, 0.02)

    return {
        'x': jax.random.normal(next(ks), (BATCH, SEQ, D_MODEL), f32),
        'norm_g': gain((L, D_MODEL)),
        'w_in': nrm((L, D_MODEL, N_IN), D_MODEL ** -0.5),
        'w_out': nrm((L, D_MIX, D_MODEL), D_MIX ** -0.5),
        'branch_beta': gain((L, N_GROUPS)),
        'rw_mu': jax.random.uniform(next(ks), (L, RW_COLS), f32),
        'rw_w0': jax.random.uniform(next(ks), (L, G), f32, -6.0, 1.0),
        'rw_w_up': nrm((L, RW_DECAY_LORA, G), 0.1 * RW_DECAY_LORA ** -0.5),
        'rw_a0': nrm((L, G), 0.1),
        'rw_a_up': nrm((L, RW_A_LORA, G), 0.1 * RW_A_LORA ** -0.5),
        'rw_v0': 1.0 + nrm((L - 1, G), 0.1),
        'rw_v_dn': nrm((L - 1, G, RW_V_LORA), G ** -0.5),
        'rw_v_up': nrm((L - 1, RW_V_LORA, G), 0.1 * RW_V_LORA ** -0.5),
        'rw_k_k': 0.85 + nrm((L, G), 0.05),
        'rw_k_a': 1.0 + nrm((L, G), 0.05),
        'rw_r_k': nrm((L, RW_HEADS, RW_HEAD), 0.1),
        'rw_ln_w': gain((L, G)),
        'rw_ln_b': nrm((L, G), 0.02),
        'ml_conv_w': nrm((L, ML_CONV, 2 * G), ML_CONV ** -0.5),
        'ml_conv_b': nrm((L, 2 * G), 0.02),
        'ml_i_b': nrm((L, ML_HEADS), 0.1),
        'ml_f_b': jax.random.uniform(next(ks), (L, ML_HEADS), f32, 3.0, 6.0),
        'ml_norm_g': gain((L, G)),
        'mla_q_norm_g': gain((L, MLA_Q_LORA)),
        'mla_kv_norm_g': gain((L, MLA_KV_LORA)),
        'mla_w_q_b': nrm((L, MLA_Q_LORA, MLA_HEADS * MLA_QK), MLA_Q_LORA ** -0.5),
        'mla_w_kv_b': nrm((L, MLA_KV_LORA, MLA_HEADS * (MLA_NOPE + MLA_V)), MLA_KV_LORA ** -0.5),
        'mla_q_g': gain((L, MLA_QK)),
        'mla_k_g': gain((L, MLA_QK)),
        'da_q_g': gain((L, DA_QK)),
        'da_k_g': gain((L, DA_QK)),
        'da_lq1': nrm((L, DA_QK), 0.1),
        'da_lk1': nrm((L, DA_QK), 0.1),
        'da_lq2': nrm((L, DA_QK), 0.1),
        'da_lk2': nrm((L, DA_QK), 0.1),
        'da_sub_g': gain((L, DA_V)),
    }

def reference(x, norm_g, w_in, w_out, branch_beta, rw_mu, rw_w0, rw_w_up, rw_a0, rw_a_up,
              rw_v0, rw_v_dn, rw_v_up, rw_k_k, rw_k_a, rw_r_k, rw_ln_w, rw_ln_b,
              ml_conv_w, ml_conv_b, ml_i_b, ml_f_b, ml_norm_g,
              mla_q_norm_g, mla_kv_norm_g, mla_w_q_b, mla_w_kv_b, mla_q_g, mla_k_g,
              da_q_g, da_k_g, da_lq1, da_lk1, da_lq2, da_lk2, da_sub_g):
    T = x.shape[1]
    cos_mla, sin_mla = rope_tables(T, MLA_ROPE)
    cos_da, sin_da = rope_tables(T, DA_ROT)
    v_first = None
    for l in range(DEPTH):
        h = rms_norm(x, norm_g[l]).astype(x.dtype)
        p = h @ w_in[l]
        z, p_rw, p_ml, p_mla, p_da = _split(p, IN_WIDTHS)
        v_res = None if l == 0 else (rw_v0[l - 1], rw_v_dn[l - 1], rw_v_up[l - 1])
        y_rw, v_first = rwkv7_group(p_rw, v_first, rw_mu[l], rw_w0[l], rw_w_up[l], rw_a0[l], rw_a_up[l],
                                    v_res, rw_k_k[l], rw_k_a[l], rw_r_k[l], rw_ln_w[l], rw_ln_b[l])
        y_ml = mlstm_group(p_ml, ml_conv_w[l], ml_conv_b[l], ml_i_b[l], ml_f_b[l], ml_norm_g[l])
        y_mla = mla_group(p_mla, cos_mla, sin_mla, mla_q_norm_g[l], mla_kv_norm_g[l],
                          mla_w_q_b[l], mla_w_kv_b[l], mla_q_g[l], mla_k_g[l])
        y_da = diff_attn_group(p_da, l, cos_da, sin_da, da_q_g[l], da_k_g[l],
                               da_lq1[l], da_lk1[l], da_lq2[l], da_lk2[l], da_sub_g[l])
        beta = branch_beta[l].astype(jnp.float32)
        y = jnp.concatenate([beta[0] * y_rw, beta[1] * y_ml, beta[2] * y_mla, beta[3] * y_da], axis=-1)
        y = y * jax.nn.silu(z.astype(jnp.float32))
        x = x + (y.astype(x.dtype) @ w_out[l]).astype(x.dtype)
    return x


_drawn_inputs = setup_inputs


def setup_inputs(seed=0):
    import zlib

    import numpy as np

    out = dict(_drawn_inputs(seed))
    spreads = {}
    factors = {'branch_beta': 5.024,
     'rw_w_up': 8.0,
     'rw_a0': 3.418,
     'rw_a_up': 3.329,
     'rw_v0': 5.938,
     'rw_v_dn': 7.558,
     'rw_v_up': 7.674,
     'rw_k_k': 3.189,
     'rw_k_a': 2.733,
     'rw_ln_w': 7.123,
     'rw_ln_b': 6.92,
     'ml_conv_b': 8.0,
     'ml_i_b': 64.0,
     'ml_norm_g': 8.0,
     'mla_q_norm_g': 8.0,
     'mla_kv_norm_g': 8.0,
     'mla_q_g': 8.0,
     'mla_k_g': 8.0,
     'da_q_g': 8.0,
     'da_k_g': 8.0,
     'da_lk1': 4.793,
     'da_lq2': 3.487,
     'da_sub_g': 8.0}
    for name, (base, spread) in spreads.items():
        noise = np.random.default_rng([zlib.crc32(name.encode()), seed]).standard_normal(out[name].shape)
        drawn = base * np.exp(spread * noise) if base else spread * noise
        out[name] = jnp.asarray(drawn.astype(out[name].dtype))
    for name, factor in factors.items():
        out[name] = (out[name] * factor).astype(out[name].dtype)
    return out
```

```python
from contextlib import ExitStack
import math

import numpy as np

import concourse.bass as bass
from concourse import mybir

F32 = mybir.dt.float32
F32R = mybir.dt.float32r
ALU = mybir.AluOpType
ACT = mybir.ActivationFunctionType
AX = mybir.AxisListType.X

P = 128
D, T, DEPTH = 2048, 512, 2
NT = T // P
KT = D // P
G = 512
EPS = 1e-6
GN_EPS = 64e-5
HEADS = 4
RW_CHUNK = 64
NCH = T // RW_CHUNK
LEVELS = (2, 4, 8, 16, 32)
MASKED = -1e30

Z0 = 0
RW0 = D
RW_COLS = 3 * G + 64
ML0 = RW0 + RW_COLS
MLA0 = ML0 + 4 * G + 8
DA0 = MLA0 + 704
N_IN = DA0 + 3 * G

PIECES = (
    [[(RW0 + j * G, G)] for j in range(3)]
    + [[(MLA0 + 512, 256), (RW0 + 3 * G, P), (ML0 + 4 * G, P)]]
    + [[(Z0, G)], [(MLA0, G)], [(Z0 + 2 * G, G)]]
    + [[(ML0 + j * G, G)] for j in range(4)]
    + [[(Z0 + G, G)]]
    + [[(DA0 + j * G, G)] for j in range(3)]
    + [[(Z0 + 3 * G, G)]]
)
(G_R, G_K, G_V, G_MISC, G_Z_RW, G_LAT, G_Z_LA, G_MLQ, G_MLK, G_MLV, G_MLO, G_Z_ML, G_DAQ, G_DAK, G_DAV, G_Z_DA) = range(16)
NG = len(PIECES)
TOKEN_MAJOR = (G_MLV, G_DAV)
KV1, KPE, LORA, GATES = (4 * G_MISC + j for j in range(4))
STEPS = NG * KT
EARLY_K, LATE_K = 12, 4
EARLY, LATE = 4 * EARLY_K, 4 * LATE_K
HI_FIRST, HI_LAST = 4 * KT, STEPS + EARLY + 4
N_RAW, N_SPLIT = 6, 4
N_PARAM_DMAS = 32
FILL = dict(da_sums=3, da_scores=2, da_half=3, da_osq=1, da_gate=1)

ROWS, _at = {}, 0
for _name, _n in (("rw_mu", 13), ("rw_w0", 4), ("rw_a0", 4), ("rw_v0", 4), ("rw_k_k", 4), ("rw_k_a", 4),
                  ("rw_r_k", 4), ("rw_ln_w", 4), ("rw_ln_b", 4), ("ml_conv_w", 32), ("ml_conv_b", 8),
                  ("ml_norm_g", 4), ("mla_q_norm_g", 3), ("mla_kv_norm_g", 2), ("mla_q_g", 2),
                  ("mla_k_g", 2), ("da_q_g", 1), ("da_k_g", 1), ("da_sub_g", 1), ("norm_g", 16)):
    ROWS[_name] = _at
    _at += _n
N_ROWS = _at

CONST = {}
_at = 0
for _name, _n in (("ident", P), ("ones", P), ("bones", P), ("eps", 2),
                  ("mask_b", 256), ("mask_k", 256), ("levels", 5 * P), ("level1", P), ("reset", T),
                  ("eye64", 64),
                  ("neg", P), ("rot_mla", 64), ("rot_da", P), ("cos_mla", T), ("sin_mla", T),
                  ("cos_da", T), ("sin_da", T),
                  ("causal", P), ("sel_u", 4 * P), ("sel_f", 4 * P), ("sel_u4", 4), ("pass", T)):
    CONST[_name] = (_at, _n)
    _at += _n
N_CONST = _at
ALWAYS = CONST["mask_b"][0]
RW_CONST = (ALWAYS, CONST["neg"][0])
ATT_CONST = (CONST["neg"][0], CONST["causal"][0])
ML_CONST = (CONST["causal"][0], N_CONST)


def constants():
    c = np.zeros((P, N_CONST), np.float32)

    def put(name, a):
        c[:a.shape[0], CONST[name][0]:CONST[name][0] + a.shape[1]] = a

    r, q = np.arange(P)[:, None], np.arange(P)[None, :]
    put("ident", np.eye(P))
    put("ones", np.ones((P, P)))
    same = r // 64 == q // 64
    put("bones", same * 1.0)
    put("eps", np.tile(np.array([[EPS, GN_EPS]]), (P, 1)))
    strict, incl = same & (r < q), same & (r <= q)
    put("mask_b", np.concatenate([strict * 1.0, incl * -1.0], 1))
    put("mask_k", np.concatenate([strict * 1.0, incl * 1.0], 1))
    put("levels", np.concatenate([
        (r // (2 * b) == q // (2 * b)) & (r // b % 2 == 1) & (q // b % 2 == 0) for b in LEVELS], 1) * 1.0)
    put("level1", ((q == r + 1) & (r % 2 == 0)) * 1.0)
    put("reset", np.tile((np.arange(T) % RW_CHUNK != 0) * 1.0, (P, 1)))
    put("eye64", (r % 64 == np.arange(64)[None, :]) * 1.0)
    put("neg", (q > r) * MASKED)
    theta = np.float32(500000.0)

    def tables(rot):
        inv = theta ** (-np.arange(0, rot, 2, dtype=np.float32) / np.float32(rot))
        ang = np.arange(T, dtype=np.float32)[:, None] * inv[None, :]
        return np.cos(ang).T.astype(np.float32), np.sin(ang).T.astype(np.float32)

    cs, sn = tables(64)
    put("cos_mla", np.concatenate([cs, cs]))
    put("sin_mla", np.concatenate([sn, sn]))

    def rotation(n, half, block):
        m = np.zeros((n, n), np.float32)
        for b in range(0, n, block):
            for j in range(half):
                m[b + half + j, b + j] = -1.0
                m[b + j, b + half + j] = 1.0
        return m

    put("rot_mla", rotation(64, 32, 64))
    put("rot_da", rotation(P, 8, 64))
    cs, sn = tables(16)
    cd, sd = np.ones((P, T), np.float32), np.zeros((P, T), np.float32)
    for b in (0, 64):
        cd[b:b + 16], sd[b:b + 16] = np.concatenate([cs, cs]), np.concatenate([sn, sn])
    put("cos_da", cd)
    put("sin_da", sd)
    put("causal", (r <= q) * 1.0)
    su, sf, s4 = np.zeros((36, 4 * P)), np.zeros((36, 4 * P)), np.zeros((36, 4))
    for h in range(HEADS):
        su[h, h * P:(h + 1) * P], su[32 + h, h * P:(h + 1) * P] = 1.0, -1.0
        sf[32 + h, h * P:(h + 1) * P] = 1.0
        s4[h, h], s4[32 + h, h] = 1.0, -1.0
    put("sel_u", su)
    put("sel_f", sf)
    put("sel_u4", s4)
    put("pass", np.ones((P, T)))
    return c


class Progress:

    def __init__(self, first=0, end=STEPS):
        self.done, self.end = first, end

    def ahead(self, n):
        first, self.done = self.done, min(self.end, self.done + n)
        return range(first, self.done)

    def rest(self):
        return self.ahead(self.end - self.done)

    def through(self, group):
        return self.ahead(max(0, (group + 1) * KT - self.done))


def groups_ended(steps):
    return [n // KT for n in steps if n % KT == KT - 1]


def early_ended(steps):
    return [(n - STEPS) // EARLY_K for n in steps if (n - STEPS) % EARLY_K == EARLY_K - 1]


def z_tile(tile):
    return 4 * (G_Z_RW, G_Z_ML, G_Z_LA, G_Z_DA)[tile // 4] + tile % 4


def build(nc, a, out):
    with ExitStack() as ctx:
        def sb(name, shape, dt=F32):
            return ctx.enter_context(nc.sbuf_tensor(name, shape, dt))

        def sem(name):
            return ctx.enter_context(nc.semaphore(name))

        h_hi = sb("h_hi", [P, KT, T], F32R)
        h_lo = sb("h_lo", [P, KT, T], F32R)
        raw = sb("raw", [P, N_RAW, G])
        w_hi = sb("w_hi", [P, N_SPLIT, G], F32R)
        w_lo = sb("w_lo", [P, N_SPLIT, G], F32R)
        always = sb("always", [P, ALWAYS])
        rows = sb("rows", [P, P])
        par = sb("par", [P, P])
        small = sb("small", [P, 64])
        v_first = sb("v_first", [P, 4, T])
        stage = sb("stage", [P, 4, T])
        ARENA = 24832
        arena = sb("arena", [P, ARENA])

        def carve(at, *shape):
            n = int(np.prod(shape))
            assert at + n <= ARENA, (at, n)
            v = arena[:, at:at + n]
            if len(shape) == 2:
                v = v.rearrange("p (a b) -> p a b", a=shape[0])
            if len(shape) == 3:
                v = v.rearrange("p (a b c) -> p a b c", a=shape[0], b=shape[1])
            return v

        class Region:

            def __init__(self, at=0):
                self.at = at

            def __call__(self, *shape):
                v = carve(self.at, *shape)
                self.at += int(np.prod(shape))
                return v

        def const(name, region=None, first=0):
            at, n = CONST[name]
            return (always if region is None else region)[:, at - first:at - first + n]

        ps_proj = ctx.enter_context(nc.psum_tensor("ps_proj", [P, 4, 512], F32))
        ps = ctx.enter_context(nc.psum_tensor("ps", [P, 4, 512], F32))

        p_dram = nc.dram_tensor("projected", (4 * NG, P, T), F32, kind="Internal").ap()
        y_dram = nc.dram_tensor("gated", (KT, P, T), F32, kind="Internal").ap()
        x_dram = out[0].rearrange("(i p) d -> p i d", p=P)

        ident, ones, bones = const("ident"), const("ones"), const("bones")
        eps_col, gn_eps_col = const("eps")[:, 0:1], const("eps")[:, 1:2]
        x_tok = carve(ARENA - NT * D, NT, D)

        def col(name, j=0):
            return par[:, ROWS[name] + j:ROWS[name] + j + 1]

        beta = small[:, 0:4]
        half_w0, half_a0, half_v0 = small[:, 4:8], small[:, 8:12], small[:, 12:16]
        one_m_half_ka = small[:, 16:20]
        gate_bias = small[:, 20:21]
        half_ka, half_beta, half_ml_g = small[:, 41:45], small[:, 45:49], small[:, 49:53]
        lam4 = small[:, 21:25]
        lam2 = small[:, 25:27]
        neg_lam = small[:, 27:28]
        sub_gain = small[:, 28:29]
        ms = small[:, 32:36]
        rs_x = small[:, 36:40]
        lam_prod = small[:, 29:31]
        half_flag = small[:, 60:61]
        lam_init = small[:, 61:62]
        one_m_lam_init = small[:, 62:63]



        s_setup, s_setup_out, s_flags = sem("setup_loaded"), sem("x_kept"), sem("flags_set")
        s_setup_x = [sem(f"x_loaded_{i}") for i in range(NT)]
        with nc.Block() as block:
            @block.sync
            def _(sp):
                sp.dma_start(always[:], a["const"][:, 0:ALWAYS]).then_inc(s_setup, 16)
                for i in range(NT):
                    sp.dma_start(x_tok[:, i, :], a["x"][0, i * P:(i + 1) * P, :]).then_inc(s_setup_x[i], 16)
                sp.dma_start(out[0], a["x"][0]).then_inc(s_setup_out, 16)

            @block.vector
            def _(dve):
                nc.vector.memset(v_first[:], 0.0).then_inc(s_flags, 1)
                nc.vector.memset(small[:, 0:60], 0.0).then_inc(s_flags, 1)
                nc.vector.memset(half_flag, 0.0).then_inc(s_flags, 1)
                nc.vector.memset(lam_init, 0.8 - 0.6).then_inc(s_flags, 1)
                nc.vector.memset(one_m_lam_init, 1.0 - (0.8 - 0.6)).then_inc(s_flags, 1)
                nc.vector.memset(rows[:], 0.0).then_inc(s_flags, 1)
                dve.wait_ge(s_flags, 6)

        rg = Region()
        rw_const = rg(RW_CONST[1] - RW_CONST[0])
        rw_lora = rg(T + 1)
        rw_in = rg(2, T + 1)
        rw_v = rg(4, T + 1)
        rw_d = rg(T)
        reused = rg.at
        rw_t = rg(3, T)
        rw_c, rw_cm, rw_wm, rw_wi, rw_kk = rg(T), rg(T), rg(T), rg(T), rg(T)
        rw_w, rw_sq, rw_nr, rw_kf = rg(T), rg(T), rg(T), rg(T)
        rw_ar = rg(NT, 2, P)
        rw_beta, rw_kappa = rg(T), rg(T)
        rw_bn_at = rg.at
        rw_bn, rw_kt = rg(T), rg(T)
        rw_bonus = rg(T)
        rw_abv = rg(NT, 2, P)
        rw_bnT, rw_ktT, rw_vT = rg(NT, P), rg(NT, P), rg(NT, P)
        rw_gb, rw_gk = rg(8, 256), rg(8, 256)
        rw_wup, rw_vup = rg(G), rg(G)
        rw_vdn = rg(4, 32)
        rw_z, rw_yo = rg(T), rg(T)
        rw_wl = rg(NCH)
        r2 = Region(reused)
        rw_xt, rw_x, rw_y, rw_pu = r2(8, P), r2(8, P), r2(8, P), r2(8, P)
        assert r2.at <= reused + 3 * T + 5 * T
        rw_gt = rw_beta.rearrange("p (c k) -> p c k", c=NCH)
        rw_wli = rw_kappa.rearrange("p (c k) -> p c k", c=NCH)
        rw_st = carve(rw_bn_at, NCH + 1, 64)
        rw_yl, rw_e, rw_vd = rw_kf, rw_w, rw_d
        mask_b = const("mask_b", rw_const, RW_CONST[0])
        mask_k = const("mask_k", rw_const, RW_CONST[0])
        levels = const("levels", rw_const, RW_CONST[0])
        level1 = const("level1", rw_const, RW_CONST[0])
        reset = const("reset", rw_const, RW_CONST[0])
        eye64 = const("eye64", rw_const, RW_CONST[0])

        rg = Region()
        at_const = rg(ATT_CONST[1] - ATT_CONST[0])
        la_in = rg(5, T)
        la_pe = rg(T)
        la_p_at = rg.at
        la_sq = rg(5, T)
        la_p = carve(la_p_at, NT, T)
        la_wq = rg(3, 768)
        la_wkv = rg(2, 1024)
        la_rs = rg(2, T)
        la_peg, la_per, la_pesq = rg(T), rg(T), rg(T)
        la_v = rg(NT, G)
        la_hsq = rg(3, T)
        la_q, la_qp, la_k = rg(T), rg(T), rg(T)
        la_kp, la_tmp = rg(T), rg(T)
        la_pt = rg(NT, T)
        la_z, la_yo, la_e = rg(T), rg(T), rg(T)
        la_mx, la_sum = rg(NT), rg(NT)
        neg = const("neg", at_const, ATT_CONST[0])
        rot_mla, rot_da = const("rot_mla", at_const, ATT_CONST[0]), const("rot_da", at_const, ATT_CONST[0])
        cos_mla, sin_mla = const("cos_mla", at_const, ATT_CONST[0]), const("sin_mla", at_const, ATT_CONST[0])
        cos_da, sin_da = const("cos_da", at_const, ATT_CONST[0]), const("sin_da", at_const, ATT_CONST[0])

        rg = Region(ATT_CONST[1] - ATT_CONST[0])
        da_in = rg(2, T)
        da_v = rg(NT, G)
        da_sq, da_g, da_rs = rg(2, T), rg(2, T), rg(2, T)
        da_p_at = rg.at
        da_p = rg(4, T)
        da_qk = carve(da_p_at, 2, T)
        da_a = rg(NT, T)
        da_pt = rg(NT, T)
        da_o, da_osq, da_ors = da_in[:, 0, :], da_sq[:, 0, :], da_sq[:, 1, :]
        da_z, da_yo, da_e = rg(T), rg(T), rg(T)
        da_mx, da_sum = rg(4), rg(4)
        assert rg.at <= ARENA - NT * D, rg.at

        rg = Region()
        ml_const = rg(ML_CONST[1] - ML_CONST[0])
        ml_in = rg(2, T + 3)
        ml_acc = rg(2, T)
        ml_sil = rg(2, T)
        ml_v = rg(NT, G)
        ml_gate = rg(T)
        ml_gt, ml_sg = rg(T), rg(T)
        ml_ucol = rg(NT, 4)
        ml_m, ml_nf = rg(T), rg(T)
        ml_w = rg(NT, T)
        ml_s = rg(NT, T)
        ml_h, ml_den, ml_sq = rg(T), rg(T), rg(T)
        ml_o, ml_oe, ml_rs = rg(T), rg(T), rg(T)
        ml_z, ml_yo, ml_e = rg(T), rg(T), rg(T)
        causal = const("causal", ml_const, ML_CONST[0])
        sel_u, sel_f = const("sel_u", ml_const, ML_CONST[0]), const("sel_f", ml_const, ML_CONST[0])
        sel_u4 = const("sel_u4", ml_const, ML_CONST[0])
        carry = const("pass", ml_const, ML_CONST[0])

        s_first = sem("layer_first")
        s_params_loaded = sem("params_loaded")
        s_params_turned = sem("params_turned")
        s_lam_ready = sem("lam_ready")
        s_h_hi_ready = sem("h_hi_ready")
        s_par_ready = sem("par_ready")
        s_small_ready = sem("small_ready")
        s_x_mean = sem("x_mean")
        s_x_scaled = sem("x_scaled")
        s_x_turned = sem("x_turned")
        s_h_split = sem("h_split")
        s_hi_split = sem("hi_split")
        s_hi_by_act = sem("hi_by_act")
        s_y_hi_ready = sem("y_hi_ready")
        s_y_split = sem("y_split")
        s_y_loaded = [sem(f"y_loaded_{m}") for m in range(4)]
        s_raw_split = sem("raw_split")
        s_split_used = sem("split_used")
        s_proj_done = sem("proj_done")
        s_proj_copied = sem("proj_copied")
        s_out_done = sem("out_done")
        s_out_added = sem("out_added")
        s_out_kept = sem("out_kept")
        s_x_prefetched = sem("x_prefetched")
        s_z_loaded = sem("z_loaded")
        s_z_tanh = sem("z_tanh")
        s_y_ready = sem("y_ready")
        s_y_kept = sem("y_kept")
        s_rw_v_shifted = sem("rw_v_shifted")
        s_rw_first_loaded = sem("rw_first_loaded")
        s_rw_rk_loaded = sem("rw_rk_loaded")
        s_rw_shifted = sem("rw_shifted")
        s_rw_lora_tanh = sem("rw_lora_tanh")
        s_rw_vdn_mm = sem("rw_vdn_mm")
        s_rw_vd_ready = sem("rw_vd_ready")
        s_rw_lora_mm = sem("rw_lora_mm")
        s_rw_sig_tanh = sem("rw_sig_tanh")
        s_rw_decay = sem("rw_decay")
        s_rw_kk_sq = sem("rw_kk_sq")
        s_rw_decay_exp = sem("rw_decay_exp")
        s_rw_kk_sum = sem("rw_kk_sum")
        s_rw_kk_root = sem("rw_kk_root")
        s_rw_factors = sem("rw_factors")
        s_rw_turned = sem("rw_turned")
        s_rw_turned_copied = sem("rw_turned_copied")
        s_rw_bonus_ready = sem("rw_bonus_ready")
        s_rw_v_turned = sem("rw_v_turned")
        s_rw_v_copied = sem("rw_v_copied")
        s_rw_gram = sem("rw_gram")
        s_rw_gram_masked = sem("rw_gram_masked")
        s_rw_xt_first = sem("rw_xt_first")
        s_rw_x_first = sem("rw_x_first")
        s_rw_x_ready = sem("rw_x_ready")
        s_rw_levelled = sem("rw_levelled")
        s_rw_level_masked = sem("rw_level_masked")
        s_rw_level_mm = sem("rw_level_mm")
        s_rw_level_done = sem("rw_level_done")
        s_rw_pu_mm = sem("rw_pu_mm")
        s_rw_pu_ready = sem("rw_pu_ready")
        s_rw_local = sem("rw_local")
        s_rw_local_ready = sem("rw_local_ready")
        s_rw_h_copied = sem("rw_h_copied")
        s_rw_state_mm = sem("rw_state_mm")
        s_rw_state_ready = sem("rw_state_ready")
        s_rw_carried = sem("rw_carried")
        s_rw_y_whole = sem("rw_y_whole")
        s_rw_mean = sem("rw_mean")
        s_rw_centred = sem("rw_centred")
        s_rw_var = sem("rw_var")
        s_rw_rstd = sem("rw_rstd")
        s_scores_mm = sem("scores_mm")
        s_row_max = sem("row_max")
        s_probs_exp = sem("probs_exp")
        s_probs_ready = sem("probs_ready")
        s_probs_turned = sem("probs_turned")
        s_probs_t_copied = sem("probs_t_copied")
        s_pv_done = sem("pv_done")
        s_la_loaded = sem("la_loaded")
        s_la_squared = sem("la_squared")
        s_la_sums = sem("la_sums")
        s_la_rs_ready = sem("la_rs_ready")
        s_la_latents = sem("la_latents")
        s_la_v_mm = sem("la_v_mm")
        s_la_v_copied = sem("la_v_copied")
        s_la_heads_mm = sem("la_heads_mm")
        s_la_heads_copied = sem("la_heads_copied")
        s_la_heads_sums = sem("la_heads_sums")
        s_la_heads_rs = sem("la_heads_rs")
        s_la_qk_ready = sem("la_qk_ready")
        s_ml_cleared = sem("ml_cleared")
        s_ml_ucol_mm = sem("ml_ucol_mm")
        s_ml_ucol_ready = sem("ml_ucol_ready")
        s_ml_first_loaded = sem("ml_first_loaded")
        s_ml_qk_loaded = sem("ml_qk_loaded")
        s_ml_conv = sem("ml_conv")
        s_ml_conv_tanh = sem("ml_conv_tanh")
        s_ml_qk_ready = sem("ml_qk_ready")
        s_ml_gate_abs = sem("ml_gate_abs")
        s_ml_gate_log = sem("ml_gate_log")
        s_ml_gates = sem("ml_gates")
        s_ml_u_mm = sem("ml_u_mm")
        s_ml_max = sem("ml_max")
        s_ml_w_exp = sem("ml_w_exp")
        s_ml_scores_mm = sem("ml_scores_mm")
        s_ml_s_ready = sem("ml_s_ready")
        s_ml_num_mm = sem("ml_num_mm")
        s_ml_h_sq = sem("ml_h_sq")
        s_ml_h_sum = sem("ml_h_sum")
        s_ml_h_rs = sem("ml_h_rs")
        s_ml_o_tanh = sem("ml_o_tanh")
        s_da_row_max = sem("da_row_max")
        s_da_scores_mm = sem("da_scores_mm")
        s_da_probs_exp = sem("da_probs_exp")
        s_da_loaded = sem("da_loaded")
        s_da_first_loaded = sem("da_first_loaded")
        s_da_squared = sem("da_squared")
        s_da_sums = sem("da_sums")
        s_da_rs_ready = sem("da_rs_ready")
        s_da_qk_ready = sem("da_qk_ready")
        s_da_half = sem("da_half")
        s_da_osq_ready = sem("da_osq_ready")
        s_da_osum_mm = sem("da_osum_mm")
        s_da_ors_ready = sem("da_ors_ready")
        s_da_lam_mm = sem("da_lam_mm")
        s_da_lam_exp = sem("da_lam_exp")
        s_stored = [sem(f"stored_{m}") for m in range(4)]
        s_raw_loaded = [sem(f"raw_loaded_{s}") for s in range(N_RAW)]
        s_act_order = sem("act_order")
        s_dve_order = sem("dve_order")
        s_last = sem("layer_last")
        of_layer = range(s_first.num, s_last.num + 1)

        def steps_of_weights():
            for g, pieces in enumerate(PIECES):
                for k in range(KT):
                    yield "w_in", k, pieces
            for part in (range(EARLY_K), range(EARLY_K, KT)):
                for n in range(4):
                    for k in part:
                        yield "w_out", k, [(n * G, G)]

        weight_steps = list(steps_of_weights())
        raw_count, raw_target = [0] * N_RAW, []
        for n, (_, _, pieces) in enumerate(weight_steps):
            raw_count[n % N_RAW] += 16 * len(pieces)
            raw_target.append(raw_count[n % N_RAW])


        with nc.Fori(0, DEPTH) as layer:
            with nc.Block() as block:
                @block.sync
                def _(sp):
                    def row(x):
                        return x.rearrange("(o n) -> o n", o=1)

                    for name, n in (("rw_w0", 4), ("rw_a0", 4), ("rw_k_k", 4), ("rw_k_a", 4),
                                    ("rw_ln_w", 4), ("rw_ln_b", 4), ("ml_conv_b", 8), ("ml_norm_g", 4),
                                    ("mla_q_norm_g", 3), ("mla_kv_norm_g", 2), ("da_sub_g", 1), ("norm_g", 16)):
                        r0 = ROWS[name]
                        sp.dma_start(rows[r0:r0 + n, :], a[name][layer].rearrange("(n p) -> n p", p=P)
                                     ).then_inc(s_params_loaded, 16)
                    r0 = ROWS["rw_r_k"]
                    sp.dma_start(rows[r0:r0 + 4, :], a["rw_r_k"][layer].rearrange("(n q) p -> n (q p)", q=2)
                                 ).then_inc(s_params_loaded, 16)
                    r0 = ROWS["rw_v0"]
                    sp.dma_start(rows[r0:r0 + 4, :], a["rw_v0"][0].rearrange("(n p) -> n p", p=P)
                                 ).then_inc(s_params_loaded, 16)
                    r0 = ROWS["rw_mu"]
                    sp.dma_start(rows[r0:r0 + 12, :], a["rw_mu"][layer, 0:3 * G].rearrange("(n p) -> n p", p=P)
                                 ).then_inc(s_params_loaded, 16)
                    sp.dma_start(rows[r0 + 12:r0 + 13, 0:64], row(a["rw_mu"][layer, 3 * G:RW_COLS])
                                 ).then_inc(s_params_loaded, 16)
                    r0 = ROWS["ml_conv_w"]
                    sp.dma_start(rows[r0:r0 + 32, :], a["ml_conv_w"][layer].rearrange("c (n p) -> (c n) p", p=P)
                                 ).then_inc(s_params_loaded, 16)
                    for name in ("mla_q_g", "mla_k_g"):
                        r0 = ROWS[name]
                        sp.dma_start(rows[r0:r0 + 1, :], row(a[name][layer, 0:P])
                                     ).then_inc(s_params_loaded, 16)
                        sp.dma_start(rows[r0 + 1:r0 + 2, 0:64], row(a[name][layer, P:P + 64])
                                     ).then_inc(s_params_loaded, 16)
                    for name in ("da_q_g", "da_k_g"):
                        r0 = ROWS[name]
                        for m in range(2):
                            sp.dma_start(rows[r0:r0 + 1, 64 * m:64 * m + 64], row(a[name][layer, :])
                                         ).then_inc(s_params_loaded, 16)
                    sp.dma_start(beta, row(a["branch_beta"][layer, :]).to_broadcast([P, 4])
                                 ).then_inc(s_params_loaded, 16)
                    sp.dma_start(gate_bias[0:4, :], a["ml_i_b"][layer].rearrange("(h o) -> h o", o=1)
                                 ).then_inc(s_params_loaded, 16)
                    sp.dma_start(gate_bias[32:36, :], a["ml_f_b"][layer].rearrange("(h o) -> h o", o=1)
                                 ).then_inc(s_params_loaded, 16)
                    for j, name in enumerate(("da_lq1", "da_lk1", "da_lq2", "da_lk2")):
                        sp.dma_start(lam4[0:64, j:j + 1], a[name][layer].rearrange("(h o) -> h o", o=1)
                                     ).then_inc(s_params_loaded, 16)
                    for n, (source, k, pieces) in enumerate(weight_steps):
                        if n >= N_RAW:
                            sp.wait_ge(s_raw_split, n - N_RAW + 1)
                        at = 0
                        for c0, width in pieces:
                            sp.dma_start(raw[:, n % N_RAW, at:at + width],
                                         a[source][layer, k * P:(k + 1) * P, c0:c0 + width]
                                         ).then_inc(s_raw_loaded[n % N_RAW], 16)
                            at += width

                @block.gpsimd
                def _(pool):
                    for n in range(len(weight_steps)):
                        pool.wait_ge(s_raw_loaded[n % N_RAW], raw_target[n])
                        if n >= N_SPLIT:
                            pool.wait_ge(s_split_used, n - N_SPLIT + 1)
                        src = raw[:, n % N_RAW, :]
                        hi, lo = w_hi[:, n % N_SPLIT, :], w_lo[:, n % N_SPLIT, :]
                        if HI_FIRST <= n < HI_LAST:
                            nc.gpsimd.tensor_scalar(hi, src, 1.0, None, ALU.mult).then_inc(s_hi_split, 1)
                            pool.wait_ge(s_hi_split, n - HI_FIRST + 1)
                        else:
                            pool.wait_ge(s_hi_by_act, n + 1 if n < HI_FIRST else n + 1 - (HI_LAST - HI_FIRST))
                        nc.gpsimd.tensor_tensor(lo, src, hi.bitcast(F32), ALU.subtract).then_inc(s_raw_split, 1)

                @block.tensor
                def _(pe):
                    mm, turn = nc.tensor.matmul, nc.tensor.transpose
                    progress = Progress()

                    def project(steps):
                        for n in steps:
                            g, k = divmod(n, KT)
                            pe.wait_ge(s_raw_split, n + 1)
                            if g == 0:
                                pe.wait_ge(s_h_split, k + 1)
                            for m in range(4):
                                if k == 0 and g:
                                    pe.wait_ge(s_proj_copied, 4 * (g - 1) + m + 1)
                                w1, w2 = w_hi[:, n % N_SPLIT, :], w_lo[:, n % N_SPLIT, :]
                                part = slice(m * P, (m + 1) * P)
                                h1, h2 = h_hi[:, k, :], h_lo[:, k, :]
                                if g in TOKEN_MAJOR:
                                    products = ((h1[:, part], w1), (h1[:, part], w2), (h2[:, part], w1))
                                else:
                                    products = ((w1[:, part], h1), (w1[:, part], h2), (w2[:, part], h1))
                                for j, (lhsT, rhs) in enumerate(products):
                                    last = mm(ps_proj[:, m, :], lhsT, rhs, start=(k == 0 and j == 0),
                                              stop=(k == KT - 1 and j == 2))
                                if k == KT - 1 and m < 3:
                                    last.then_inc(s_proj_done, 1)
                            last.then_inc(s_split_used, 1)

                    def fill(n=1):
                        project(progress.ahead(n))

                    pe.wait_ge(s_setup, 16)
                    pe.wait_ge(s_params_loaded, 16 * N_PARAM_DMAS)
                    turn(ps[:, 0, 0:P], rows[:, :], ident).then_inc(s_params_turned, 1)
                    pe.wait_ge(s_lam_ready, 1)
                    mm(ps[:, 1, 0:2], ones[0:64, :], lam_prod[0:64, :], start=True, stop=True
                       ).then_inc(s_da_lam_mm, 1)
                    pe.wait_ge(s_small_ready, 1)

                    pe.wait_ge(s_x_scaled, NT)
                    for k in range(KT):
                        if k >= 4:
                            pe.wait_ge(s_h_split, k - 3)
                        for i in range(NT):
                            last = turn(ps[:, k % 4, i * P:(i + 1) * P], x_tok[:, i, k * P:(k + 1) * P], ident)
                        last.then_inc(s_x_turned, 1)
                    project(progress.through(G_MISC))

                    pe.wait_ge(s_h_split, KT)
                    pe.wait_ge(s_rw_first_loaded, 16 * 8)
                    pe.wait_ge(s_rw_v_shifted, 1)
                    for j in range(4):
                        last = mm(ps[0:32, 0, :], rw_vdn[:, j, :], rw_v[:, j, 1:T + 1], start=(j == 0), stop=(j == 3))
                    last.then_inc(s_rw_vdn_mm, 1)
                    pe.wait_ge(s_rw_vd_ready, 1)
                    pe.wait_ge(s_rw_lora_tanh, 1)
                    for hp in range(4):
                        if hp:
                            pe.wait_ge(s_y_ready, hp)
                        cols = slice(hp * P, (hp + 1) * P)
                        mm(ps[:, 0, :], rw_wup[0:32, cols], rw_lora[0:32, 1:T + 1], start=True, stop=True)
                        mm(ps[:, 1, :], rw_wup[32:64, cols], rw_lora[32:64, 1:T + 1], start=True, stop=True)
                        mm(ps[:, 2, :], rw_vup[0:32, cols], rw_vd[0:32, :], start=True, stop=True
                           ).then_inc(s_rw_lora_mm, 1)
                        fill(8)
                        pe.wait_ge(s_rw_kk_sq, hp + 1)
                        mm(ps[:, 3, :], bones, rw_sq, start=True, stop=True).then_inc(s_rw_kk_sum, 1)
                        fill(5)
                        pe.wait_ge(s_rw_factors, hp + 1)
                        for i in range(NT):
                            turn(ps[:, 0, i * P:(i + 1) * P], rw_ar[:, i, 0, :], ident)
                            turn(ps[:, 1, i * P:(i + 1) * P], rw_bn[:, i * P:(i + 1) * P], ident)
                            turn(ps[:, 2, i * P:(i + 1) * P], rw_kt[:, i * P:(i + 1) * P], ident)
                        mm(ps[:, 3, :], bones, rw_sq, start=True, stop=True).then_inc(s_rw_turned, 1)
                        pe.wait_ge(s_rw_turned_copied, 3 * hp + 3)
                        for i in range(NT):
                            last = turn(ps[:, 0, i * P:(i + 1) * P], rw_v[:, hp, 1 + i * P:1 + (i + 1) * P], ident)
                        last.then_inc(s_rw_v_turned, 1)
                        fill()
                        pe.wait_ge(s_rw_v_copied, hp + 1)
                        pe.wait_ge(s_rw_bonus_ready, hp + 1)
                        for ip in range(2):
                            if ip:
                                pe.wait_ge(s_rw_gram_masked, 2 * hp + 1)
                            for i in (2 * ip, 2 * ip + 1):
                                for f, factor in enumerate((rw_beta, rw_kappa)):
                                    for h in range(2):
                                        half = slice(64 * h, 64 * h + 64)
                                        last = mm(ps[:, 2 * f + h, (i % 2) * 256:(i % 2) * 256 + 256],
                                                  factor[half, i * P:(i + 1) * P], rw_ar[half, i, :, :],
                                                  start=True, stop=True)
                            last.then_inc(s_rw_gram, 1)
                            fill()
                        pe.wait_ge(s_rw_xt_first, hp + 1)
                        for h in range(2):
                            for i in range(NT):
                                turn(ps[:, h, i * P:(i + 1) * P], rw_xt[:, 4 * h + i, :], ident)
                        for h in range(2):
                            for i in range(NT):
                                last = mm(ps[:, 2 + h, i * 64:(i + 1) * 64], rw_gk[:, 4 * h + i, 0:P],
                                          rw_vT[:, i, 64 * h:64 * h + 64], start=True, stop=True)
                        last.then_inc(s_rw_x_first, 1)
                        fill()
                        pe.wait_ge(s_rw_x_ready, 4 * hp + 4)
                        for lv in range(len(LEVELS)):
                            for h in range(2):
                                if lv:
                                    pe.wait_ge(s_rw_level_done, 10 * hp + 2 * (lv - 1) + h + 1)
                                for i in range(NT):
                                    j = 4 * h + i
                                    last = mm(ps[:, 2 * h, i * P:(i + 1) * P], rw_gb[:, j, 0:P], rw_x[:, j, :],
                                              start=True, stop=True)
                                last.then_inc(s_rw_levelled, 1)
                                if h:
                                    fill()
                            for h in range(2):
                                pe.wait_ge(s_rw_level_masked, 10 * hp + 2 * lv + h + 1)
                                for i in range(NT):
                                    j = 4 * h + i
                                    if lv < len(LEVELS) - 1:
                                        mm(ps[:, 2 * h, i * P:(i + 1) * P], rw_xt[:, j, :], rw_y[:, j, :],
                                           start=True, stop=True)
                                    last = mm(ps[:, 2 * h + 1, i * P:(i + 1) * P], rw_y[:, j, :], rw_xt[:, j, :],
                                              start=True, stop=True)
                                last.then_inc(s_rw_level_mm, 1)
                        fill()
                        for h in range(2):
                            pe.wait_ge(s_rw_level_done, 10 * hp + 8 + h + 1)
                            for i in range(NT):
                                j = 4 * h + i
                                last = mm(ps[:, h, i * P:(i + 1) * P], rw_xt[:, j, :], rw_abv[:, i, h, :],
                                          start=True, stop=True)
                            last.then_inc(s_rw_pu_mm, 1)
                        fill()
                        pe.wait_ge(s_rw_pu_ready, 2 * hp + 2)
                        for h in range(2):
                            half = slice(64 * h, 64 * h + 64)
                            for i in range(NT):
                                j = 4 * h + i
                                pt = slice(i * P, (i + 1) * P)
                                mm(ps[half, 2, pt], rw_pu[:, j, 0:64], rw_gb[:, j, P:2 * P], start=True, stop=True)
                                mm(ps[half, 3, pt], rw_vT[:, i, half], rw_gk[:, j, P:2 * P], start=True, stop=False)
                                last = mm(ps[half, 3, pt], rw_pu[:, j, 64:P], rw_gb[:, j, P:2 * P],
                                          start=False, stop=True)
                        for c in range(NCH):
                            i, q = c // 2, slice(64 * (c % 2), 64 * (c % 2) + 64)
                            for h in range(2):
                                half, j = slice(64 * h, 64 * h + 64), 4 * h + i
                                mm(ps[half, c % 2, i * P:i * P + 64], rw_pu[q, j, 0:64], rw_bnT[q, i, half],
                                   start=True, stop=True)
                                mm(ps[half, c % 2, i * P + 64:(i + 1) * P], rw_ktT[q, i, half], rw_vT[q, i, half],
                                   start=True, stop=False)
                                last = mm(ps[half, c % 2, i * P + 64:(i + 1) * P], rw_bnT[q, i, half],
                                          rw_pu[q, j, 64:P], start=False, stop=True)
                        last.then_inc(s_rw_local, 1)
                        fill()
                        pe.wait_ge(s_rw_local_ready, hp + 1)
                        for c in range(1, NCH - 1):
                            if c > 1:
                                pe.wait_ge(s_rw_state_ready, (NCH - 2) * hp + c - 1)
                            for h in range(2):
                                half = slice(64 * h, 64 * h + 64)
                                last = mm(ps[half, h, c * 64:(c + 1) * 64], rw_gt[half, c, :], rw_st[half, c, :],
                                          start=True, stop=True)
                            last.then_inc(s_rw_state_mm, 1)
                            if c % 2:
                                fill()
                        pe.wait_ge(s_rw_state_ready, (NCH - 2) * (hp + 1))
                        for c in range(NCH):
                            for h in range(2):
                                half = slice(64 * h, 64 * h + 64)
                                last = mm(ps[half, 2 + h, c * 64:(c + 1) * 64], rw_st[half, c, :],
                                          rw_ar[half, c // 2, 1, 64 * (c % 2):64 * (c % 2) + 64],
                                          start=True, stop=True)
                        last.then_inc(s_rw_carried, 1)
                        fill()
                        pe.wait_ge(s_rw_y_whole, hp + 1)
                        mm(ps[:, 0, :], bones, rw_yl, start=True, stop=True).then_inc(s_rw_mean, 1)
                        fill()
                        pe.wait_ge(s_rw_centred, hp + 1)
                        mm(ps[:, 1, :], bones, rw_sq, start=True, stop=True).then_inc(s_rw_var, 1)
                        if hp == 0:
                            project(progress.through(G_Z_RW))
                        else:
                            fill()

                    project(progress.through(G_Z_LA))
                    pe.wait_ge(s_y_ready, 4)
                    pe.wait_ge(s_la_squared, 1)
                    for j in range(3):
                        mm(ps[:, 0, :], ones, la_sq[:, j, :], start=(j == 0), stop=(j == 2))
                    for j in range(2):
                        mm(ps[:, 1, :], ones, la_sq[:, 3 + j, :], start=(j == 0), stop=(j == 1))
                    mm(ps[0:64, 2, :], rot_mla[0:64, :], la_peg[0:64, :], start=True, stop=True
                       ).then_inc(s_la_sums, 1)
                    fill()
                    pe.wait_ge(s_la_latents, 1)
                    for i in range(NT):
                        for j in range(2):
                            last = mm(ps[:, i, :], la_in[:, 3 + j, i * P:(i + 1) * P],
                                      la_wkv[:, j, :].rearrange("p (h c) -> p h c", h=HEADS)[:, :, P:2 * P],
                                      start=(j == 0), stop=(j == 1))
                        last.then_inc(s_la_v_mm, 1)
                    fill()
                    pe.wait_ge(s_la_v_copied, NT)

                    def turn_probs(n, probs, pt, v, h, fill):
                        for j in range(NT):
                            for i in range(j, NT):
                                last = turn(ps[:, j, i * P:(i + 1) * P], probs[:, i, j * P:(j + 1) * P], ident)
                        last.then_inc(s_probs_turned, 1)
                        fill()
                        pe.wait_ge(s_probs_t_copied, NT * (n + 1))
                        for j in range(NT):
                            last = mm(ps[:, 0, j * P:T], v[:, j, h * P:(h + 1) * P], pt[:, j, j * P:T],
                                      start=(j == 0), stop=(j == NT - 1))
                        last.then_inc(s_pv_done, 1)

                    for h in range(HEADS):
                        if h:
                            pe.wait_ge(s_y_ready, 4 + h)
                        q0 = h * 192
                        for j in range(3):
                            mm(ps[:, 0, :], la_wq[:, j, q0:q0 + P], la_in[:, j, :], start=(j == 0), stop=(j == 2))
                        for j in range(3):
                            mm(ps[0:64, 1, :], la_wq[:, j, q0 + P:q0 + 192], la_in[:, j, :],
                               start=(j == 0), stop=(j == 2))
                        for j in range(2):
                            last = mm(ps[:, 2, :], la_wkv[:, j, h * 256:h * 256 + P], la_in[:, 3 + j, :],
                                      start=(j == 0), stop=(j == 1))
                        last.then_inc(s_la_heads_mm, 1)
                        fill()
                        pe.wait_ge(s_la_heads_copied, h + 1)
                        mm(ps[:, 3, :], ones, la_hsq[:, 0, :], start=True, stop=False)
                        mm(ps[:, 3, :], ones[0:64, :], la_hsq[0:64, 1, :], start=False, stop=True)
                        mm(ps[:, 0, :], ones, la_hsq[:, 2, :], start=True, stop=False)
                        mm(ps[:, 0, :], ones[0:64, :], la_pesq[0:64, :], start=False, stop=True)
                        mm(ps[0:64, 1, :], rot_mla[0:64, :], la_qp[0:64, :], start=True, stop=True
                           ).then_inc(s_la_heads_sums, 1)
                        fill()
                        pe.wait_ge(s_la_qk_ready, h + 1)
                        for i in range(NT):
                            qs, ks = slice(i * P, (i + 1) * P), slice(0, (i + 1) * P)
                            mm(ps[:, i, ks], la_q[:, qs], la_k[:, ks], start=True, stop=False)
                            mm(ps[:, i, ks], la_qp[0:64, qs], la_kp[0:64, ks], start=False, stop=False)
                            mm(ps[:, i, qs], ident, neg, start=False, stop=True).then_inc(s_scores_mm, 1)
                        fill(2)
                        pe.wait_ge(s_probs_ready, h + 1)
                        turn_probs(h, la_p, la_pt, la_v, h, fill)
                        fill()

                    project(progress.through(G_Z_ML))
                    pe.wait_ge(s_y_ready, 8)
                    pe.wait_ge(s_ml_gates, 1)
                    for i in range(NT):
                        last = mm(ps[:, 3, 4 * i:4 * i + 4], ml_gt[0:36, i * P:(i + 1) * P], sel_u4[0:36, :],
                                  start=True, stop=True)
                    last.then_inc(s_ml_ucol_mm, 1)
                    pe.wait_ge(s_ml_ucol_ready, 1)
                    for h in range(HEADS):
                        if h:
                            pe.wait_ge(s_y_ready, 8 + h)
                        mm(ps[:, 0, :], sel_u[0:36, h * P:(h + 1) * P], ml_gt[0:36, :], start=True, stop=True)
                        mm(ps[:, 1, :], sel_f[0:36, h * P:(h + 1) * P], ml_gt[0:36, :], start=True, stop=True
                           ).then_inc(s_ml_u_mm, 1)
                        fill(2)
                        pe.wait_ge(s_ml_max, h + 1)
                        pe.wait_ge(s_ml_qk_ready, h + 1)
                        for i in range(NT):
                            last = mm(ps[:, i, i * P:T], ml_acc[:, 1, i * P:(i + 1) * P], ml_acc[:, 0, i * P:T],
                                      start=True, stop=True)
                        last.then_inc(s_ml_scores_mm, 1)
                        fill()
                        pe.wait_ge(s_ml_s_ready, h + 1)
                        for i in range(NT):
                            mm(ps[:, 0, i * P:T], ml_v[:, i, h * P:(h + 1) * P], ml_s[:, i, i * P:T],
                               start=(i == 0), stop=(i == NT - 1))
                        for i in range(NT):
                            last = mm(ps[:, 1, i * P:T], ones, ml_s[:, i, i * P:T],
                                      start=(i == 0), stop=(i == NT - 1))
                        last.then_inc(s_ml_num_mm, 1)
                        fill()
                        pe.wait_ge(s_ml_h_sq, h + 1)
                        mm(ps[:, 2, :], ones, ml_sq, start=True, stop=True).then_inc(s_ml_h_sum, 1)
                        fill()

                    project(progress.rest())
                    pe.wait_ge(s_y_ready, 12)
                    early = Progress(STEPS, STEPS + EARLY)

                    def out_product(n, k, bank, first, last_k):
                        pe.wait_ge(s_raw_split, n + 1)
                        w1, w2 = w_hi[:, n % N_SPLIT, :], w_lo[:, n % N_SPLIT, :]
                        for i in range(NT):
                            if first:
                                yield i
                            y1, y2 = h_hi[:, k, i * P:(i + 1) * P], h_lo[:, k, i * P:(i + 1) * P]
                            for j, (lhsT, rhs) in enumerate(((y1, w1), (y1, w2), (y2, w1))):
                                last = mm(bank[:, i, :], lhsT, rhs, start=(first and j == 0),
                                          stop=(last_k and j == 2))
                            if last_k and i < 3:
                                last.then_inc(s_out_done, 1)
                        last.then_inc(s_split_used, 1)

                    def fill_out(n=1):
                        for s in early.ahead(n):
                            c, k = divmod(s - STEPS, EARLY_K)
                            if c == 0:
                                pe.wait_ge(s_y_split, k + 1)
                            for i in out_product(s, k, ps_proj, k == 0, k == EARLY_K - 1):
                                if c:
                                    pe.wait_ge(s_out_added, 4 * (c - 1) + i + 1)
                                else:
                                    pe.wait_ge(s_proj_copied, 4 * NG)

                    for h in range(HEADS):
                        if h:
                            pe.wait_ge(s_y_ready, 12 + h)
                        pe.wait_ge(s_da_squared, h + 1)
                        mm(ps[:, 0, :], bones, da_sq[:, 0, :], start=True, stop=True)
                        mm(ps[:, 1, :], bones, da_sq[:, 1, :], start=True, stop=True)
                        mm(ps[:, 2, :], rot_da, da_g[:, 0, :], start=True, stop=True)
                        mm(ps[:, 3, :], rot_da, da_g[:, 1, :], start=True, stop=True).then_inc(s_da_sums, 1)
                        fill_out(FILL["da_sums"])
                        pe.wait_ge(s_da_qk_ready, h + 1)
                        for f in range(2):
                            if f:
                                fill_out(FILL["da_scores"])
                                pe.wait_ge(s_da_probs_exp, 8 * h + 4)
                            for i in (2 * f, 2 * f + 1):
                                qs, ks = slice(i * P, (i + 1) * P), slice(0, (i + 1) * P)
                                for m in range(2):
                                    half, b = slice(64 * m, 64 * m + 64), 2 * (i % 2) + m
                                    mm(ps[:, b, ks], da_g[half, 0, qs], da_g[half, 1, ks], start=True, stop=False)
                                    last = mm(ps[:, b, qs], ident, neg, start=False, stop=True)
                            last.then_inc(s_da_scores_mm, 1)
                        fill_out(FILL["da_half"])
                        pe.wait_ge(s_da_half, 2 * h + 2)
                        turn_probs(HEADS + h, da_a, da_pt, da_v, h, fill_out)
                        fill_out(FILL["da_osq"])
                        pe.wait_ge(s_da_osq_ready, h + 1)
                        mm(ps[:, 1, :], ones, da_osq, start=True, stop=True).then_inc(s_da_osum_mm, 1)
                        fill_out(FILL["da_gate"] if h < HEADS - 1 else EARLY)

                    pe.wait_ge(s_y_ready, 16)
                    for c in range(4):
                        bank = (ps, ps_proj)[c % 2]
                        for k in range(EARLY_K, KT):
                            s = STEPS + EARLY + c * LATE_K + k - EARLY_K
                            if c == 0:
                                pe.wait_ge(s_y_split, k + 1)
                            for i in out_product(s, k, bank, k == EARLY_K, k == KT - 1):
                                if c:
                                    pe.wait_ge(s_out_added, (13 if c == 1 else 4 * c + 9) + i)

                @block.scalar
                def _(act):
                    progress, counts = Progress(), [0]

                    def link(ins):
                        counts[0] += 1
                        ins.then_inc(s_act_order, 1)
                        act.wait_ge(s_act_order, counts[0])

                    def evacuate(steps):
                        for g in groups_ended(steps):
                            for m in range(4):
                                if m < 3:
                                    act.wait_ge(s_proj_done, 3 * g + m + 1)
                                else:
                                    act.wait_ge(s_split_used, KT * (g + 1))
                                if g:
                                    act.wait_ge(s_stored[m], 16 * g)
                                nc.scalar.activation(stage[:, m, :], ps_proj[:, m, :], ACT.Copy).then_inc(s_proj_copied, 1)
                                act.wait_ge(s_proj_copied, 4 * g + m + 1)
                                act.dma_start(p_dram[4 * g + m], stage[:, m, :]).then_inc(s_stored[m], 16)

                    def high_part(n):
                        act.wait_ge(s_raw_loaded[n % N_RAW], raw_target[n])
                        if n >= N_SPLIT:
                            act.wait_ge(s_split_used, n - N_SPLIT + 1)
                        nc.scalar.activation(w_hi[:, n % N_SPLIT, :], raw[:, n % N_RAW, :], ACT.Copy
                                             ).then_inc(s_hi_by_act, 1)

                    def fill(n=1):
                        evacuate(progress.ahead(n))

                    def wait_stored(g):
                        for m in range(4):
                            act.wait_ge(s_stored[m], 16 * (g + 1))

                    def gate(n, tile, z, e, yo):
                        act.dma_start(z, p_dram[z_tile(tile)]).then_inc(s_z_loaded, 16)
                        act.wait_ge(s_z_loaded, 16 * (n + 1))
                        nc.scalar.activation(e, z, ACT.Tanh, scale=0.5).then_inc(s_z_tanh, 1)
                        act.wait_ge(s_y_ready, n + 1)
                        act.dma_start(y_dram[tile], yo).then_inc(s_y_kept, 16)

                    def rstd(dst, src, n, eps):
                        link(nc.scalar.activation(dst, src, ACT.Ln, scale=1.0 / n, bias=eps))
                        return nc.scalar.activation(dst, dst, ACT.Exp, scale=-0.5)

                    junk = carve(0, D)
                    for i in range(NT):
                        act.wait_ge(s_setup_x[i], 16)
                        link(nc.scalar.activation(junk, x_tok[:, i, :], ACT.Square, accum_out=ms[:, i:i + 1]))
                    rstd(rs_x, ms, D, EPS).then_inc(s_x_mean, 1)
                    act.wait_ge(s_da_lam_mm, 1)
                    nc.scalar.activation(lam2, ps[:, 1, 0:2], ACT.Exp).then_inc(s_da_lam_exp, 1)
                    act.wait_ge(s_par_ready, 1)
                    for k in range(KT):
                        act.wait_ge(s_x_turned, k + 1)
                        nc.scalar.activation(h_hi[:, k, :], ps[:, k % 4, :], ACT.Copy, scale=col("norm_g", k)).then_inc(s_h_hi_ready, 1)

                    act.dma_start(rw_const, a["const"][:, RW_CONST[0]:RW_CONST[1]]).then_inc(s_rw_first_loaded, 16)
                    act.dma_start(rw_wup[0:32, :], a["rw_w_up"][layer]).then_inc(s_rw_first_loaded, 16)
                    act.dma_start(rw_wup[32:64, :], a["rw_a_up"][layer]).then_inc(s_rw_first_loaded, 16)
                    act.dma_start(rw_vup[0:32, :], a["rw_v_up"][0]).then_inc(s_rw_first_loaded, 16)
                    act.dma_start(rw_vdn, a["rw_v_dn"][0].rearrange("(k p) r -> p k r", p=P)).then_inc(s_rw_first_loaded, 16)
                    for n in range(HI_FIRST + 3):
                        if n < HI_FIRST:
                            high_part(n)
                        if n > KT and n % KT == 2:
                            evacuate(progress.ahead(KT))
                    wait_stored(G_MISC)
                    act.dma_start(rw_lora[0:64, 1:T + 1], p_dram[LORA, 0:64]).then_inc(s_rw_first_loaded, 16)
                    act.dma_start(rw_v[:, 0:2, 1:T + 1], p_dram[4 * G_V:4 * G_V + 2].rearrange("j p t -> p j t")).then_inc(s_rw_first_loaded, 16)
                    act.dma_start(rw_v[:, 2:4, 1:T + 1], p_dram[4 * G_V + 2:4 * G_V + 4].rearrange("j p t -> p j t")).then_inc(s_rw_first_loaded, 16)
                    act.dma_start(rw_in[:, 0, 1:T + 1], p_dram[4 * G_R]).then_inc(s_rw_rk_loaded, 16)
                    act.dma_start(rw_in[:, 1, 1:T + 1], p_dram[4 * G_K]).then_inc(s_rw_rk_loaded, 16)
                    act.wait_ge(s_rw_shifted, 1)
                    nc.scalar.activation(rw_lora[0:32, 1:T + 1], rw_lora[0:32, 1:T + 1], ACT.Tanh).then_inc(s_rw_lora_tanh, 1)
                    for hp in range(4):
                        act.wait_ge(s_rw_lora_mm, hp + 1)
                        link(nc.scalar.activation(rw_t[:, 0, :], ps[:, 0, :], ACT.Tanh, scale=0.5, bias=half_w0[:, hp:hp + 1]))
                        link(nc.scalar.activation(rw_t[:, 1, :], ps[:, 1, :], ACT.Tanh, scale=0.5, bias=half_a0[:, hp:hp + 1]))
                        nc.scalar.activation(rw_t[:, 2, :], ps[:, 2, :], ACT.Tanh, scale=0.5, bias=half_v0[:, hp:hp + 1]).then_inc(s_rw_sig_tanh, 1)
                        fill(8)
                        act.wait_ge(s_rw_decay, hp + 1)
                        link(nc.scalar.activation(rw_w, rw_c, ACT.Exp))
                        link(nc.scalar.activation(rw_wm, rw_cm, ACT.Exp))
                        nc.scalar.activation(rw_wi, rw_c, ACT.Exp, scale=-1.0).then_inc(s_rw_decay_exp, 1)
                        act.wait_ge(s_rw_kk_sum, hp + 1)
                        nc.scalar.activation(rw_nr, ps[:, 3, :], ACT.Sqrt).then_inc(s_rw_kk_root, 1)
                        fill(5)
                        act.wait_ge(s_rw_turned, hp + 1)
                        if hp < 3:
                            act.dma_start(rw_in[:, 0, 1:T + 1], p_dram[4 * G_R + hp + 1]).then_inc(s_rw_rk_loaded, 16)
                            act.dma_start(rw_in[:, 1, 1:T + 1], p_dram[4 * G_K + hp + 1]).then_inc(s_rw_rk_loaded, 16)
                        nc.scalar.activation(rw_abv[:, :, :, 0:64], ps[:, 0, :].rearrange("p (i h k) -> p i h k", i=NT, h=2), ACT.Copy).then_inc(s_rw_turned_copied, 1)
                        nc.scalar.activation(rw_bnT, ps[:, 1, :].rearrange("p (i c) -> p i c", i=NT), ACT.Copy).then_inc(s_rw_turned_copied, 1)
                        nc.scalar.activation(rw_ktT, ps[:, 2, :].rearrange("p (i c) -> p i c", i=NT), ACT.Copy).then_inc(s_rw_turned_copied, 1)
                        act.wait_ge(s_rw_v_turned, hp + 1)
                        nc.scalar.activation(rw_vT, ps[:, 0, :].rearrange("p (i c) -> p i c", i=NT), ACT.Copy).then_inc(s_rw_v_copied, 1)
                        fill()
                        for ip in range(2):
                            fill()
                        act.wait_ge(s_rw_x_first, hp + 1)
                        for h in range(2):
                            nc.scalar.activation(rw_x[:, 4 * h:4 * h + 4, :], ps[:, h, :].rearrange("p (i c) -> p i c", i=NT), ACT.Copy).then_inc(s_rw_x_ready, 1)
                        for h in range(2):
                            nc.scalar.activation(rw_abv[:, :, h, 64:P], ps[:, 2 + h, 0:256].rearrange("p (i c) -> p i c", i=NT), ACT.Copy).then_inc(s_rw_x_ready, 1)
                        fill()
                        for lv in range(len(LEVELS)):
                            fill()
                        fill()
                        for h in range(2):
                            act.wait_ge(s_rw_pu_mm, 2 * hp + h + 1)
                            nc.scalar.activation(rw_pu[:, 4 * h:4 * h + 4, :], ps[:, h, :].rearrange("p (i c) -> p i c", i=NT), ACT.Copy).then_inc(s_rw_pu_ready, 1)
                        fill()
                        act.wait_ge(s_rw_local, hp + 1)
                        for q in range(2):
                            nc.scalar.activation(rw_st[:, 1 + q:NCH + 1:2, :], ps[:, q, :].rearrange("p (i s c) -> p i s c", i=NT, s=2)[:, :, 1, :], ACT.Copy).then_inc(s_rw_h_copied, 1)
                        fill()
                        for c in range(1, NCH - 1):
                            if c % 2:
                                fill()
                        fill()
                        fill()
                        act.wait_ge(s_rw_var, hp + 1)
                        rstd(rw_nr, ps[:, 1, :], 64, GN_EPS).then_inc(s_rw_rstd, 1)
                        if hp == 0:
                            evacuate(progress.through(G_Z_RW))
                            wait_stored(G_Z_RW)
                        else:
                            fill()
                        gate(hp, hp, rw_z, rw_e, rw_yo)

                    act.wait_ge(s_y_kept, 16 * 4)
                    evacuate(progress.through(G_Z_LA))
                    wait_stored(G_Z_LA)
                    act.dma_start(at_const, a["const"][:, ATT_CONST[0]:ATT_CONST[1]]).then_inc(s_la_loaded, 16)
                    act.dma_start(la_in[:, 0:4, :], p_dram[4 * G_LAT:4 * G_LAT + 4].rearrange("j p t -> p j t")).then_inc(s_la_loaded, 16)
                    act.dma_start(la_in[:, 4, :], p_dram[KV1]).then_inc(s_la_loaded, 16)
                    act.dma_start(la_pe[0:64, :], p_dram[KPE, 0:64]).then_inc(s_la_loaded, 16)
                    act.dma_start(la_wq, a["mla_w_q_b"][layer].rearrange("(k p) n -> p k n", p=P)).then_inc(s_la_loaded, 16)
                    act.dma_start(la_wkv, a["mla_w_kv_b"][layer].rearrange("(k p) n -> p k n", p=P)).then_inc(s_la_loaded, 16)
                    act.wait_ge(s_la_sums, 1)
                    link(nc.scalar.activation(la_rs[:, 0, :], ps[:, 0, :], ACT.Ln, scale=1.0 / 384, bias=EPS))
                    link(nc.scalar.activation(la_rs[:, 1, :], ps[:, 1, :], ACT.Ln, scale=1.0 / 256, bias=EPS))
                    nc.scalar.activation(la_rs, la_rs, ACT.Exp, scale=-0.5).then_inc(s_la_rs_ready, 1)
                    fill()
                    for i in range(NT):
                        act.wait_ge(s_la_v_mm, i + 1)
                        nc.scalar.activation(la_v[:, i, :], ps[:, i, :], ACT.Copy).then_inc(s_la_v_copied, 1)
                    fill()

                    def copy_turned(n, pt):
                        act.wait_ge(s_probs_turned, n + 1)
                        for j in range(NT):
                            nc.scalar.activation(pt[:, j, j * P:T], ps[:, j, j * P:T], ACT.Copy).then_inc(s_probs_t_copied, 1)
                        fill()

                    for h in range(HEADS):
                        act.wait_ge(s_la_heads_mm, h + 1)
                        link(nc.scalar.activation(la_hsq[:, 0, :], ps[:, 0, :], ACT.Square))
                        link(nc.scalar.activation(la_hsq[0:64, 1, :], ps[0:64, 1, :], ACT.Square))
                        link(nc.scalar.activation(la_hsq[:, 2, :], ps[:, 2, :], ACT.Square))
                        link(nc.scalar.activation(la_q, ps[:, 0, :], ACT.Copy, scale=col("mla_q_g")))
                        link(nc.scalar.activation(la_qp[0:64, :], ps[0:64, 1, :], ACT.Copy, scale=col("mla_q_g", 1)[0:64, :]))
                        nc.scalar.activation(la_k, ps[:, 2, :], ACT.Copy, scale=col("mla_k_g")).then_inc(s_la_heads_copied, 1)
                        fill()
                        act.wait_ge(s_la_heads_sums, h + 1)
                        link(nc.scalar.activation(la_rs[:, 0, :], ps[:, 3, :], ACT.Ln, scale=1.0 / 192, bias=EPS))
                        link(nc.scalar.activation(la_rs[:, 1, :], ps[:, 0, :], ACT.Ln, scale=1.0 / 192, bias=EPS))
                        nc.scalar.activation(la_rs, la_rs, ACT.Exp, scale=-0.5).then_inc(s_la_heads_rs, 1)
                        fill()
                        act.wait_ge(s_row_max, h + 1)
                        for i in range(NT):
                            nc.scalar.activation(la_p[:, i, 0:(i + 1) * P], ps[:, i, 0:(i + 1) * P], ACT.Exp, scale=192.0 ** -0.5, bias=la_mx[:, i:i + 1], accum_out=la_sum[:, i:i + 1]).then_inc(s_probs_exp, 1)
                        fill(2)
                        copy_turned(h, la_pt)
                        gate(4 + h, 8 + h, la_z, la_e, la_yo)
                        fill()

                    act.wait_ge(s_y_kept, 16 * 8)
                    act.dma_start(ml_const, a["const"][:, ML_CONST[0]:ML_CONST[1]]).then_inc(s_ml_first_loaded, 16)
                    evacuate(progress.through(G_Z_ML))
                    wait_stored(G_Z_ML)
                    act.wait_ge(s_ml_cleared, 1)
                    act.dma_start(ml_gate[0:4, :], p_dram[GATES, 0:4]).then_inc(s_ml_first_loaded, 16)
                    act.dma_start(ml_gate[32:36, :], p_dram[GATES, 4:8]).then_inc(s_ml_first_loaded, 16)
                    act.dma_start(ml_v, p_dram[4 * G_MLV:4 * G_MLV + 4].rearrange("j p t -> p j t")).then_inc(s_ml_first_loaded, 16)
                    for h in range(HEADS):
                        act.dma_start(ml_in[:, 0, 3:T + 3], p_dram[4 * G_MLQ + h]).then_inc(s_ml_qk_loaded, 16)
                        act.dma_start(ml_in[:, 1, 3:T + 3], p_dram[4 * G_MLK + h]).then_inc(s_ml_qk_loaded, 16)
                        act.dma_start(ml_o, p_dram[4 * G_MLO + h]).then_inc(s_ml_qk_loaded, 16)
                        if h == 0:
                            act.wait_ge(s_ml_gate_abs, 1)
                            link(nc.scalar.activation(ml_sg[32:36, :], ml_sg[32:36, :], ACT.Exp, scale=-1.0))
                            nc.scalar.activation(ml_sg[32:36, :], ml_sg[32:36, :], ACT.Ln, bias=1.0).then_inc(s_ml_gate_log, 1)
                        act.wait_ge(s_ml_conv, h + 1)
                        nc.scalar.activation(ml_sil, ml_acc, ACT.Tanh, scale=0.5).then_inc(s_ml_conv_tanh, 1)
                        act.wait_ge(s_ml_qk_loaded, 48 * (h + 1))
                        nc.scalar.activation(ml_oe, ml_o, ACT.Tanh, scale=0.5).then_inc(s_ml_o_tanh, 1)
                        fill(2)
                        act.wait_ge(s_ml_max, h + 1)
                        link(nc.scalar.activation(ml_nf, ml_nf, ACT.Exp))
                        for i in range(NT):
                            nc.scalar.activation(ml_w[:, i, i * P:T], ml_w[:, i, i * P:T], ACT.Exp, scale=-1.0).then_inc(s_ml_w_exp, 1)
                        fill()
                        fill()
                        act.wait_ge(s_ml_h_sum, h + 1)
                        rstd(ml_rs, ps[:, 2, :], P, EPS).then_inc(s_ml_h_rs, 1)
                        fill()
                        gate(8 + h, 4 + h, ml_z, ml_e, ml_yo)

                    act.wait_ge(s_y_kept, 16 * 12)
                    evacuate(progress.rest())
                    wait_stored(NG - 1)
                    act.wait_ge(s_setup_out, 16)
                    act.dma_start(x_tok, x_dram).then_inc(s_x_prefetched, 16)
                    act.dma_start(at_const, a["const"][:, ATT_CONST[0]:ATT_CONST[1]]).then_inc(s_da_first_loaded, 16)
                    act.dma_start(da_v, p_dram[4 * G_DAV:4 * G_DAV + 4].rearrange("j p t -> p j t")).then_inc(s_da_first_loaded, 16)
                    for h in range(HEADS):
                        act.dma_start(da_in[:, 0, :], p_dram[4 * G_DAQ + h]).then_inc(s_da_loaded, 16)
                        act.dma_start(da_in[:, 1, :], p_dram[4 * G_DAK + h]).then_inc(s_da_loaded, 16)
                        act.wait_ge(s_da_loaded, 32 * (h + 1))
                        link(nc.scalar.activation(da_sq, da_in, ACT.Square))
                        link(nc.scalar.activation(da_g[:, 0, :], da_in[:, 0, :], ACT.Copy, scale=col("da_q_g")))
                        nc.scalar.activation(da_g[:, 1, :], da_in[:, 1, :], ACT.Copy, scale=col("da_k_g")).then_inc(s_da_squared, 1)
                        if h == 0:
                            act.wait_ge(s_split_used, STEPS)
                            for k in range(EARLY_K + 4):
                                if k >= 4:
                                    act.wait_ge(s_y_loaded[k % 4], 16 * (k // 4))
                                    nc.scalar.activation(h_hi[:, k - 4, :], stage[:, k % 4, :], ACT.Copy
                                                         ).then_inc(s_y_hi_ready, 1)
                                if k < EARLY_K:
                                    if k >= 4:
                                        act.wait_ge(s_y_split, k - 3)
                                    act.dma_start(stage[:, k % 4, :], y_dram[k]).then_inc(s_y_loaded[k % 4], 16)
                        act.wait_ge(s_da_sums, h + 1)
                        rstd(da_rs, ps[:, 0:2, :], 64, EPS).then_inc(s_da_rs_ready, 1)
                        for half in range(2):
                            act.wait_ge(s_da_row_max, 2 * h + half + 1)
                            for b in range(4):
                                i = 2 * half + b // 2
                                nc.scalar.activation(da_p[:, b, 0:(i + 1) * P], ps[:, b, 0:(i + 1) * P], ACT.Exp, scale=64.0 ** -0.5, bias=da_mx[:, b:b + 1], accum_out=da_sum[:, b:b + 1]).then_inc(s_da_probs_exp, 1)
                        copy_turned(HEADS + h, da_pt)
                        act.wait_ge(s_pv_done, HEADS + h + 1)
                        nc.scalar.activation(da_osq, ps[:, 0, :], ACT.Square).then_inc(s_da_osq_ready, 1)
                        act.wait_ge(s_da_osum_mm, h + 1)
                        rstd(da_ors, ps[:, 1, :], P, EPS).then_inc(s_da_ors_ready, 1)
                        act.dma_start(da_z, p_dram[z_tile(12 + h)]).then_inc(s_z_loaded, 16)
                        act.wait_ge(s_z_loaded, 16 * (12 + h + 1))
                        nc.scalar.activation(da_e, da_z, ACT.Tanh, scale=0.5).then_inc(s_z_tanh, 1)
                        act.wait_ge(s_y_ready, 12 + h + 1)
                        nc.scalar.activation(h_hi[:, EARLY_K + h, :], da_yo, ACT.Copy).then_inc(s_y_hi_ready, 1)

                    for n in range(HI_LAST, STEPS + EARLY + LATE):
                        high_part(n)
                    for c in range(4):
                        act.wait_ge(s_out_added, 16 + 4 * (c + 1))
                        act.dma_start(x_dram[:, :, c * G:(c + 1) * G], x_tok[:, :, c * G:(c + 1) * G]
                                      ).then_inc(s_out_kept, 16)
                    act.wait_ge(s_out_kept, 64)

                @block.vector
                def _(dve):
                    counts = [0]
                    v = nc.vector

                    def link(ins):
                        counts[0] += 1
                        ins.then_inc(s_dve_order, 1)
                        dve.wait_ge(s_dve_order, counts[0])

                    MUL, ADD, SUB, MAX, MIN = ALU.mult, ALU.add, ALU.subtract, ALU.max, ALU.min

                    def gate(n, j, z, e, yo, y):
                        dve.wait_ge(s_z_tanh, n + 1)
                        link(v.scalar_tensor_tensor(out=e, in0=e, scalar=1.0, in1=z, op0=ADD, op1=MUL))
                        if 0 < n <= EARLY_K:
                            dve.wait_ge(s_y_kept, 16 * n)
                        if n > EARLY_K:
                            dve.wait_ge(s_y_split, n)
                        v.scalar_tensor_tensor(out=yo, in0=y, scalar=half_beta[:, j:j + 1], in1=e, op0=MUL, op1=MUL
                                               ).then_inc(s_y_ready, 1)
                        dve.wait_ge(s_y_ready, n + 1)

                    dve.wait_ge(s_params_loaded, 16 * N_PARAM_DMAS)
                    v.tensor_tensor(lam_prod[0:64, :], lam4[0:64, 0:4:2], lam4[0:64, 1:4:2], MUL).then_inc(s_lam_ready, 1)
                    dve.wait_ge(s_params_turned, 1)
                    v.tensor_copy(par[:, 0:N_ROWS], ps[:, 0, 0:N_ROWS]).then_inc(s_par_ready, 1)
                    dve.wait_ge(s_par_ready, 1)
                    for dst, name in ((half_w0, "rw_w0"), (half_a0, "rw_a0"), (half_v0, "rw_v0"),
                                      (half_ka, "rw_k_a"), (half_ml_g, "ml_norm_g")):
                        link(v.tensor_scalar(dst, par[:, ROWS[name]:ROWS[name] + 4], 0.5, None, MUL))
                    link(v.tensor_scalar(half_beta, beta, 0.5, None, MUL))
                    link(v.tensor_scalar(one_m_half_ka, half_ka, -1.0, 1.0, MUL, ADD))
                    link(v.tensor_tensor(sub_gain, col("da_sub_g"), one_m_lam_init, MUL))
                    dve.wait_ge(s_da_lam_exp, 1)
                    link(v.tensor_tensor(neg_lam, lam2[:, 1:2], lam2[:, 0:1], SUB))
                    v.tensor_tensor(neg_lam, neg_lam, lam_init, SUB).then_inc(s_small_ready, 1)

                    dve.wait_ge(s_x_mean, 1)
                    for i in range(NT):
                        v.tensor_scalar(x_tok[:, i, :], x_tok[:, i, :], rs_x[:, i:i + 1], None, MUL).then_inc(s_x_scaled, 1)
                    for k in range(KT):
                        dve.wait_ge(s_h_hi_ready, k + 1)
                        v.scalar_tensor_tensor(out=h_lo[:, k, :], in0=ps[:, k % 4, :], scalar=col("norm_g", k), in1=h_hi[:, k, :].bitcast(F32), op0=MUL, op1=SUB).then_inc(s_h_split, 1)

                    def shift(x, mu, rows_=slice(0, P)):
                        link(v.tensor_tensor(rw_d[rows_, :], x[rows_, 0:T], x[rows_, 1:T + 1], SUB))
                        return v.scalar_tensor_tensor(out=x[rows_, 1:T + 1], in0=rw_d[rows_, :],
                                                      scalar=mu[rows_, :], in1=x[rows_, 1:T + 1], op0=MUL, op1=ADD)

                    dve.wait_ge(s_x_turned, KT)
                    link(v.memset(rw_lora[0:64, 0:1], 0.0))
                    link(v.memset(rw_in[:, :, 0:1], 0.0))
                    link(v.memset(rw_v[:, :, 0:1], 0.0))
                    dve.wait_ge(s_rw_first_loaded, 16 * 8)
                    shift(rw_lora, col("rw_mu", 12), slice(0, 64)).then_inc(s_rw_shifted, 1)
                    dve.wait_ge(s_rw_shifted, 1)
                    for j in range(4):
                        ins = shift(rw_v[:, j, :], col("rw_mu", 8 + j))
                        if j < 3:
                            link(ins)
                    ins.then_inc(s_rw_v_shifted, 1)
                    dve.wait_ge(s_rw_vdn_mm, 1)
                    v.tensor_copy(rw_vd[0:32, :], ps[0:32, 0, :]).then_inc(s_rw_vd_ready, 1)
                    for hp in range(4):
                        r, k, vv = rw_in[:, 0, 1:T + 1], rw_in[:, 1, 1:T + 1], rw_v[:, hp, 1:T + 1]
                        dve.wait_ge(s_rw_rk_loaded, 32 * (hp + 1))
                        for x, mu in ((rw_in[:, 0, :], col("rw_mu", hp)), (rw_in[:, 1, :], col("rw_mu", 4 + hp))):
                            link(v.tensor_tensor(rw_kf, x[:, 0:T], x[:, 1:T + 1], SUB))
                            link(v.scalar_tensor_tensor(out=x[:, 1:T + 1], in0=rw_kf, scalar=mu, in1=x[:, 1:T + 1], op0=MUL, op1=ADD))
                        link(v.tensor_scalar(rw_kk, k, col("rw_k_k", hp), None, MUL))
                        v.tensor_tensor(rw_sq, rw_kk, rw_kk, MUL).then_inc(s_rw_kk_sq, 1)
                        dve.wait_ge(s_rw_sig_tanh, hp + 1)
                        decay, rate, mix = rw_t[:, 0, :], rw_t[:, 1, :], rw_t[:, 2, :]
                        link(v.tensor_scalar(decay, decay, -0.5 * math.exp(-0.5), -0.5 * math.exp(-0.5), MUL, ADD))
                        link(v.tensor_tensor_scan(rw_c, reset, decay, 0.0, MUL, ADD))
                        v.tensor_tensor(rw_cm, rw_c, decay, SUB).then_inc(s_rw_decay, 1)
                        dve.wait_ge(s_rw_decay, hp + 1)
                        link(v.tensor_tensor(decay, v_first[:, hp, :], vv, SUB))
                        link(v.scalar_tensor_tensor(out=decay, in0=mix, scalar=1.0, in1=decay, op0=ADD, op1=MUL))
                        link(v.scalar_tensor_tensor(out=vv, in0=decay, scalar=half_flag, in1=vv, op0=MUL, op1=ADD))
                        link(v.tensor_copy(v_first[:, hp, :], vv))
                        link(v.tensor_scalar(rw_kf, rate, half_ka[:, hp:hp + 1], one_m_half_ka[:, hp:hp + 1], MUL, ADD))
                        link(v.tensor_tensor(rw_kf, rw_kf, k, MUL))
                        dve.wait_ge(s_rw_kk_root, hp + 1)
                        link(v.tensor_scalar(rw_nr, rw_nr, 1e-12, None, MAX))
                        link(v.reciprocal(rw_nr, rw_nr))
                        link(v.tensor_tensor(rw_kk, rw_kk, rw_nr, MUL))
                        link(v.scalar_tensor_tensor(out=rw_sq, in0=r, scalar=col("rw_r_k", hp), in1=rw_kf, op0=MUL, op1=MUL))
                        dve.wait_ge(s_rw_decay_exp, hp + 1)
                        by_tile = "p (i t) -> p i t"
                        link(v.tensor_tensor(rw_ar[:, :, 0, :], rw_wm.rearrange(by_tile, i=NT), rw_kk.rearrange(by_tile, i=NT), MUL))
                        link(v.tensor_tensor(rw_ar[:, :, 1, :], rw_w.rearrange(by_tile, i=NT), r.rearrange(by_tile, i=NT), MUL))
                        link(v.scalar_tensor_tensor(out=rw_beta, in0=rate, scalar=1.0, in1=rw_kk, op0=ADD, op1=MUL))
                        link(v.scalar_tensor_tensor(out=rw_beta, in0=rw_beta, scalar=0.5, in1=rw_wi, op0=MUL, op1=MUL))
                        link(v.tensor_tensor(rw_kappa, rw_kf, rw_wi, MUL))
                        by_chunk = "p (c t) -> p c t"
                        link(v.tensor_copy(rw_wl, rw_w.rearrange(by_chunk, c=NCH)[:, :, 63]))
                        last_w = rw_wl[:, :, None].to_broadcast([P, NCH, 64])
                        link(v.scalar_tensor_tensor(out=rw_bn.rearrange(by_chunk, c=NCH), in0=rw_beta.rearrange(by_chunk, c=NCH), scalar=-1.0, in1=last_w, op0=MUL, op1=MUL))
                        v.tensor_tensor(rw_kt.rearrange(by_chunk, c=NCH), rw_kappa.rearrange(by_chunk, c=NCH), last_w, MUL).then_inc(s_rw_factors, 1)
                        dve.wait_ge(s_rw_turned, hp + 1)
                        v.tensor_tensor(rw_bonus, ps[:, 3, :], vv, MUL).then_inc(s_rw_bonus_ready, 1)
                        for ip in range(2):
                            dve.wait_ge(s_rw_gram, 2 * hp + ip + 1)
                            for f, (dst, mask) in enumerate(((rw_gb, mask_b), (rw_gk, mask_k))):
                                for h in range(2):
                                    ins = v.tensor_tensor(dst[:, 4 * h + 2 * ip:4 * h + 2 * ip + 2, :], ps[:, 2 * f + h, :].rearrange("p (i c) -> p i c", i=2), mask[:, None, :].to_broadcast([P, 2, 256]), MUL)
                                    if f and h:
                                        ins.then_inc(s_rw_gram_masked, 1)
                                    else:
                                        link(ins)
                        for h in range(2):
                            j = slice(4 * h, 4 * h + 4)
                            link(v.tensor_tensor(rw_xt[:, j, :], rw_gb[:, j, 0:P], level1[:, None, :].to_broadcast([P, NT, P]), MUL))
                            ins = v.tensor_tensor(rw_xt[:, j, :], ident[:, None, :].to_broadcast([P, NT, P]), rw_xt[:, j, :], SUB)
                            if h:
                                ins.then_inc(s_rw_xt_first, 1)
                            else:
                                link(ins)
                        for lv in range(len(LEVELS)):
                            level_mask = levels[:, lv * P:(lv + 1) * P][:, None, :].to_broadcast([P, NT, P])
                            for h in range(2):
                                dve.wait_ge(s_rw_levelled, 10 * hp + 2 * lv + h + 1)
                                v.tensor_tensor(rw_y[:, 4 * h:4 * h + 4, :], ps[:, 2 * h, :].rearrange("p (i c) -> p i c", i=NT), level_mask, MUL).then_inc(s_rw_level_masked, 1)
                            for h in range(2):
                                dve.wait_ge(s_rw_level_mm, 10 * hp + 2 * lv + h + 1)
                                j = slice(4 * h, 4 * h + 4)
                                if lv < len(LEVELS) - 1:
                                    link(v.tensor_tensor(rw_x[:, j, :], rw_x[:, j, :], ps[:, 2 * h, :].rearrange("p (i c) -> p i c", i=NT), SUB))
                                v.tensor_tensor(rw_xt[:, j, :], rw_xt[:, j, :], ps[:, 2 * h + 1, :].rearrange("p (i c) -> p i c", i=NT), SUB).then_inc(s_rw_level_done, 1)
                        dve.wait_ge(s_rw_local, hp + 1)
                        link(v.tensor_tensor(rw_ar[:, :, 1, :], rw_ar[:, :, 1, :], ps[:, 2, :].rearrange(by_tile, i=NT), ADD))
                        link(v.tensor_copy(rw_yl, ps[:, 3, :]))
                        link(v.tensor_tensor(rw_wli, eye64[:, None, :].to_broadcast([P, NCH, 64]), last_w, MUL))
                        dve.wait_ge(s_rw_h_copied, 2 * hp + 2)
                        for q in range(2):
                            link(v.tensor_tensor(rw_gt[:, q:NCH:2, :], rw_wli[:, q:NCH:2, :], ps[:, q, :].rearrange("p (i s c) -> p i s c", i=NT, s=2)[:, :, 0, :], ADD))
                        v.memset(rw_st[:, 0, :], 0.0).then_inc(s_rw_local_ready, 1)
                        for c in range(1, NCH - 1):
                            dve.wait_ge(s_rw_state_mm, (NCH - 2) * hp + c)
                            for h in range(2):
                                half = slice(64 * h, 64 * h + 64)
                                ins = v.tensor_tensor(rw_st[half, c + 1, :], rw_st[half, c + 1, :], ps[half, h, c * 64:(c + 1) * 64], ADD)
                                if h:
                                    ins.then_inc(s_rw_state_ready, 1)
                                else:
                                    link(ins)
                        dve.wait_ge(s_rw_carried, hp + 1)
                        for h in range(2):
                            half = slice(64 * h, 64 * h + 64)
                            ins = v.tensor_tensor(rw_yl[half, :], rw_yl[half, :], ps[half, 2 + h, :], ADD)
                            if h:
                                ins.then_inc(s_rw_y_whole, 1)
                            else:
                                link(ins)
                        dve.wait_ge(s_rw_mean, hp + 1)
                        link(v.scalar_tensor_tensor(out=rw_yl, in0=ps[:, 0, :], scalar=-1.0 / 64, in1=rw_yl, op0=MUL, op1=ADD))
                        v.tensor_tensor(rw_sq, rw_yl, rw_yl, MUL).then_inc(s_rw_centred, 1)
                        dve.wait_ge(s_rw_rstd, hp + 1)
                        link(v.tensor_tensor(rw_yl, rw_yl, rw_nr, MUL))
                        link(v.tensor_scalar(rw_yl, rw_yl, col("rw_ln_w", hp), col("rw_ln_b", hp), MUL, ADD))
                        link(v.tensor_tensor(rw_yl, rw_yl, rw_bonus, ADD))
                        gate(hp, 0, rw_z, rw_e, rw_yo, rw_yl)

                    dve.wait_ge(s_la_loaded, 16 * 6)
                    link(v.tensor_tensor(la_sq, la_in, la_in, MUL))
                    pe64 = slice(0, 64)
                    link(v.tensor_scalar(la_peg[pe64, :], la_pe[pe64, :], col("mla_k_g", 1)[pe64, :], None, MUL))
                    v.tensor_tensor(la_pesq[pe64, :], la_pe[pe64, :], la_pe[pe64, :], MUL).then_inc(s_la_squared, 1)
                    dve.wait_ge(s_la_rs_ready, 1)
                    for j in range(5):
                        gain = col("mla_q_norm_g", j) if j < 3 else col("mla_kv_norm_g", j - 3)
                        link(v.scalar_tensor_tensor(out=la_in[:, j, :], in0=la_in[:, j, :], scalar=gain, in1=la_rs[:, int(j > 2), :], op0=MUL, op1=MUL))
                    link(v.tensor_tensor(la_tmp[pe64, :], ps[pe64, 2, :], sin_mla[pe64, :], MUL))
                    link(v.tensor_tensor(la_per[pe64, :], la_peg[pe64, :], cos_mla[pe64, :], MUL))
                    v.tensor_tensor(la_per[pe64, :], la_per[pe64, :], la_tmp[pe64, :], ADD).then_inc(s_la_latents, 1)

                    def row_maxima(mx, banks, scale):
                        for b, i in banks:
                            link(v.tensor_reduce(mx[:, b:b + 1], ps[:, b, 0:(i + 1) * P], AX, MAX))
                        return v.tensor_scalar(mx, mx, -scale, None, MUL)

                    for h in range(HEADS):
                        dve.wait_ge(s_la_heads_sums, h + 1)
                        link(v.tensor_tensor(la_tmp[pe64, :], ps[pe64, 1, :], sin_mla[pe64, :], MUL))
                        link(v.tensor_tensor(la_qp[pe64, :], la_qp[pe64, :], cos_mla[pe64, :], MUL))
                        link(v.tensor_tensor(la_qp[pe64, :], la_qp[pe64, :], la_tmp[pe64, :], ADD))
                        dve.wait_ge(s_la_heads_rs, h + 1)
                        link(v.tensor_tensor(la_qp[pe64, :], la_qp[pe64, :], la_rs[pe64, 0, :], MUL))
                        link(v.tensor_tensor(la_kp[pe64, :], la_per[pe64, :], la_rs[pe64, 1, :], MUL))
                        link(v.tensor_tensor(la_q, la_q, la_rs[:, 0, :], MUL))
                        v.tensor_tensor(la_k, la_k, la_rs[:, 1, :], MUL).then_inc(s_la_qk_ready, 1)
                        dve.wait_ge(s_scores_mm, NT * (h + 1))
                        row_maxima(la_mx, [(i, i) for i in range(NT)], 192.0 ** -0.5).then_inc(s_row_max, 1)
                        dve.wait_ge(s_probs_exp, NT * (h + 1))
                        link(v.reciprocal(la_sum, la_sum))
                        for i in range(NT):
                            ins = v.tensor_scalar(la_p[:, i, 0:(i + 1) * P], la_p[:, i, 0:(i + 1) * P], la_sum[:, i:i + 1], None, MUL)
                            if i == NT - 1:
                                ins.then_inc(s_probs_ready, 1)
                            else:
                                link(ins)
                        dve.wait_ge(s_pv_done, h + 1)
                        gate(4 + h, 2, la_z, la_e, la_yo, ps[:, 0, :])

                    link(v.memset(ml_gate, 0.0))
                    v.memset(ml_in[:, :, 0:3], 0.0).then_inc(s_ml_cleared, 1)
                    dve.wait_ge(s_ml_first_loaded, 16 * 4)
                    gates, forget = slice(0, 36), slice(32, 36)
                    link(v.tensor_scalar(ml_gt[gates, :], ml_gate[gates, :], gate_bias[gates, :], None, ADD))
                    v.scalar_tensor_tensor(out=ml_sg[forget, :], in0=ml_gt[forget, :], scalar=-1.0, in1=ml_gt[forget, :], op0=MUL, op1=MAX).then_inc(s_ml_gate_abs, 1)
                    dve.wait_ge(s_ml_gate_log, 1)
                    link(v.scalar_tensor_tensor(out=ml_sg[forget, :], in0=ml_gt[forget, :], scalar=0.0, in1=ml_sg[forget, :], op0=MIN, op1=SUB))
                    v.tensor_tensor_scan(ml_gt[forget, :], carry[forget, :], ml_sg[forget, :], 0.0, MUL, ADD).then_inc(s_ml_gates, 1)
                    dve.wait_ge(s_ml_ucol_mm, 1)
                    v.tensor_copy(ml_ucol, ps[:, 3, 0:4 * NT].rearrange("p (i h) -> p i h", i=NT)).then_inc(s_ml_ucol_ready, 1)
                    for h in range(HEADS):
                        dve.wait_ge(s_ml_qk_loaded, 48 * (h + 1))
                        for s, n in ((0, h), (1, 4 + h)):
                            link(v.tensor_scalar(ml_acc[:, s, :], ml_in[:, s, 3:T + 3], col("ml_conv_w", 24 + n), col("ml_conv_b", n), MUL, ADD))
                            for tap in (2, 1, 0):
                                ins = v.scalar_tensor_tensor(out=ml_acc[:, s, :], in0=ml_in[:, s, tap:tap + T], scalar=col("ml_conv_w", 8 * tap + n), in1=ml_acc[:, s, :], op0=MUL, op1=ADD)
                                if s and not tap:
                                    ins.then_inc(s_ml_conv, 1)
                                else:
                                    link(ins)
                        dve.wait_ge(s_ml_u_mm, h + 1)
                        link(v.tensor_tensor_scan(ml_m, carry, ps[:, 0, :], 0.0, MUL, MAX))
                        link(v.scalar_tensor_tensor(out=ml_nf, in0=ps[:, 1, :], scalar=-1.0, in1=ml_m, op0=MUL, op1=SUB))
                        for i in range(NT):
                            ins = v.tensor_scalar(ml_w[:, i, i * P:T], ml_m[:, i * P:T], ml_ucol[:, i, h:h + 1], 0.0, SUB, MAX)
                            if i == NT - 1:
                                ins.then_inc(s_ml_max, 1)
                            else:
                                link(ins)
                        dve.wait_ge(s_ml_conv_tanh, h + 1)
                        v.scalar_tensor_tensor(out=ml_acc, in0=ml_sil, scalar=1.0, in1=ml_acc, op0=ADD, op1=MUL).then_inc(s_ml_qk_ready, 1)
                        dve.wait_ge(s_ml_scores_mm, h + 1)
                        dve.wait_ge(s_ml_w_exp, NT * (h + 1))
                        for i in range(NT):
                            link(v.scalar_tensor_tensor(out=ml_s[:, i, i * P:T], in0=ps[:, i, i * P:T], scalar=0.25 * float(P) ** -0.5, in1=ml_w[:, i, i * P:T], op0=MUL, op1=MUL))
                            ins = v.tensor_tensor(ml_s[:, i, i * P:(i + 1) * P], ml_s[:, i, i * P:(i + 1) * P], causal, MUL)
                            if i == NT - 1:
                                ins.then_inc(s_ml_s_ready, 1)
                            else:
                                link(ins)
                        dve.wait_ge(s_ml_num_mm, h + 1)
                        link(v.scalar_tensor_tensor(out=ml_den, in0=ps[:, 1, :], scalar=-1.0, in1=ml_nf, op0=MUL, op1=MAX))
                        link(v.tensor_tensor(ml_den, ps[:, 1, :], ml_den, MAX))
                        link(v.reciprocal(ml_den, ml_den))
                        link(v.tensor_tensor(ml_h, ps[:, 0, :], ml_den, MUL))
                        v.tensor_tensor(ml_sq, ml_h, ml_h, MUL).then_inc(s_ml_h_sq, 1)
                        dve.wait_ge(s_ml_o_tanh, h + 1)
                        dve.wait_ge(s_ml_h_rs, h + 1)
                        link(v.scalar_tensor_tensor(out=ml_h, in0=ml_h, scalar=half_ml_g[:, h:h + 1], in1=ml_rs, op0=MUL, op1=MUL))
                        link(v.scalar_tensor_tensor(out=ml_h, in0=ml_oe, scalar=1.0, in1=ml_h, op0=ADD, op1=MUL))
                        gate(8 + h, 1, ml_z, ml_e, ml_yo, ml_h)

                    def split_y(k, y):
                        dve.wait_ge(s_y_hi_ready, k + 1)
                        v.tensor_tensor(h_lo[:, k, :], y, h_hi[:, k, :].bitcast(F32), SUB).then_inc(s_y_split, 1)

                    def add_out(c, bank, steps):
                        for i in range(NT):
                            if i < 3:
                                dve.wait_ge(s_out_done, 3 * taken[0] + i + 1)
                            else:
                                dve.wait_ge(s_split_used, steps)
                            part = x_tok[:, i, c * G:(c + 1) * G]
                            v.tensor_tensor(part, part, bank[:, i, :], ADD).then_inc(s_out_added, 1)
                        taken[0] += 1

                    def fill_out(n=1):
                        for c in early_ended(early.ahead(n)):
                            if c == 0:
                                dve.wait_ge(s_x_prefetched, 16)
                            add_out(c, ps_proj, STEPS + EARLY_K * (c + 1))

                    for k in range(EARLY_K):
                        split_y(k, stage[:, k % 4, :])
                    early, taken = Progress(STEPS, STEPS + EARLY), [0]
                    dve.wait_ge(s_da_first_loaded, 32)
                    for h in range(HEADS):
                        dve.wait_ge(s_da_sums, h + 1)
                        wide_sin, wide_cos = (t[:, None, :].to_broadcast([P, 2, T]) for t in (sin_da, cos_da))
                        link(v.tensor_tensor(da_qk, ps[:, 2:4, :], wide_sin, MUL))
                        link(v.tensor_tensor(da_g, da_g, wide_cos, MUL))
                        link(v.tensor_tensor(da_g, da_g, da_qk, ADD))
                        dve.wait_ge(s_da_rs_ready, h + 1)
                        v.tensor_tensor(da_g, da_g, da_rs, MUL).then_inc(s_da_qk_ready, 1)
                        fill_out(FILL["da_sums"])
                        for f in range(2):
                            if f:
                                fill_out(FILL["da_scores"])
                            dve.wait_ge(s_da_scores_mm, 2 * h + f + 1)
                            row_maxima(da_mx, [(b, 2 * f + b // 2) for b in range(4)], 64.0 ** -0.5).then_inc(s_da_row_max, 1)
                            dve.wait_ge(s_da_probs_exp, 8 * h + 4 * f + 4)
                            link(v.reciprocal(da_sum, da_sum))
                            link(v.tensor_scalar(da_sum[:, 1:4:2], da_sum[:, 1:4:2], neg_lam, None, MUL))
                            for i in (2 * f, 2 * f + 1):
                                b, ks = 2 * (i % 2), slice(0, (i + 1) * P)
                                link(v.tensor_scalar(da_a[:, i, ks], da_p[:, b, ks], da_sum[:, b:b + 1], None, MUL))
                                ins = v.scalar_tensor_tensor(out=da_a[:, i, ks], in0=da_p[:, b + 1, ks], scalar=da_sum[:, b + 1:b + 2], in1=da_a[:, i, ks], op0=MUL, op1=ADD)
                                if i % 2:
                                    ins.then_inc(s_da_half, 1)
                                else:
                                    link(ins)
                        fill_out(FILL["da_half"])
                        fill_out()
                        dve.wait_ge(s_da_ors_ready, h + 1)
                        link(v.scalar_tensor_tensor(out=da_o, in0=ps[:, 0, :], scalar=sub_gain, in1=da_ors, op0=MUL, op1=MUL))
                        gate(12 + h, 3, da_z, da_e, da_yo, da_o)
                        split_y(EARLY_K + h, da_yo)
                        fill_out(FILL["da_osq"])
                        fill_out(FILL["da_gate"] if h < HEADS - 1 else EARLY)

                    link(v.memset(half_flag, 0.5))
                    link(v.memset(lam_init, 0.8 - 0.6 * math.exp(-0.3)))
                    link(v.memset(one_m_lam_init, 1.0 - (0.8 - 0.6 * math.exp(-0.3))))

                    for c in range(4):
                        add_out(c, (ps, ps_proj)[c % 2], STEPS + EARLY + LATE_K * (c + 1))

            nc.all_engine_barrier(sems_to_clear=of_layer)


_INS = ["x", "norm_g", "w_in", "w_out", "branch_beta", "rw_mu", "rw_w0", "rw_w_up", "rw_a0", "rw_a_up", "rw_v0",
        "rw_v_dn", "rw_v_up", "rw_k_k", "rw_k_a", "rw_r_k", "rw_ln_w", "rw_ln_b", "ml_conv_w", "ml_conv_b", "ml_i_b",
        "ml_f_b", "ml_norm_g", "mla_q_norm_g", "mla_kv_norm_g", "mla_w_q_b", "mla_w_kv_b", "mla_q_g", "mla_k_g",
        "da_q_g", "da_k_g", "da_lq1", "da_lk1", "da_lq2", "da_lk2", "da_sub_g"]
_OUT = ((1, T, D), "float32")


def kernel(**inputs):
    import concourse.bacc as _bacc
    from concourse.bass_utils import run_bass_kernel_spmd as _run

    nc = _bacc.Bacc("TRN2", target_bir_lowering=False, num_devices=1)
    arrays, args = {}, {}
    given = {name: np.ascontiguousarray(inputs[name]) for name in _INS}
    given["const"] = constants()
    for name, a in given.items():
        arrays[f"in_{name}_dram"] = a
        args[name] = nc.dram_tensor(f"in_{name}_dram", a.shape, mybir.dt.from_np(a.dtype), kind="ExternalInput").ap()
    out = nc.dram_tensor("out_0_dram", _OUT[0], mybir.dt.from_np(np.dtype(_OUT[1])), kind="ExternalOutput").ap()
    build(nc, args, out)
    r = _run(nc, [arrays], core_ids=[0])
    return r.results[0]["out_0_dram"]
```

```python
from contextlib import ExitStack
import math

import numpy as np

import concourse.bass as bass
from concourse import mybir

BF16 = mybir.dt.bfloat16
F32 = mybir.dt.float32
F32R = mybir.dt.float32r
ALU = mybir.AluOpType
ACT = mybir.ActivationFunctionType
AX = mybir.AxisListType.X

P = 128
D, T, DEPTH = 2048, 512, 2
NT = T // P
KT = D // P
G = 512
EPS = 1e-6
GN_EPS = 64e-5
HEADS = 4
RW_CHUNK = 64
NCH = T // RW_CHUNK
LEVELS = (2, 4, 8, 16, 32)
MASKED = -1e30

Z0 = 0
RW0 = D
RW_COLS = 3 * G + 64
ML0 = RW0 + RW_COLS
MLA0 = ML0 + 4 * G + 8
DA0 = MLA0 + 704
N_IN = DA0 + 3 * G

PIECES = (
    [[(RW0 + j * G, G)] for j in range(3)]
    + [[(MLA0 + 512, P + 64), (RW0 + 3 * G, 64), (ML0 + 4 * G, P)]]
    + [[(Z0, G)], [(MLA0, G)], [(Z0 + 2 * G, G)]]
    + [[(ML0 + j * G, G)] for j in range(4)]
    + [[(Z0 + G, G)]]
    + [[(DA0 + j * G, G)] for j in range(3)]
    + [[(Z0 + 3 * G, G)]]
)
(G_R, G_K, G_V, G_MISC, G_Z_RW, G_LAT, G_Z_LA, G_MLQ, G_MLK, G_MLV, G_MLO, G_Z_ML, G_DAQ, G_DAK, G_DAV, G_Z_DA) = range(16)
NG = len(PIECES)
TOKEN_MAJOR = (G_MLV, G_DAV)
KV1, KPE_LORA, GATES = (4 * G_MISC + j for j in range(3))
STEPS = NG * KT
EARLY_K, LATE_K = 12, 4
EARLY, LATE = 4 * EARLY_K, 4 * LATE_K
HI_FIRST, HI_LAST = 4 * KT, STEPS + EARLY + 4
N_RAW, N_SPLIT = 6, 4
FILL = dict(
    rw_first=8, rw_lora=(0, 0, 0, 0), rw_factors=(7, 7, 7, 7), rw_turned=(1, 1, 1, 1), rw_v=(0, 0, 0, 0),
    rw_gram=(1, 1, 1, 1), rw_xt=(1, 1, 1, 1), rw_x=(1, 1, 1, 1), rw_level=(0, 0, 0, 0), rw_levels=(0, 0, 0, 0),
    rw_pu=(0, 0, 0, 0), rw_local=(1, 1, 1, 1), rw_state=(0, 0, 0, 0), rw_carried=(1, 1, 1, 1), rw_mean=(0, 0, 0, 0),
    rw_gate=(3, 3, 3, 3), la_first=9, la_sums=4, la_v=1, la_heads=(2, 2, 2, 2), la_qk=(3, 3, 2, 3),
    la_probs=(3, 3, 3, 3), la_gate=(1, 1, 1, 1), ml_first=7, ml_qk=(3, 3, 4, 3), ml_s=(1, 1, 1, 1),
    ml_h=(3, 3, 3, 3), ml_gate=(3, 3, 3, 3), da_first=5, da_sums=(4, 8, 3, 3), da_scores=(2, 2, 2, 1),
    da_half=(3, 4, 3, 3), da_osq=(1, 1, 1, 1), da_gate=(3, 3, 3, 3), la_turned=(1, 1, 1, 1), da_turned=(1, 1, 1, 1))

COLS, _at = {}, 0
for _name, _n in (("rw_mu", 13), ("rw_w0", 4), ("rw_a0", 4), ("rw_v0", 4), ("rw_k_k", 4), ("rw_k_a", 4),
                  ("rw_r_k", 4), ("rw_ln_w", 4), ("rw_ln_b", 4), ("ml_conv_w", 32), ("ml_conv_b", 8),
                  ("ml_norm_g", 4), ("mla_q_norm_g", 3), ("mla_kv_norm_g", 2), ("mla_q_g", 2),
                  ("mla_k_g", 2), ("da_q_g", 1), ("da_k_g", 1), ("da_sub_g", 1), ("norm_g", 16),
                  ("gate_bias", 1), ("lambdas", 4)):
    COLS[_name] = _at
    _at += _n
N_PAR = _at

CONST = {}
_at = 0
for _name, _n in (("ident", P), ("ones", P), ("bones", P), ("eps", 2),
                  ("mask_b", 256), ("mask_k", 256), ("levels", 5 * P), ("level1", P), ("reset", T),
                  ("eye64", 64),
                  ("neg", P), ("rot_mla", 64), ("rot_da", P), ("cos_mla", T), ("sin_mla", T),
                  ("cos_da", T), ("sin_da", T),
                  ("causal", P), ("sel_u", 4 * P), ("sel_f", 4 * P), ("sel_u4", 4), ("pass", T)):
    CONST[_name] = (_at, _n)
    _at += _n
N_CONST = _at
ALWAYS = CONST["mask_b"][0]
RW_CONST = (ALWAYS, CONST["neg"][0])
ATT_CONST = (CONST["rot_mla"][0], CONST["causal"][0])
ML_CONST = (CONST["causal"][0], N_CONST)


def constants():
    c = np.zeros((P, N_CONST), np.float32)

    def put(name, a):
        c[:a.shape[0], CONST[name][0]:CONST[name][0] + a.shape[1]] = a

    r, q = np.arange(P)[:, None], np.arange(P)[None, :]
    put("ident", np.eye(P))
    put("ones", np.ones((P, P)))
    same = r // 64 == q // 64
    put("bones", same * 1.0)
    put("eps", np.tile(np.array([[EPS, GN_EPS]]), (P, 1)))
    strict, incl = same & (r < q), same & (r <= q)
    put("mask_b", np.concatenate([strict * 1.0, incl * -1.0], 1))
    put("mask_k", np.concatenate([strict * 1.0, incl * 1.0], 1))
    put("levels", np.concatenate([
        (r // (2 * b) == q // (2 * b)) & (r // b % 2 == 1) & (q // b % 2 == 0) for b in LEVELS], 1) * 1.0)
    put("level1", ((q == r + 1) & (r % 2 == 0)) * 1.0)
    put("reset", np.tile((np.arange(T) % RW_CHUNK != 0) * 1.0, (P, 1)))
    put("eye64", (r % 64 == np.arange(64)[None, :]) * 1.0)
    put("neg", (q > r) * MASKED)
    theta = np.float32(500000.0)

    def tables(rot):
        inv = theta ** (-np.arange(0, rot, 2, dtype=np.float32) / np.float32(rot))
        ang = np.arange(T, dtype=np.float32)[:, None] * inv[None, :]
        return np.cos(ang).T.astype(np.float32), np.sin(ang).T.astype(np.float32)

    cs, sn = tables(64)
    put("cos_mla", np.concatenate([cs, cs]))
    put("sin_mla", np.concatenate([sn, sn]))

    def rotation(n, half, block):
        m = np.zeros((n, n), np.float32)
        for b in range(0, n, block):
            for j in range(half):
                m[b + half + j, b + j] = -1.0
                m[b + j, b + half + j] = 1.0
        return m

    put("rot_mla", rotation(64, 32, 64))
    put("rot_da", rotation(P, 8, 64))
    cs, sn = tables(16)
    cd, sd = np.ones((P, T), np.float32), np.zeros((P, T), np.float32)
    for b in (0, 64):
        cd[b:b + 16], sd[b:b + 16] = np.concatenate([cs, cs]), np.concatenate([sn, sn])
    put("cos_da", cd)
    put("sin_da", sd)
    put("causal", (r <= q) * 1.0)
    su, sf, s4 = np.zeros((36, 4 * P)), np.zeros((36, 4 * P)), np.zeros((36, 4))
    for h in range(HEADS):
        su[h, h * P:(h + 1) * P], su[32 + h, h * P:(h + 1) * P] = 1.0, -1.0
        sf[32 + h, h * P:(h + 1) * P] = 1.0
        s4[h, h], s4[32 + h, h] = 1.0, -1.0
    put("sel_u", su)
    put("sel_f", sf)
    put("sel_u4", s4)
    put("pass", np.ones((P, T)))
    return c


def parameters(given):
    table = np.zeros((P, DEPTH, N_PAR + 4), np.float32)

    def put(name, layer, values, at=0):
        first = COLS[name]
        table[at:at + values.shape[1], layer, first:first + values.shape[0]] = values.T

    for layer in range(DEPTH):
        for name in ("rw_w0", "rw_a0", "rw_k_k", "rw_k_a", "rw_ln_w", "rw_ln_b", "rw_r_k", "ml_conv_w", "ml_conv_b",
                     "ml_norm_g", "mla_q_norm_g", "mla_kv_norm_g", "da_sub_g", "norm_g"):
            put(name, layer, given[name][layer].reshape(-1, P))
        put("rw_v0", layer, given["rw_v0"][0].reshape(-1, P))
        put("rw_mu", layer, given["rw_mu"][layer, :3 * G].reshape(-1, P))
        table[0:64, layer, COLS["rw_mu"] + 12] = given["rw_mu"][layer, 3 * G:]
        for name in ("mla_q_g", "mla_k_g"):
            table[:, layer, COLS[name]] = given[name][layer, :P]
            table[0:64, layer, COLS[name] + 1] = given[name][layer, P:]
        for name in ("da_q_g", "da_k_g"):
            for half in range(2):
                put(name, layer, given[name][layer:layer + 1], 64 * half)
        for at, name in ((0, "ml_i_b"), (32, "ml_f_b")):
            put("gate_bias", layer, given[name][layer:layer + 1], at)
        for j, name in enumerate(("da_lq1", "da_lk1", "da_lq2", "da_lk2")):
            table[0:64, layer, COLS["lambdas"] + j] = given[name][layer]
        table[:, layer, N_PAR:] = given["branch_beta"][layer]
    return table


class Progress:

    def __init__(self, first=0, end=STEPS):
        self.done, self.end = first, end

    def ahead(self, n):
        first, self.done = self.done, min(self.end, self.done + n)
        return range(first, self.done)

    def rest(self):
        return self.ahead(self.end - self.done)

    def through(self, group):
        return self.ahead(max(0, (group + 1) * KT - self.done))


def tiles_of(g):
    return 3 if g == G_MISC else 4


def tiles_before(g):
    return 4 * g - (g > G_MISC)


def groups_ended(steps):
    return [n // KT for n in steps if n % KT == KT - 1]


def early_ended(steps):
    return [(n - STEPS) // EARLY_K for n in steps if (n - STEPS) % EARLY_K == EARLY_K - 1]


def y_count(k):
    return 1 if k == EARLY_K else k + 2 if k < EARLY_K else k + 1


def z_tile(tile):
    return 4 * (G_Z_RW, G_Z_ML, G_Z_LA, G_Z_DA)[tile // 4] + tile % 4


def build(nc, a, out):
    with ExitStack() as ctx:
        def sb(name, shape, dt=F32):
            return ctx.enter_context(nc.sbuf_tensor(name, shape, dt))

        def sem(name):
            return ctx.enter_context(nc.semaphore(name))

        h_hi = sb("h_hi", [P, KT, T], F32R)
        h_lo = sb("h_lo", [P, KT, T], F32R)
        raw = sb("raw", [P, N_RAW, G])
        w_hi = sb("w_hi", [P, N_SPLIT, G], F32R)
        w_lo = sb("w_lo", [P, N_SPLIT, G], F32R)
        always = sb("always", [P, ALWAYS])
        par_all = sb("par_all", [P, DEPTH, N_PAR + 4])
        par = sb("par", [P, N_PAR + 4])
        mask_ident = sb("mask_ident", [P, P], BF16)[:]
        neg = sb("neg", [P, P], BF16)[:]
        small = sb("small", [P, 80])
        v_first = sb("v_first", [P, 4, T])
        stage = sb("stage", [P, 4, T])
        ARENA = 24528
        arena = sb("arena", [P, ARENA])

        def carve(at, *shape):
            n = int(np.prod(shape))
            assert at + n <= ARENA, (at, n)
            v = arena[:, at:at + n]
            if len(shape) == 2:
                v = v.rearrange("p (a b) -> p a b", a=shape[0])
            if len(shape) == 3:
                v = v.rearrange("p (a b c) -> p a b c", a=shape[0], b=shape[1])
            return v

        class Region:

            def __init__(self, at=0):
                self.at = at

            def __call__(self, *shape):
                v = carve(self.at, *shape)
                self.at += int(np.prod(shape))
                return v

        def const(name, region=None, first=0):
            at, n = CONST[name]
            return (always if region is None else region)[:, at - first:at - first + n]

        ps_proj = ctx.enter_context(nc.psum_tensor("ps_proj", [P, 4, 512], F32))
        ps = ctx.enter_context(nc.psum_tensor("ps", [P, 4, 512], F32))

        p_dram = nc.dram_tensor("projected", (4 * NG, P, T), F32, kind="Internal").ap()
        y_dram = nc.dram_tensor("gated", (KT, P, T), F32, kind="Internal").ap()
        x_dram = out[0].rearrange("(i p) d -> p i d", p=P)

        ident, ones, bones = const("ident"), const("ones"), const("bones")
        eps_col, gn_eps_col = const("eps")[:, 0:1], const("eps")[:, 1:2]
        x_tok = carve(ARENA - NT * D, NT, D)

        def col(name, j=0):
            return par[:, COLS[name] + j:COLS[name] + j + 1]

        beta = par[:, N_PAR:N_PAR + 4]
        lam4 = par[:, COLS["lambdas"]:COLS["lambdas"] + 4]
        gate_bias = par[:, COLS["gate_bias"]:COLS["gate_bias"] + 1]
        half_w0, half_a0, half_v0 = small[:, 4:8], small[:, 8:12], small[:, 12:16]
        one_m_half_ka = small[:, 16:20]
        half_ka, half_beta, half_ml_g = small[:, 41:45], small[:, 45:49], small[:, 49:53]
        lam2 = small[:, 25:27]
        neg_lam = small[:, 27:28]
        sub_gain = small[:, 28:29]
        ms = small[:, 32:36]
        ms_parts = small[:, 64:80].rearrange("p (i c) -> p i c", i=NT)
        rs_x = small[:, 36:40]
        lam_prod = small[:, 29:31]
        half_flag = small[:, 60:61]
        lam_init = small[:, 61:62]
        one_m_lam_init = small[:, 62:63]



        s_setup, s_setup_out, s_flags = sem("setup_loaded"), sem("x_kept"), sem("flags_set")
        s_setup_squared = sem("setup_squared")
        s_params_loaded = sem("params_loaded")
        s_setup_x = [sem(f"x_loaded_{i}") for i in range(NT)]
        neg_f32 = carve(D, P)

        with nc.Block() as block:
            @block.sync
            def _(sp):
                for i in range(NT):
                    sp.dma_start(x_tok[:, i, :], a["x"][0, i * P:(i + 1) * P, :]).then_inc(s_setup_x[i], 16)
                sp.dma_start(par_all[:], a["params"]).then_inc(s_params_loaded, 16)
                sp.dma_start(always[:], a["const"][:, 0:ALWAYS]).then_inc(s_setup, 16)
                sp.dma_start(neg_f32, a["const"][:, CONST["neg"][0]:CONST["neg"][0] + P]).then_inc(s_setup, 16)
                sp.dma_start(out[0], a["x"][0]).then_inc(s_setup_out, 16)

            @block.scalar
            def _(act):
                act.wait_ge(s_flags, 1)
                for i in range(NT):
                    act.wait_ge(s_setup_x[i], 16)
                    nc.scalar.activation(carve(0, D), x_tok[:, i, :], ACT.Square, accum_out=ms_parts[:, i, 0:1]
                                         ).then_inc(s_setup_squared, 1)
                    act.wait_ge(s_setup_squared, i + 1)

            @block.vector
            def _(dve):
                nc.vector.memset(small[:, 64:80], 0.0).then_inc(s_flags, 1)
                nc.vector.memset(v_first[:], 0.0).then_inc(s_flags, 1)
                nc.vector.memset(small[:, 0:60], 0.0).then_inc(s_flags, 1)
                nc.vector.memset(half_flag, 0.0).then_inc(s_flags, 1)
                nc.vector.memset(lam_init, 0.8 - 0.6).then_inc(s_flags, 1)
                nc.vector.memset(one_m_lam_init, 1.0 - (0.8 - 0.6)).then_inc(s_flags, 1)
                dve.wait_ge(s_setup, 32)
                nc.vector.tensor_copy(mask_ident, ident).then_inc(s_flags, 1)
                nc.vector.tensor_copy(neg, neg_f32).then_inc(s_flags, 1)
                dve.wait_ge(s_flags, 8)

        rg = Region()
        rw_const = rg(RW_CONST[1] - RW_CONST[0])
        rw_lora = rg(T + 1)
        rw_in = rg(2, T + 1)
        rw_v = rg(4, T + 1)
        rw_d = rg(T)
        reused = rg.at
        rw_t = rg(3, T)
        rw_c, rw_cm, rw_wm, rw_wi, rw_kk = rg(T), rg(T), rg(T), rg(T), rg(T)
        rw_w, rw_sq, rw_nr, rw_kf = rg(T), rg(T), rg(T), rg(T)
        rw_ar = rg(NT, 2, P)
        rw_beta, rw_kappa = rg(T), rg(T)
        rw_bn_at = rg.at
        rw_bn, rw_kt = rg(T), rg(T)
        rw_bonus = rg(T)
        rw_abv = rg(NT, 2, P)
        rw_bnT, rw_ktT, rw_vT = rg(NT, P), rg(NT, P), rg(NT, P)
        rw_gb, rw_gk = rg(8, 256), rg(8, 256)
        rw_wup, rw_vup = rg(G), rg(G)
        rw_vdn = rg(4, 32)
        rw_z, rw_yo = rg(T), rg(T)
        rw_wl = rg(NCH)
        r2 = Region(reused)
        rw_xt, rw_x, rw_y, rw_pu = r2(8, P), r2(8, P), r2(8, P), r2(8, P)
        assert r2.at <= reused + 3 * T + 5 * T
        rw_gt = rw_beta.rearrange("p (c k) -> p c k", c=NCH)
        rw_wli = rw_kappa.rearrange("p (c k) -> p c k", c=NCH)
        rw_st = carve(rw_bn_at, NCH + 1, 64)
        rw_yl, rw_e, rw_vd = rw_kf, rw_w, rw_d
        mask_b = const("mask_b", rw_const, RW_CONST[0])
        mask_k = const("mask_k", rw_const, RW_CONST[0])
        levels = const("levels", rw_const, RW_CONST[0])
        level1 = const("level1", rw_const, RW_CONST[0])
        reset = const("reset", rw_const, RW_CONST[0])
        eye64 = const("eye64", rw_const, RW_CONST[0])

        rg = Region()
        at_const = rg(ATT_CONST[1] - ATT_CONST[0])
        la_in = rg(5, T)
        la_pe = rg(T)
        la_p_at = rg.at
        la_sq = rg(5, T)
        la_p = carve(la_p_at, NT, T)
        la_wq = rg(3, 768)
        la_wkv = rg(2, 1024)
        la_rs = rg(2, T)
        la_peg, la_per, la_pesq = rg(T), rg(T), rg(T)
        la_v = rg(NT, G)
        la_hsq = rg(3, T)
        la_q, la_qp, la_k = rg(T), rg(T), rg(T)
        la_kp, la_tmp = rg(T), rg(T)
        la_pt = rg(NT, T)
        la_z, la_yo, la_e = rg(T), rg(T), rg(T)
        la_mx, la_sum = rg(NT), rg(NT)
        rot_mla, rot_da = const("rot_mla", at_const, ATT_CONST[0]), const("rot_da", at_const, ATT_CONST[0])
        cos_mla, sin_mla = const("cos_mla", at_const, ATT_CONST[0]), const("sin_mla", at_const, ATT_CONST[0])
        cos_da, sin_da = const("cos_da", at_const, ATT_CONST[0]), const("sin_da", at_const, ATT_CONST[0])

        rg = Region(ATT_CONST[1] - ATT_CONST[0])
        da_in = rg(2, T)
        da_v = rg(NT, G)
        da_sq, da_g, da_rs = rg(2, T), rg(2, T), rg(2, T)
        da_p_at = rg.at
        da_p = rg(4, T)
        da_qk = carve(da_p_at, 2, T)
        da_a = rg(NT, T)
        da_pt = rg(NT, T)
        da_o, da_osq, da_ors = da_rs[:, 0, :], da_sq[:, 0, :], da_sq[:, 1, :]
        da_z, da_yo, da_e = rg(T), rg(T), rg(T)
        da_mx, da_sum = rg(4), rg(4)
        x_junk = da_pt[:, 0, :]
        assert rg.at <= ARENA - NT * D, rg.at

        rg = Region()
        ml_const = rg(ML_CONST[1] - ML_CONST[0])
        ml_in = rg(2, T + 3)
        ml_acc = rg(2, T)
        ml_sil = rg(2, T)
        ml_v = rg(NT, G)
        ml_gate = rg(T)
        ml_gt, ml_sg = rg(T), rg(T)
        ml_ucol = rg(NT, 4)
        ml_m, ml_nf = rg(T), rg(T)
        ml_w = rg(NT, T)
        ml_s = rg(NT, T)
        ml_h, ml_den, ml_sq = rg(T), rg(T), rg(T)
        ml_o, ml_oe, ml_rs = rg(T), rg(T), rg(T)
        ml_z, ml_yo, ml_e = rg(T), rg(T), rg(T)
        causal = const("causal", ml_const, ML_CONST[0])
        sel_u, sel_f = const("sel_u", ml_const, ML_CONST[0]), const("sel_f", ml_const, ML_CONST[0])
        sel_u4 = const("sel_u4", ml_const, ML_CONST[0])
        carry = const("pass", ml_const, ML_CONST[0])

        s_first = sem("layer_first")
        s_lam_ready = sem("lam_ready")
        s_h_hi_ready = sem("h_hi_ready")
        s_par_ready = sem("par_ready")
        s_small_ready = sem("small_ready")
        s_x_squares = sem("x_squares")
        s_x_mean = sem("x_mean")
        s_x_scaled = sem("x_scaled")
        s_x_scaled_act = sem("x_scaled_act")
        s_x_turned = sem("x_turned")
        s_h_split = sem("h_split")
        s_hi_split = sem("hi_split")
        s_hi_by_act = sem("hi_by_act")
        s_y_hi_ready = sem("y_hi_ready")
        s_y_split = sem("y_split")
        s_y_loaded = [sem(f"y_loaded_{m}") for m in range(4)]
        s_raw_split = sem("raw_split")
        s_split_used = sem("split_used")
        s_proj_done = sem("proj_done")
        s_proj_copied = sem("proj_copied")
        s_out_done = sem("out_done")
        s_out_added = sem("out_added")
        s_out_kept = sem("out_kept")
        s_x_prefetched = sem("x_prefetched")
        s_z_loaded = sem("z_loaded")
        s_z_tanh = sem("z_tanh")
        s_y_ready = sem("y_ready")
        s_y_kept = sem("y_kept")
        s_rw_v_shifted = sem("rw_v_shifted")
        s_rw_first_loaded = sem("rw_first_loaded")
        s_rw_rk_loaded = sem("rw_rk_loaded")
        s_rw_shifted = sem("rw_shifted")
        s_rw_lora_tanh = sem("rw_lora_tanh")
        s_rw_vdn_mm = sem("rw_vdn_mm")
        s_rw_vd_ready = sem("rw_vd_ready")
        s_rw_lora_mm = sem("rw_lora_mm")
        s_rw_sig_tanh = sem("rw_sig_tanh")
        s_rw_decay = sem("rw_decay")
        s_rw_kk_sq = sem("rw_kk_sq")
        s_rw_decay_exp = sem("rw_decay_exp")
        s_rw_kk_sum = sem("rw_kk_sum")
        s_rw_kk_root = sem("rw_kk_root")
        s_rw_factors = sem("rw_factors")
        s_rw_turned = sem("rw_turned")
        s_rw_turned_copied = sem("rw_turned_copied")
        s_rw_bonus_ready = sem("rw_bonus_ready")
        s_rw_v_turned = sem("rw_v_turned")
        s_rw_v_copied = sem("rw_v_copied")
        s_rw_gram = sem("rw_gram")
        s_rw_gram_masked = sem("rw_gram_masked")
        s_rw_xt_first = sem("rw_xt_first")
        s_rw_x_first = sem("rw_x_first")
        s_rw_x_ready = sem("rw_x_ready")
        s_rw_levelled = sem("rw_levelled")
        s_rw_level_masked = sem("rw_level_masked")
        s_rw_level_mm = sem("rw_level_mm")
        s_rw_level_done = sem("rw_level_done")
        s_rw_pu_mm = sem("rw_pu_mm")
        s_rw_pu_ready = sem("rw_pu_ready")
        s_rw_local = sem("rw_local")
        s_rw_local_ready = sem("rw_local_ready")
        s_rw_h_copied = sem("rw_h_copied")
        s_rw_state_mm = sem("rw_state_mm")
        s_rw_state_ready = sem("rw_state_ready")
        s_rw_carried = sem("rw_carried")
        s_rw_y_whole = sem("rw_y_whole")
        s_rw_mean = sem("rw_mean")
        s_rw_centred = sem("rw_centred")
        s_rw_var = sem("rw_var")
        s_rw_rstd = sem("rw_rstd")
        s_scores_mm = sem("scores_mm")
        s_row_max = sem("row_max")
        s_probs_exp = sem("probs_exp")
        s_probs_ready = sem("probs_ready")
        s_probs_turned = sem("probs_turned")
        s_probs_t_copied = sem("probs_t_copied")
        s_pv_done = sem("pv_done")
        s_la_loaded = sem("la_loaded")
        s_la_squared = sem("la_squared")
        s_la_sums = sem("la_sums")
        s_la_rs_ready = sem("la_rs_ready")
        s_la_latents = sem("la_latents")
        s_la_v_mm = sem("la_v_mm")
        s_la_v_copied = sem("la_v_copied")
        s_la_heads_mm = sem("la_heads_mm")
        s_la_heads_copied = sem("la_heads_copied")
        s_la_heads_sums = sem("la_heads_sums")
        s_la_heads_rs = sem("la_heads_rs")
        s_la_qk_ready = sem("la_qk_ready")
        s_ml_cleared = sem("ml_cleared")
        s_ml_ucol_mm = sem("ml_ucol_mm")
        s_ml_ucol_ready = sem("ml_ucol_ready")
        s_ml_first_loaded = sem("ml_first_loaded")
        s_ml_qk_loaded = sem("ml_qk_loaded")
        s_ml_o_loaded = sem("ml_o_loaded")
        s_ml_conv = sem("ml_conv")
        s_ml_conv_tanh = sem("ml_conv_tanh")
        s_ml_qk_ready = sem("ml_qk_ready")
        s_ml_gate_abs = sem("ml_gate_abs")
        s_ml_gate_log = sem("ml_gate_log")
        s_ml_gates = sem("ml_gates")
        s_ml_u_mm = sem("ml_u_mm")
        s_ml_max = sem("ml_max")
        s_ml_w_exp = sem("ml_w_exp")
        s_ml_scores_mm = sem("ml_scores_mm")
        s_ml_s_ready = sem("ml_s_ready")
        s_ml_num_mm = sem("ml_num_mm")
        s_ml_h_sq = sem("ml_h_sq")
        s_ml_h_sum = sem("ml_h_sum")
        s_ml_h_rs = sem("ml_h_rs")
        s_ml_o_tanh = sem("ml_o_tanh")
        s_da_row_max = sem("da_row_max")
        s_da_scores_mm = sem("da_scores_mm")
        s_da_probs_exp = sem("da_probs_exp")
        s_da_loaded = sem("da_loaded")
        s_da_first_loaded = sem("da_first_loaded")
        s_da_squared = sem("da_squared")
        s_da_sums = sem("da_sums")
        s_da_rs_ready = sem("da_rs_ready")
        s_da_qk_ready = sem("da_qk_ready")
        s_da_half = sem("da_half")
        s_da_osq_ready = sem("da_osq_ready")
        s_da_osum_mm = sem("da_osum_mm")
        s_da_ors_ready = sem("da_ors_ready")
        s_da_lam_mm = sem("da_lam_mm")
        s_da_lam_exp = sem("da_lam_exp")
        s_stored = [sem(f"stored_{m}") for m in range(4)]
        s_raw_loaded = [sem(f"raw_loaded_{s}") for s in range(N_RAW)]
        s_act_order = sem("act_order")
        s_dve_order = sem("dve_order")
        s_last = sem("layer_last")
        of_layer = range(s_first.num, s_last.num + 1)

        def steps_of_weights():
            for g, pieces in enumerate(PIECES):
                for k in range(KT):
                    yield "w_in", k, pieces
            for part in (range(EARLY_K), range(EARLY_K, KT)):
                for n in range(4):
                    for k in part:
                        yield "w_out", k, [(n * G, G)]

        weight_steps = list(steps_of_weights())
        widths = [sum(width for _, width in pieces) for _, _, pieces in weight_steps]
        raw_count, raw_target = [0] * N_RAW, []
        for n, (_, _, pieces) in enumerate(weight_steps):
            raw_count[n % N_RAW] += 16 * len(pieces)
            raw_target.append(raw_count[n % N_RAW])


        with nc.Fori(0, DEPTH) as layer:
            with nc.Block() as block:
                @block.sync
                def _(sp):
                    for n, (source, k, pieces) in enumerate(weight_steps):
                        if n >= N_RAW:
                            sp.wait_ge(s_raw_split, n - N_RAW + 1)
                        at = 0
                        for c0, width in pieces:
                            sp.dma_start(raw[:, n % N_RAW, at:at + width],
                                         a[source][layer, k * P:(k + 1) * P, c0:c0 + width]
                                         ).then_inc(s_raw_loaded[n % N_RAW], 16)
                            at += width

                @block.gpsimd
                def _(pool):
                    for n in range(len(weight_steps)):
                        pool.wait_ge(s_raw_loaded[n % N_RAW], raw_target[n])
                        if n >= N_SPLIT:
                            pool.wait_ge(s_split_used, n - N_SPLIT + 1)
                        width = widths[n]
                        src = raw[:, n % N_RAW, 0:width]
                        hi, lo = w_hi[:, n % N_SPLIT, 0:width], w_lo[:, n % N_SPLIT, 0:width]
                        if HI_FIRST <= n < HI_LAST:
                            nc.gpsimd.tensor_scalar(hi, src, 1.0, None, ALU.mult).then_inc(s_hi_split, 1)
                            pool.wait_ge(s_hi_split, n - HI_FIRST + 1)
                        else:
                            pool.wait_ge(s_hi_by_act, n + 1 if n < HI_FIRST else n + 1 - (HI_LAST - HI_FIRST))
                        nc.gpsimd.tensor_tensor(lo, src, hi.bitcast(F32), ALU.subtract).then_inc(s_raw_split, 1)

                @block.tensor
                def _(pe):
                    mm, turn = nc.tensor.matmul, nc.tensor.transpose
                    progress = Progress()

                    def project(steps):
                        for n in steps:
                            g, k = divmod(n, KT)
                            pe.wait_ge(s_raw_split, n + 1)
                            if g == 0:
                                pe.wait_ge(s_h_split, k + 1)
                            for m in range(tiles_of(g)):
                                if k == 0 and g:
                                    in_bank = g - 1 if m < tiles_of(g - 1) else g - 2
                                    pe.wait_ge(s_proj_copied, tiles_before(in_bank) + m + 1)
                                w1, w2 = w_hi[:, n % N_SPLIT, :], w_lo[:, n % N_SPLIT, :]
                                part = slice(m * P, (m + 1) * P)
                                h1, h2 = h_hi[:, k, :], h_lo[:, k, :]
                                if g in TOKEN_MAJOR:
                                    products = ((h1[:, part], w1), (h1[:, part], w2), (h2[:, part], w1))
                                else:
                                    products = ((w1[:, part], h1), (w1[:, part], h2), (w2[:, part], h1))
                                for j, (lhsT, rhs) in enumerate(products):
                                    last = mm(ps_proj[:, m, :], lhsT, rhs, start=(k == 0 and j == 0),
                                              stop=(k == KT - 1 and j == 2))
                                if k == KT - 1 and m < tiles_of(g) - 1:
                                    last.then_inc(s_proj_done, 1)
                            last.then_inc(s_split_used, 1)

                    def fill(n=1):
                        project(progress.ahead(n))

                    pe.wait_ge(s_setup, 32)
                    pe.wait_ge(s_lam_ready, 1)
                    mm(ps_proj[:, 1, 0:2], ones[0:64, :], lam_prod[0:64, :], start=True, stop=True
                       ).then_inc(s_da_lam_mm, 1)

                    for i in range(NT):
                        if i < 2:
                            pe.wait_ge(s_x_scaled_act, i + 1)
                        else:
                            pe.wait_ge(s_x_scaled, i - 1)
                        for k in range(4):
                            last = turn(ps[:, k, i * P:(i + 1) * P], x_tok[:, i, k * P:(k + 1) * P], ident)
                            if i == NT - 1:
                                last.then_inc(s_x_turned, 1)
                    pe.wait_ge(s_da_lam_exp, 1)
                    for k in range(4, KT):
                        pe.wait_ge(s_h_split, k - 3)
                        for i in range(NT):
                            last = turn(ps[:, k % 4, i * P:(i + 1) * P], x_tok[:, i, k * P:(k + 1) * P], ident)
                        last.then_inc(s_x_turned, 1)
                        project(progress.ahead(1))
                    project(progress.through(G_MISC))
                    fill(FILL["rw_first"])

                    pe.wait_ge(s_h_split, KT)
                    pe.wait_ge(s_rw_first_loaded, 16 * 8)
                    pe.wait_ge(s_rw_v_shifted, 1)
                    for j in range(4):
                        last = mm(ps[0:32, 0, :], rw_vdn[:, j, :], rw_v[:, j, 1:T + 1], start=(j == 0), stop=(j == 3))
                    last.then_inc(s_rw_vdn_mm, 1)
                    pe.wait_ge(s_rw_vd_ready, 1)
                    pe.wait_ge(s_rw_lora_tanh, 1)
                    for hp in range(4):
                        if hp:
                            pe.wait_ge(s_y_ready, hp)
                        cols = slice(hp * P, (hp + 1) * P)
                        mm(ps[:, 0, :], rw_wup[0:32, cols], rw_lora[0:32, 1:T + 1], start=True, stop=True)
                        mm(ps[:, 1, :], rw_wup[32:64, cols], rw_lora[32:64, 1:T + 1], start=True, stop=True)
                        mm(ps[:, 2, :], rw_vup[0:32, cols], rw_vd[0:32, :], start=True, stop=True
                           ).then_inc(s_rw_lora_mm, 1)
                        fill(FILL["rw_lora"][hp])
                        pe.wait_ge(s_rw_kk_sq, hp + 1)
                        mm(ps[:, 3, :], bones, rw_sq, start=True, stop=True).then_inc(s_rw_kk_sum, 1)
                        fill(FILL["rw_factors"][hp])
                        pe.wait_ge(s_rw_factors, hp + 1)
                        for i in range(NT):
                            turn(ps[:, 0, i * P:(i + 1) * P], rw_ar[:, i, 0, :], ident)
                            turn(ps[:, 1, i * P:(i + 1) * P], rw_bn[:, i * P:(i + 1) * P], ident)
                            turn(ps[:, 2, i * P:(i + 1) * P], rw_kt[:, i * P:(i + 1) * P], ident)
                        mm(ps[:, 3, :], bones, rw_sq, start=True, stop=True).then_inc(s_rw_turned, 1)
                        fill(FILL["rw_turned"][hp])
                        pe.wait_ge(s_rw_turned_copied, 3 * hp + 3)
                        for i in range(NT):
                            last = turn(ps[:, 0, i * P:(i + 1) * P], rw_v[:, hp, 1 + i * P:1 + (i + 1) * P], ident)
                        last.then_inc(s_rw_v_turned, 1)
                        fill(FILL["rw_v"][hp])
                        pe.wait_ge(s_rw_v_copied, hp + 1)
                        pe.wait_ge(s_rw_bonus_ready, hp + 1)
                        for ip in range(2):
                            if ip:
                                pe.wait_ge(s_rw_gram_masked, 2 * hp + 1)
                            for i in (2 * ip, 2 * ip + 1):
                                for f, factor in enumerate((rw_beta, rw_kappa)):
                                    for h in range(2):
                                        half = slice(64 * h, 64 * h + 64)
                                        last = mm(ps[:, 2 * f + h, (i % 2) * 256:(i % 2) * 256 + 256],
                                                  factor[half, i * P:(i + 1) * P], rw_ar[half, i, :, :],
                                                  start=True, stop=True)
                            last.then_inc(s_rw_gram, 1)
                            fill(FILL["rw_gram"][hp])
                        fill(FILL["rw_xt"][hp])
                        pe.wait_ge(s_rw_xt_first, hp + 1)
                        for h in range(2):
                            for i in range(NT):
                                turn(ps[:, h, i * P:(i + 1) * P], rw_xt[:, 4 * h + i, :], ident)
                        for h in range(2):
                            for i in range(NT):
                                last = mm(ps[:, 2 + h, i * 64:(i + 1) * 64], rw_gk[:, 4 * h + i, 0:P],
                                          rw_vT[:, i, 64 * h:64 * h + 64], start=True, stop=True)
                        last.then_inc(s_rw_x_first, 1)
                        fill(FILL["rw_x"][hp])
                        pe.wait_ge(s_rw_x_ready, 4 * hp + 4)
                        for lv in range(len(LEVELS)):
                            for h in range(2):
                                if lv:
                                    pe.wait_ge(s_rw_level_done, 10 * hp + 2 * (lv - 1) + h + 1)
                                for i in range(NT):
                                    j = 4 * h + i
                                    last = mm(ps[:, 2 * h, i * P:(i + 1) * P], rw_gb[:, j, 0:P], rw_x[:, j, :],
                                              start=True, stop=True)
                                last.then_inc(s_rw_levelled, 1)
                                if h:
                                    fill(FILL["rw_level"][hp])
                            for h in range(2):
                                pe.wait_ge(s_rw_level_masked, 10 * hp + 2 * lv + h + 1)
                                for i in range(NT):
                                    j = 4 * h + i
                                    if lv < len(LEVELS) - 1:
                                        mm(ps[:, 2 * h, i * P:(i + 1) * P], rw_xt[:, j, :], rw_y[:, j, :],
                                           start=True, stop=True)
                                    last = mm(ps[:, 2 * h + 1, i * P:(i + 1) * P], rw_y[:, j, :], rw_xt[:, j, :],
                                              start=True, stop=True)
                                last.then_inc(s_rw_level_mm, 1)
                        fill(FILL["rw_levels"][hp])
                        for h in range(2):
                            pe.wait_ge(s_rw_level_done, 10 * hp + 8 + h + 1)
                            for i in range(NT):
                                j = 4 * h + i
                                last = mm(ps[:, h, i * P:(i + 1) * P], rw_xt[:, j, :], rw_abv[:, i, h, :],
                                          start=True, stop=True)
                            last.then_inc(s_rw_pu_mm, 1)
                        fill(FILL["rw_pu"][hp])
                        pe.wait_ge(s_rw_pu_ready, 2 * hp + 2)
                        for h in range(2):
                            half = slice(64 * h, 64 * h + 64)
                            for i in range(NT):
                                j = 4 * h + i
                                pt = slice(i * P, (i + 1) * P)
                                mm(ps[half, 2, pt], rw_pu[:, j, 0:64], rw_gb[:, j, P:2 * P], start=True, stop=True)
                                mm(ps[half, 3, pt], rw_vT[:, i, half], rw_gk[:, j, P:2 * P], start=True, stop=False)
                                last = mm(ps[half, 3, pt], rw_pu[:, j, 64:P], rw_gb[:, j, P:2 * P],
                                          start=False, stop=True)
                        for c in range(NCH):
                            i, q = c // 2, slice(64 * (c % 2), 64 * (c % 2) + 64)
                            for h in range(2):
                                half, j = slice(64 * h, 64 * h + 64), 4 * h + i
                                mm(ps[half, c % 2, i * P:i * P + 64], rw_pu[q, j, 0:64], rw_bnT[q, i, half],
                                   start=True, stop=True)
                                mm(ps[half, c % 2, i * P + 64:(i + 1) * P], rw_ktT[q, i, half], rw_vT[q, i, half],
                                   start=True, stop=False)
                                last = mm(ps[half, c % 2, i * P + 64:(i + 1) * P], rw_bnT[q, i, half],
                                          rw_pu[q, j, 64:P], start=False, stop=True)
                        last.then_inc(s_rw_local, 1)
                        fill(FILL["rw_local"][hp])
                        pe.wait_ge(s_rw_local_ready, hp + 1)
                        for c in range(1, NCH - 1):
                            if c > 1:
                                pe.wait_ge(s_rw_state_ready, (NCH - 2) * hp + c - 1)
                            for h in range(2):
                                half = slice(64 * h, 64 * h + 64)
                                last = mm(ps[half, h, c * 64:(c + 1) * 64], rw_gt[half, c, :], rw_st[half, c, :],
                                          start=True, stop=True)
                            last.then_inc(s_rw_state_mm, 1)
                            if c % 2:
                                fill(FILL["rw_state"][hp])
                        pe.wait_ge(s_rw_state_ready, (NCH - 2) * (hp + 1))
                        for c in range(NCH):
                            for h in range(2):
                                half = slice(64 * h, 64 * h + 64)
                                last = mm(ps[half, 2 + h, c * 64:(c + 1) * 64], rw_st[half, c, :],
                                          rw_ar[half, c // 2, 1, 64 * (c % 2):64 * (c % 2) + 64],
                                          start=True, stop=True)
                        last.then_inc(s_rw_carried, 1)
                        fill(FILL["rw_carried"][hp])
                        pe.wait_ge(s_rw_y_whole, hp + 1)
                        mm(ps[:, 0, :], bones, rw_yl, start=True, stop=True).then_inc(s_rw_mean, 1)
                        fill(FILL["rw_mean"][hp])
                        pe.wait_ge(s_rw_centred, hp + 1)
                        mm(ps[:, 1, :], bones, rw_sq, start=True, stop=True).then_inc(s_rw_var, 1)
                        if hp == 0:
                            project(progress.through(G_Z_RW))
                        fill(FILL["rw_gate"][hp])

                    project(progress.through(G_LAT))
                    fill(FILL["la_first"])
                    pe.wait_ge(s_y_ready, 4)
                    pe.wait_ge(s_la_squared, 1)
                    for j in range(3):
                        mm(ps[:, 0, :], ones, la_sq[:, j, :], start=(j == 0), stop=(j == 2))
                    for j in range(2):
                        mm(ps[:, 1, :], ones, la_sq[:, 3 + j, :], start=(j == 0), stop=(j == 1))
                    mm(ps[0:64, 2, :], rot_mla[0:64, :], la_peg[0:64, :], start=True, stop=True
                       ).then_inc(s_la_sums, 1)
                    fill(FILL["la_sums"])
                    pe.wait_ge(s_la_latents, 1)
                    for i in range(NT):
                        for j in range(2):
                            last = mm(ps[:, i, :], la_in[:, 3 + j, i * P:(i + 1) * P],
                                      la_wkv[:, j, :].rearrange("p (h c) -> p h c", h=HEADS)[:, :, P:2 * P],
                                      start=(j == 0), stop=(j == 1))
                        last.then_inc(s_la_v_mm, 1)
                    fill(FILL["la_v"])
                    pe.wait_ge(s_la_v_copied, NT)

                    def turn_probs(n, probs, pt, v, h, fill, steps):
                        for j in range(NT):
                            for i in range(j, NT):
                                last = turn(ps[:, j, i * P:(i + 1) * P], probs[:, i, j * P:(j + 1) * P], ident)
                        last.then_inc(s_probs_turned, 1)
                        fill(steps)
                        pe.wait_ge(s_probs_t_copied, NT * (n + 1))
                        for j in range(NT):
                            last = mm(ps[:, 0, j * P:T], v[:, j, h * P:(h + 1) * P], pt[:, j, j * P:T],
                                      start=(j == 0), stop=(j == NT - 1))
                        last.then_inc(s_pv_done, 1)

                    for h in range(HEADS):
                        if h:
                            pe.wait_ge(s_y_ready, 4 + h)
                        q0 = h * 192
                        for j in range(3):
                            mm(ps[:, 0, :], la_wq[:, j, q0:q0 + P], la_in[:, j, :], start=(j == 0), stop=(j == 2))
                        for j in range(3):
                            mm(ps[0:64, 1, :], la_wq[:, j, q0 + P:q0 + 192], la_in[:, j, :],
                               start=(j == 0), stop=(j == 2))
                        for j in range(2):
                            last = mm(ps[:, 2, :], la_wkv[:, j, h * 256:h * 256 + P], la_in[:, 3 + j, :],
                                      start=(j == 0), stop=(j == 1))
                        last.then_inc(s_la_heads_mm, 1)
                        fill(FILL["la_heads"][h])
                        pe.wait_ge(s_la_heads_copied, h + 1)
                        mm(ps[:, 3, :], ones, la_hsq[:, 0, :], start=True, stop=False)
                        mm(ps[:, 3, :], ones[0:64, :], la_hsq[0:64, 1, :], start=False, stop=True)
                        mm(ps[:, 0, :], ones, la_hsq[:, 2, :], start=True, stop=False)
                        mm(ps[:, 0, :], ones[0:64, :], la_pesq[0:64, :], start=False, stop=True)
                        mm(ps[0:64, 1, :], rot_mla[0:64, :], la_qp[0:64, :], start=True, stop=True
                           ).then_inc(s_la_heads_sums, 1)
                        fill(FILL["la_qk"][h])
                        pe.wait_ge(s_la_qk_ready, h + 1)
                        for i in range(NT):
                            qs, ks = slice(i * P, (i + 1) * P), slice(0, (i + 1) * P)
                            mm(ps[:, i, ks], la_q[:, qs], la_k[:, ks], start=True, stop=False)
                            mm(ps[:, i, ks], la_qp[0:64, qs], la_kp[0:64, ks], start=False, stop=False)
                            mm(ps[:, i, qs], mask_ident, neg, start=False, stop=True).then_inc(s_scores_mm, 1)
                        fill(FILL["la_probs"][h])
                        pe.wait_ge(s_probs_ready, h + 1)
                        turn_probs(h, la_p, la_pt, la_v, h, fill, FILL["la_turned"][h])
                        if h == 0:
                            project(progress.through(G_Z_LA))
                        fill(FILL["la_gate"][h])

                    project(progress.through(G_MLO))
                    fill(FILL["ml_first"])
                    pe.wait_ge(s_y_ready, 8)
                    pe.wait_ge(s_ml_gates, 1)
                    for i in range(NT):
                        last = mm(ps[:, 3, 4 * i:4 * i + 4], ml_gt[0:36, i * P:(i + 1) * P], sel_u4[0:36, :],
                                  start=True, stop=True)
                    last.then_inc(s_ml_ucol_mm, 1)
                    pe.wait_ge(s_ml_ucol_ready, 1)
                    for h in range(HEADS):
                        if h:
                            pe.wait_ge(s_y_ready, 8 + h)
                        mm(ps[:, 0, :], sel_u[0:36, h * P:(h + 1) * P], ml_gt[0:36, :], start=True, stop=True)
                        mm(ps[:, 1, :], sel_f[0:36, h * P:(h + 1) * P], ml_gt[0:36, :], start=True, stop=True
                           ).then_inc(s_ml_u_mm, 1)
                        fill(FILL["ml_qk"][h])
                        pe.wait_ge(s_ml_max, h + 1)
                        pe.wait_ge(s_ml_qk_ready, h + 1)
                        for i in range(NT):
                            last = mm(ps[:, i, i * P:T], ml_acc[:, 1, i * P:(i + 1) * P], ml_acc[:, 0, i * P:T],
                                      start=True, stop=True)
                        last.then_inc(s_ml_scores_mm, 1)
                        fill(FILL["ml_s"][h])
                        pe.wait_ge(s_ml_s_ready, h + 1)
                        for i in range(NT):
                            mm(ps[:, 0, i * P:T], ml_v[:, i, h * P:(h + 1) * P], ml_s[:, i, i * P:T],
                               start=(i == 0), stop=(i == NT - 1))
                        for i in range(NT):
                            last = mm(ps[:, 1, i * P:T], ones, ml_s[:, i, i * P:T],
                                      start=(i == 0), stop=(i == NT - 1))
                        last.then_inc(s_ml_num_mm, 1)
                        if h == 0:
                            project(progress.through(G_Z_ML))
                        fill(FILL["ml_h"][h])
                        pe.wait_ge(s_ml_h_sq, h + 1)
                        mm(ps[:, 2, :], ones, ml_sq, start=True, stop=True).then_inc(s_ml_h_sum, 1)
                        fill(FILL["ml_gate"][h])

                    project(progress.through(G_DAV))
                    pe.wait_ge(s_y_ready, 12)
                    early = Progress(STEPS, STEPS + EARLY)

                    def out_product(n, k, bank, first, last_k):
                        pe.wait_ge(s_raw_split, n + 1)
                        w1, w2 = w_hi[:, n % N_SPLIT, :], w_lo[:, n % N_SPLIT, :]
                        for i in range(NT):
                            if first:
                                yield i
                            y1, y2 = h_hi[:, k, i * P:(i + 1) * P], h_lo[:, k, i * P:(i + 1) * P]
                            for j, (lhsT, rhs) in enumerate(((y1, w1), (y1, w2), (y2, w1))):
                                last = mm(bank[:, i, :], lhsT, rhs, start=(first and j == 0),
                                          stop=(last_k and j == 2))
                            if last_k and i < 3:
                                last.then_inc(s_out_done, 1)
                        last.then_inc(s_split_used, 1)

                    def fill_out(n=1):
                        for s in early.ahead(n):
                            c, k = divmod(s - STEPS, EARLY_K)
                            if c == 0:
                                pe.wait_ge(s_y_split, y_count(k))
                            for i in out_product(s, k, ps_proj, k == 0, k == EARLY_K - 1):
                                if c:
                                    pe.wait_ge(s_out_added, 4 * (c - 1) + i + 1)
                                else:
                                    pe.wait_ge(s_proj_copied, tiles_before(NG))

                    fill(FILL["da_first"])
                    for h in range(HEADS):
                        between = fill_out if h else fill
                        if h:
                            pe.wait_ge(s_y_ready, 12 + h)
                        if h == 0:
                            pe.wait_ge(s_da_first_loaded, 32)
                        pe.wait_ge(s_da_squared, h + 1)
                        mm(ps[:, 0, :], bones, da_sq[:, 0, :], start=True, stop=True)
                        mm(ps[:, 1, :], bones, da_sq[:, 1, :], start=True, stop=True)
                        mm(ps[:, 2, :], rot_da, da_g[:, 0, :], start=True, stop=True)
                        mm(ps[:, 3, :], rot_da, da_g[:, 1, :], start=True, stop=True).then_inc(s_da_sums, 1)
                        between(FILL["da_sums"][h])
                        pe.wait_ge(s_da_qk_ready, h + 1)
                        for f in range(2):
                            if f:
                                between(FILL["da_scores"][h])
                                pe.wait_ge(s_da_probs_exp, 8 * h + 4)
                            for i in (2 * f, 2 * f + 1):
                                qs, ks = slice(i * P, (i + 1) * P), slice(0, (i + 1) * P)
                                for m in range(2):
                                    half, b = slice(64 * m, 64 * m + 64), 2 * (i % 2) + m
                                    mm(ps[:, b, ks], da_g[half, 0, qs], da_g[half, 1, ks], start=True, stop=False)
                                    last = mm(ps[:, b, qs], mask_ident, neg, start=False, stop=True)
                            last.then_inc(s_da_scores_mm, 1)
                        between(FILL["da_half"][h])
                        pe.wait_ge(s_da_half, 2 * h + 2)
                        turn_probs(HEADS + h, da_a, da_pt, da_v, h, between, FILL["da_turned"][h])
                        between(FILL["da_osq"][h])
                        pe.wait_ge(s_da_osq_ready, h + 1)
                        mm(ps[:, 1, :], ones, da_osq, start=True, stop=True).then_inc(s_da_osum_mm, 1)
                        if h == 0:
                            project(progress.rest())
                        else:
                            fill_out(FILL["da_gate"][h] if h < HEADS - 1 else EARLY)

                    pe.wait_ge(s_y_ready, 16)
                    for c in range(4):
                        bank = (ps, ps_proj)[c % 2]
                        for k in range(EARLY_K, KT):
                            s = STEPS + EARLY + c * LATE_K + k - EARLY_K
                            if c == 0:
                                pe.wait_ge(s_y_split, y_count(k))
                            for i in out_product(s, k, bank, k == EARLY_K, k == KT - 1):
                                if c:
                                    pe.wait_ge(s_out_added, (13 if c == 1 else 4 * c + 9) + i)

                @block.scalar
                def _(act):
                    progress, counts = Progress(), [0]

                    def link(ins):
                        counts[0] += 1
                        ins.then_inc(s_act_order, 1)
                        act.wait_ge(s_act_order, counts[0])

                    def evacuate(steps):
                        for g in groups_ended(steps):
                            for m in range(tiles_of(g)):
                                if m < tiles_of(g) - 1:
                                    act.wait_ge(s_proj_done, tiles_before(g) - g + m + 1)
                                else:
                                    act.wait_ge(s_split_used, KT * (g + 1))
                                if g:
                                    act.wait_ge(s_stored[m], 16 * (g - (m == 3 and g > G_MISC)))
                                nc.scalar.activation(stage[:, m, :], ps_proj[:, m, :], ACT.Copy).then_inc(s_proj_copied, 1)
                                act.wait_ge(s_proj_copied, tiles_before(g) + m + 1)
                                act.dma_start(p_dram[4 * g + m], stage[:, m, :]).then_inc(s_stored[m], 16)

                    def high_part(n):
                        act.wait_ge(s_raw_loaded[n % N_RAW], raw_target[n])
                        if n >= N_SPLIT:
                            act.wait_ge(s_split_used, n - N_SPLIT + 1)
                        nc.scalar.activation(w_hi[:, n % N_SPLIT, 0:widths[n]], raw[:, n % N_RAW, 0:widths[n]], ACT.Copy
                                             ).then_inc(s_hi_by_act, 1)

                    def fill(n=1):
                        evacuate(progress.ahead(n))

                    def wait_stored(g):
                        for m in range(4):
                            act.wait_ge(s_stored[m], 16 * (g + 1 - (m == 3 and g >= G_MISC)))

                    def load_z(tile, z):
                        act.dma_start(z, p_dram[z_tile(tile)]).then_inc(s_z_loaded, 16)

                    def tanh_z(n, z, e):
                        act.wait_ge(s_z_loaded, 16 * (n + 1))
                        nc.scalar.activation(e, z, ACT.Tanh, scale=0.5).then_inc(s_z_tanh, 1)

                    def keep_y(n, tile, yo, z):
                        act.wait_ge(s_y_ready, n + 1)
                        if n % 4 < 3:
                            load_z(tile + 1, z)
                        act.dma_start(y_dram[tile], yo).then_inc(s_y_kept, 16)

                    def rstd(dst, src, n, eps):
                        link(nc.scalar.activation(dst, src, ACT.Ln, scale=1.0 / n, bias=eps))
                        return nc.scalar.activation(dst, dst, ACT.Exp, scale=-0.5)

                    act.wait_ge(s_x_squares, 1)
                    rstd(rs_x, ms, D, EPS).then_inc(s_x_mean, 1)
                    act.wait_ge(s_x_mean, 1)
                    for i in range(2):
                        nc.scalar.activation(x_tok[:, i, :], x_tok[:, i, :], ACT.Copy, scale=rs_x[:, i:i + 1]
                                             ).then_inc(s_x_scaled_act, 1)
                    act.wait_ge(s_da_lam_mm, 1)
                    nc.scalar.activation(lam2, ps_proj[:, 1, 0:2], ACT.Exp).then_inc(s_da_lam_exp, 1)
                    act.wait_ge(s_par_ready, 1)
                    for k in range(KT):
                        act.wait_ge(s_x_turned, k + 1)
                        nc.scalar.activation(h_hi[:, k, :], ps[:, k % 4, :], ACT.Copy, scale=col("norm_g", k)).then_inc(s_h_hi_ready, 1)
                        for n in (range(4) if k == 3 else (k,) if k > 3 else ()):
                            high_part(n)

                    act.dma_start(rw_const, a["const"][:, RW_CONST[0]:RW_CONST[1]]).then_inc(s_rw_first_loaded, 16)
                    act.dma_start(rw_wup[0:32, :], a["rw_w_up"][layer]).then_inc(s_rw_first_loaded, 16)
                    act.dma_start(rw_wup[32:64, :], a["rw_a_up"][layer]).then_inc(s_rw_first_loaded, 16)
                    act.dma_start(rw_vup[0:32, :], a["rw_v_up"][0]).then_inc(s_rw_first_loaded, 16)
                    act.dma_start(rw_vdn, a["rw_v_dn"][0].rearrange("(k p) r -> p k r", p=P)).then_inc(s_rw_first_loaded, 16)
                    for n in range(HI_FIRST + 3):
                        if KT <= n < HI_FIRST:
                            high_part(n)
                        if n > KT and n % KT == 2:
                            evacuate(progress.ahead(KT))
                    evacuate(progress.ahead(FILL["rw_first"]))
                    wait_stored(G_MISC)
                    act.dma_start(rw_lora[0:64, 1:T + 1], p_dram[KPE_LORA, 64:P]).then_inc(s_rw_first_loaded, 16)
                    act.dma_start(rw_v[:, 0:2, 1:T + 1], p_dram[4 * G_V:4 * G_V + 2].rearrange("j p t -> p j t")).then_inc(s_rw_first_loaded, 16)
                    act.dma_start(rw_v[:, 2:4, 1:T + 1], p_dram[4 * G_V + 2:4 * G_V + 4].rearrange("j p t -> p j t")).then_inc(s_rw_first_loaded, 16)
                    act.dma_start(rw_in[:, 0, 1:T + 1], p_dram[4 * G_R]).then_inc(s_rw_rk_loaded, 16)
                    act.dma_start(rw_in[:, 1, 1:T + 1], p_dram[4 * G_K]).then_inc(s_rw_rk_loaded, 16)
                    act.wait_ge(s_rw_shifted, 1)
                    nc.scalar.activation(rw_lora[0:32, 1:T + 1], rw_lora[0:32, 1:T + 1], ACT.Tanh).then_inc(s_rw_lora_tanh, 1)
                    for hp in range(4):
                        act.wait_ge(s_rw_lora_mm, hp + 1)
                        link(nc.scalar.activation(rw_t[:, 0, :], ps[:, 0, :], ACT.Tanh, scale=0.5, bias=half_w0[:, hp:hp + 1]))
                        link(nc.scalar.activation(rw_t[:, 1, :], ps[:, 1, :], ACT.Tanh, scale=0.5, bias=half_a0[:, hp:hp + 1]))
                        nc.scalar.activation(rw_t[:, 2, :], ps[:, 2, :], ACT.Tanh, scale=0.5, bias=half_v0[:, hp:hp + 1]).then_inc(s_rw_sig_tanh, 1)
                        fill(FILL["rw_lora"][hp])
                        act.wait_ge(s_rw_decay, hp + 1)
                        link(nc.scalar.activation(rw_w, rw_c, ACT.Exp))
                        link(nc.scalar.activation(rw_wm, rw_cm, ACT.Exp))
                        nc.scalar.activation(rw_wi, rw_c, ACT.Exp, scale=-1.0).then_inc(s_rw_decay_exp, 1)
                        act.wait_ge(s_rw_kk_sum, hp + 1)
                        nc.scalar.activation(rw_nr, ps[:, 3, :], ACT.Sqrt).then_inc(s_rw_kk_root, 1)
                        fill(FILL["rw_factors"][hp])
                        act.wait_ge(s_rw_turned, hp + 1)
                        if hp < 3:
                            act.dma_start(rw_in[:, 0, 1:T + 1], p_dram[4 * G_R + hp + 1]).then_inc(s_rw_rk_loaded, 16)
                            act.dma_start(rw_in[:, 1, 1:T + 1], p_dram[4 * G_K + hp + 1]).then_inc(s_rw_rk_loaded, 16)
                        nc.scalar.activation(rw_abv[:, :, :, 0:64], ps[:, 0, :].rearrange("p (i h k) -> p i h k", i=NT, h=2), ACT.Copy).then_inc(s_rw_turned_copied, 1)
                        nc.scalar.activation(rw_bnT, ps[:, 1, :].rearrange("p (i c) -> p i c", i=NT), ACT.Copy).then_inc(s_rw_turned_copied, 1)
                        nc.scalar.activation(rw_ktT, ps[:, 2, :].rearrange("p (i c) -> p i c", i=NT), ACT.Copy).then_inc(s_rw_turned_copied, 1)
                        fill(FILL["rw_turned"][hp])
                        act.wait_ge(s_rw_v_turned, hp + 1)
                        nc.scalar.activation(rw_vT, ps[:, 0, :].rearrange("p (i c) -> p i c", i=NT), ACT.Copy).then_inc(s_rw_v_copied, 1)
                        fill(FILL["rw_v"][hp])
                        for ip in range(2):
                            fill(FILL["rw_gram"][hp])
                        fill(FILL["rw_xt"][hp])
                        act.wait_ge(s_rw_x_first, hp + 1)
                        for h in range(2):
                            nc.scalar.activation(rw_x[:, 4 * h:4 * h + 4, :], ps[:, h, :].rearrange("p (i c) -> p i c", i=NT), ACT.Copy).then_inc(s_rw_x_ready, 1)
                        for h in range(2):
                            nc.scalar.activation(rw_abv[:, :, h, 64:P], ps[:, 2 + h, 0:256].rearrange("p (i c) -> p i c", i=NT), ACT.Copy).then_inc(s_rw_x_ready, 1)
                        fill(FILL["rw_x"][hp])
                        for lv in range(len(LEVELS)):
                            fill(FILL["rw_level"][hp])
                        fill(FILL["rw_levels"][hp])
                        for h in range(2):
                            act.wait_ge(s_rw_pu_mm, 2 * hp + h + 1)
                            nc.scalar.activation(rw_pu[:, 4 * h:4 * h + 4, :], ps[:, h, :].rearrange("p (i c) -> p i c", i=NT), ACT.Copy).then_inc(s_rw_pu_ready, 1)
                        fill(FILL["rw_pu"][hp])
                        act.wait_ge(s_rw_local, hp + 1)
                        for q in range(2):
                            nc.scalar.activation(rw_st[:, 1 + q:NCH + 1:2, :], ps[:, q, :].rearrange("p (i s c) -> p i s c", i=NT, s=2)[:, :, 1, :], ACT.Copy).then_inc(s_rw_h_copied, 1)
                        fill(FILL["rw_local"][hp])
                        for c in range(1, NCH - 1):
                            if c % 2:
                                fill(FILL["rw_state"][hp])
                        fill(FILL["rw_carried"][hp])
                        fill(FILL["rw_mean"][hp])
                        act.wait_ge(s_rw_var, hp + 1)
                        rstd(rw_nr, ps[:, 1, :], 64, GN_EPS).then_inc(s_rw_rstd, 1)
                        if hp == 0:
                            evacuate(progress.through(G_Z_RW))
                            wait_stored(G_Z_RW)
                            load_z(0, rw_z)
                        fill(FILL["rw_gate"][hp])
                        tanh_z(hp, rw_z, rw_e)
                        keep_y(hp, hp, rw_yo, rw_z)

                    act.wait_ge(s_y_kept, 16 * 4)
                    evacuate(progress.through(G_LAT))
                    wait_stored(G_LAT)
                    act.dma_start(at_const, a["const"][:, ATT_CONST[0]:ATT_CONST[1]]).then_inc(s_la_loaded, 16)
                    act.dma_start(la_in[:, 0:4, :], p_dram[4 * G_LAT:4 * G_LAT + 4].rearrange("j p t -> p j t")).then_inc(s_la_loaded, 16)
                    act.dma_start(la_in[:, 4, :], p_dram[KV1]).then_inc(s_la_loaded, 16)
                    act.dma_start(la_pe[0:64, :], p_dram[KPE_LORA, 0:64]).then_inc(s_la_loaded, 16)
                    act.dma_start(la_wq, a["mla_w_q_b"][layer].rearrange("(k p) n -> p k n", p=P)).then_inc(s_la_loaded, 16)
                    act.dma_start(la_wkv, a["mla_w_kv_b"][layer].rearrange("(k p) n -> p k n", p=P)).then_inc(s_la_loaded, 16)
                    fill(FILL["la_first"])
                    act.wait_ge(s_la_sums, 1)
                    link(nc.scalar.activation(la_rs[:, 0, :], ps[:, 0, :], ACT.Ln, scale=1.0 / 384, bias=EPS))
                    link(nc.scalar.activation(la_rs[:, 1, :], ps[:, 1, :], ACT.Ln, scale=1.0 / 256, bias=EPS))
                    nc.scalar.activation(la_rs, la_rs, ACT.Exp, scale=-0.5).then_inc(s_la_rs_ready, 1)
                    fill(FILL["la_sums"])
                    for i in range(NT):
                        act.wait_ge(s_la_v_mm, i + 1)
                        nc.scalar.activation(la_v[:, i, :], ps[:, i, :], ACT.Copy).then_inc(s_la_v_copied, 1)
                    fill(FILL["la_v"])

                    def copy_turned(n, pt, steps):
                        act.wait_ge(s_probs_turned, n + 1)
                        for j in range(NT):
                            nc.scalar.activation(pt[:, j, j * P:T], ps[:, j, j * P:T], ACT.Copy).then_inc(s_probs_t_copied, 1)
                        fill(steps)

                    for h in range(HEADS):
                        act.wait_ge(s_la_heads_mm, h + 1)
                        link(nc.scalar.activation(la_hsq[:, 0, :], ps[:, 0, :], ACT.Square))
                        link(nc.scalar.activation(la_hsq[0:64, 1, :], ps[0:64, 1, :], ACT.Square))
                        link(nc.scalar.activation(la_hsq[:, 2, :], ps[:, 2, :], ACT.Square))
                        link(nc.scalar.activation(la_q, ps[:, 0, :], ACT.Copy, scale=col("mla_q_g")))
                        link(nc.scalar.activation(la_qp[0:64, :], ps[0:64, 1, :], ACT.Copy, scale=col("mla_q_g", 1)[0:64, :]))
                        nc.scalar.activation(la_k, ps[:, 2, :], ACT.Copy, scale=col("mla_k_g")).then_inc(s_la_heads_copied, 1)
                        fill(FILL["la_heads"][h])
                        act.wait_ge(s_la_heads_sums, h + 1)
                        link(nc.scalar.activation(la_rs[:, 0, :], ps[:, 3, :], ACT.Ln, scale=1.0 / 192, bias=EPS))
                        link(nc.scalar.activation(la_rs[:, 1, :], ps[:, 0, :], ACT.Ln, scale=1.0 / 192, bias=EPS))
                        nc.scalar.activation(la_rs, la_rs, ACT.Exp, scale=-0.5).then_inc(s_la_heads_rs, 1)
                        fill(FILL["la_qk"][h])
                        act.wait_ge(s_row_max, h + 1)
                        for i in range(NT):
                            nc.scalar.activation(la_p[:, i, 0:(i + 1) * P], ps[:, i, 0:(i + 1) * P], ACT.Exp, scale=192.0 ** -0.5, bias=la_mx[:, i:i + 1], accum_out=la_sum[:, i:i + 1]).then_inc(s_probs_exp, 1)
                        fill(FILL["la_probs"][h])
                        if h:
                            tanh_z(4 + h, la_z, la_e)
                        copy_turned(h, la_pt, FILL["la_turned"][h])
                        if h == 0:
                            evacuate(progress.through(G_Z_LA))
                            wait_stored(G_Z_LA)
                            load_z(8, la_z)
                            tanh_z(4, la_z, la_e)
                        keep_y(4 + h, 8 + h, la_yo, la_z)
                        fill(FILL["la_gate"][h])

                    act.wait_ge(s_y_kept, 16 * 8)
                    act.dma_start(ml_const, a["const"][:, ML_CONST[0]:ML_CONST[1]]).then_inc(s_ml_first_loaded, 16)
                    evacuate(progress.through(G_MLO))
                    wait_stored(G_MLO)
                    act.wait_ge(s_ml_cleared, 1)
                    act.dma_start(ml_gate[0:4, :], p_dram[GATES, 0:4]).then_inc(s_ml_first_loaded, 16)
                    act.dma_start(ml_gate[32:36, :], p_dram[GATES, 4:8]).then_inc(s_ml_first_loaded, 16)
                    act.dma_start(ml_v, p_dram[4 * G_MLV:4 * G_MLV + 4].rearrange("j p t -> p j t")).then_inc(s_ml_first_loaded, 16)

                    def load_ml_qk(h):
                        act.dma_start(ml_in[:, 0, 3:T + 3], p_dram[4 * G_MLQ + h]).then_inc(s_ml_qk_loaded, 16)
                        act.dma_start(ml_in[:, 1, 3:T + 3], p_dram[4 * G_MLK + h]).then_inc(s_ml_qk_loaded, 16)

                    def load_ml_o(h):
                        act.dma_start(ml_o, p_dram[4 * G_MLO + h]).then_inc(s_ml_o_loaded, 16)

                    load_ml_qk(0)
                    load_ml_o(0)
                    for h in range(HEADS):
                        if h == 0:
                            act.wait_ge(s_ml_gate_abs, 1)
                            link(nc.scalar.activation(ml_sg[32:36, :], ml_sg[32:36, :], ACT.Exp, scale=-1.0))
                            nc.scalar.activation(ml_sg[32:36, :], ml_sg[32:36, :], ACT.Ln, bias=1.0).then_inc(s_ml_gate_log, 1)
                            fill(FILL["ml_first"])
                        act.wait_ge(s_ml_conv, h + 1)
                        if h < HEADS - 1:
                            load_ml_qk(h + 1)
                        nc.scalar.activation(ml_sil, ml_acc, ACT.Tanh, scale=0.5).then_inc(s_ml_conv_tanh, 1)
                        act.wait_ge(s_ml_o_loaded, 16 * (h + 1))
                        nc.scalar.activation(ml_oe, ml_o, ACT.Tanh, scale=0.5).then_inc(s_ml_o_tanh, 1)
                        if h < HEADS - 1:
                            act.wait_ge(s_ml_o_tanh, h + 1)
                            load_ml_o(h + 1)
                        if h:
                            tanh_z(8 + h, ml_z, ml_e)
                        fill(FILL["ml_qk"][h])
                        act.wait_ge(s_ml_max, h + 1)
                        link(nc.scalar.activation(ml_nf, ml_nf, ACT.Exp))
                        for i in range(NT):
                            nc.scalar.activation(ml_w[:, i, i * P:T], ml_w[:, i, i * P:T], ACT.Exp, scale=-1.0).then_inc(s_ml_w_exp, 1)
                        fill(FILL["ml_s"][h])
                        if h == 0:
                            evacuate(progress.through(G_Z_ML))
                            wait_stored(G_Z_ML)
                            load_z(4, ml_z)
                            tanh_z(8, ml_z, ml_e)
                        fill(FILL["ml_h"][h])
                        act.wait_ge(s_ml_h_sum, h + 1)
                        rstd(ml_rs, ps[:, 2, :], P, EPS).then_inc(s_ml_h_rs, 1)
                        fill(FILL["ml_gate"][h])
                        keep_y(8 + h, 4 + h, ml_yo, ml_z)

                    act.wait_ge(s_y_kept, 16 * 12)
                    evacuate(progress.through(G_DAV))
                    wait_stored(G_DAV)

                    def load_da_qk(h):
                        act.dma_start(da_in[:, 0, :], p_dram[4 * G_DAQ + h]).then_inc(s_da_loaded, 16)
                        act.dma_start(da_in[:, 1, :], p_dram[4 * G_DAK + h]).then_inc(s_da_loaded, 16)

                    load_da_qk(0)
                    act.dma_start(at_const, a["const"][:, ATT_CONST[0]:ATT_CONST[1]]).then_inc(s_da_first_loaded, 16)
                    act.dma_start(da_v, p_dram[4 * G_DAV:4 * G_DAV + 4].rearrange("j p t -> p j t")).then_inc(s_da_first_loaded, 16)
                    fill(FILL["da_first"])
                    for h in range(HEADS):
                        act.wait_ge(s_da_loaded, 32 * (h + 1))
                        link(nc.scalar.activation(da_sq, da_in, ACT.Square))
                        link(nc.scalar.activation(da_g[:, 0, :], da_in[:, 0, :], ACT.Copy, scale=col("da_q_g")))
                        nc.scalar.activation(da_g[:, 1, :], da_in[:, 1, :], ACT.Copy, scale=col("da_k_g")).then_inc(s_da_squared, 1)
                        if h < HEADS - 1:
                            act.wait_ge(s_da_squared, h + 1)
                            load_da_qk(h + 1)
                        if h == 0:
                            act.wait_ge(s_setup_out, 16)
                            act.dma_start(x_tok, x_dram).then_inc(s_x_prefetched, 16)
                            fill(FILL["da_sums"][h])
                        if h == 1:
                            for k in range(EARLY_K + 4):
                                if k >= 4:
                                    act.wait_ge(s_y_loaded[k % 4], 16 * (k // 4))
                                    nc.scalar.activation(h_hi[:, k - 4, :], stage[:, k % 4, :], ACT.Copy
                                                         ).then_inc(s_y_hi_ready, 1)
                                if k < EARLY_K:
                                    if k >= 4:
                                        act.wait_ge(s_y_split, y_count(k - 4))
                                    act.dma_start(stage[:, k % 4, :], y_dram[k]).then_inc(s_y_loaded[k % 4], 16)
                        act.wait_ge(s_da_sums, h + 1)
                        rstd(da_rs, ps[:, 0:2, :], 64, EPS).then_inc(s_da_rs_ready, 1)
                        for half in range(2):
                            if half and h == 0:
                                fill(FILL["da_scores"][h])
                            act.wait_ge(s_da_row_max, 2 * h + half + 1)
                            for b in range(4):
                                i = 2 * half + b // 2
                                nc.scalar.activation(da_p[:, b, 0:(i + 1) * P], ps[:, b, 0:(i + 1) * P], ACT.Exp, scale=64.0 ** -0.5, bias=da_mx[:, b:b + 1], accum_out=da_sum[:, b:b + 1]).then_inc(s_da_probs_exp, 1)
                        if h:
                            tanh_z(12 + h, da_z, da_e)
                        else:
                            fill(FILL["da_half"][h])
                        copy_turned(HEADS + h, da_pt, FILL["da_turned"][h] if h == 0 else 0)
                        act.wait_ge(s_pv_done, HEADS + h + 1)
                        nc.scalar.activation(da_osq, ps[:, 0, :], ACT.Square).then_inc(s_da_osq_ready, 1)
                        if h == 0:
                            fill(FILL["da_osq"][h])
                        act.wait_ge(s_da_osum_mm, h + 1)
                        rstd(da_ors, ps[:, 1, :], P, EPS).then_inc(s_da_ors_ready, 1)
                        if h == 0:
                            evacuate(progress.rest())
                            wait_stored(NG - 1)
                            load_z(12, da_z)
                            tanh_z(12, da_z, da_e)
                            act.wait_ge(s_split_used, STEPS)
                        act.wait_ge(s_y_ready, 12 + h + 1)
                        if h < HEADS - 1:
                            load_z(12 + h + 1, da_z)
                        nc.scalar.activation(h_hi[:, EARLY_K + h, :], da_yo, ACT.Copy).then_inc(s_y_hi_ready, 1)

                    def keep_x(c):
                        act.wait_ge(s_out_added, 16 + 4 * (c + 1))
                        act.dma_start(x_dram[:, :, c * G:(c + 1) * G], x_tok[:, :, c * G:(c + 1) * G]
                                      ).then_inc(s_out_kept, 16)
                        for i in range(NT):
                            link(nc.scalar.activation(x_junk, x_tok[:, i, c * G:(c + 1) * G], ACT.Square,
                                                      accum_out=ms_parts[:, i, c:c + 1]))

                    for n in range(HI_LAST, STEPS + EARLY + LATE):
                        high_part(n)
                        if (n + 1) % LATE_K == 0:
                            keep_x((n - STEPS - EARLY) // LATE_K - 1)
                    keep_x(3)
                    act.wait_ge(s_out_kept, 64)

                @block.vector
                def _(dve):
                    counts = [0]
                    v = nc.vector

                    def link(ins):
                        counts[0] += 1
                        ins.then_inc(s_dve_order, 1)
                        dve.wait_ge(s_dve_order, counts[0])

                    MUL, ADD, SUB, MAX, MIN = ALU.mult, ALU.add, ALU.subtract, ALU.max, ALU.min

                    def gate(n, j, z, e, yo, y):
                        dve.wait_ge(s_z_tanh, n + 1)
                        link(v.scalar_tensor_tensor(out=e, in0=e, scalar=1.0, in1=z, op0=ADD, op1=MUL))
                        if 0 < n <= EARLY_K:
                            dve.wait_ge(s_y_kept, 16 * n)
                        if n > EARLY_K:
                            dve.wait_ge(s_y_split, n)
                        v.scalar_tensor_tensor(out=yo, in0=y, scalar=half_beta[:, j:j + 1], in1=e, op0=MUL, op1=MUL
                                               ).then_inc(s_y_ready, 1)
                        dve.wait_ge(s_y_ready, n + 1)

                    v.tensor_reduce(ms, ms_parts, AX, ADD).then_inc(s_x_squares, 1)

                    dve.wait_ge(s_params_loaded, 16)
                    v.tensor_copy(par[:], par_all[:, layer, :]).then_inc(s_par_ready, 1)
                    dve.wait_ge(s_par_ready, 1)
                    v.tensor_tensor(lam_prod[0:64, :], lam4[0:64, 0:4:2], lam4[0:64, 1:4:2], MUL).then_inc(s_lam_ready, 1)
                    for dst, name in ((half_w0, "rw_w0"), (half_a0, "rw_a0"), (half_v0, "rw_v0"),
                                      (half_ka, "rw_k_a"), (half_ml_g, "ml_norm_g")):
                        link(v.tensor_scalar(dst, par[:, COLS[name]:COLS[name] + 4], 0.5, None, MUL))
                    link(v.tensor_scalar(half_beta, beta, 0.5, None, MUL))
                    link(v.tensor_scalar(one_m_half_ka, half_ka, -1.0, 1.0, MUL, ADD))
                    link(v.tensor_tensor(sub_gain, col("da_sub_g"), one_m_lam_init, MUL))

                    dve.wait_ge(s_x_mean, 1)
                    for i in range(2, NT):
                        v.tensor_scalar(x_tok[:, i, :], x_tok[:, i, :], rs_x[:, i:i + 1], None, MUL).then_inc(s_x_scaled, 1)
                    for k in range(KT):
                        dve.wait_ge(s_h_hi_ready, k + 1)
                        v.scalar_tensor_tensor(out=h_lo[:, k, :], in0=ps[:, k % 4, :], scalar=col("norm_g", k), in1=h_hi[:, k, :].bitcast(F32), op0=MUL, op1=SUB).then_inc(s_h_split, 1)
                    dve.wait_ge(s_da_lam_exp, 1)
                    link(v.tensor_tensor(neg_lam, lam2[:, 1:2], lam2[:, 0:1], SUB))
                    v.tensor_tensor(neg_lam, neg_lam, lam_init, SUB).then_inc(s_small_ready, 1)

                    def shift(x, mu, rows_=slice(0, P)):
                        link(v.tensor_tensor(rw_d[rows_, :], x[rows_, 0:T], x[rows_, 1:T + 1], SUB))
                        return v.scalar_tensor_tensor(out=x[rows_, 1:T + 1], in0=rw_d[rows_, :],
                                                      scalar=mu[rows_, :], in1=x[rows_, 1:T + 1], op0=MUL, op1=ADD)

                    dve.wait_ge(s_x_turned, KT)
                    link(v.memset(rw_lora[0:64, 0:1], 0.0))
                    link(v.memset(rw_in[:, :, 0:1], 0.0))
                    link(v.memset(rw_v[:, :, 0:1], 0.0))
                    dve.wait_ge(s_rw_first_loaded, 16 * 8)
                    shift(rw_lora, col("rw_mu", 12), slice(0, 64)).then_inc(s_rw_shifted, 1)
                    dve.wait_ge(s_rw_shifted, 1)
                    for j in range(4):
                        ins = shift(rw_v[:, j, :], col("rw_mu", 8 + j))
                        if j < 3:
                            link(ins)
                    ins.then_inc(s_rw_v_shifted, 1)
                    dve.wait_ge(s_rw_vdn_mm, 1)
                    v.tensor_copy(rw_vd[0:32, :], ps[0:32, 0, :]).then_inc(s_rw_vd_ready, 1)
                    for hp in range(4):
                        r, k, vv = rw_in[:, 0, 1:T + 1], rw_in[:, 1, 1:T + 1], rw_v[:, hp, 1:T + 1]
                        dve.wait_ge(s_rw_rk_loaded, 32 * (hp + 1))
                        for x, mu in ((rw_in[:, 0, :], col("rw_mu", hp)), (rw_in[:, 1, :], col("rw_mu", 4 + hp))):
                            link(v.tensor_tensor(rw_kf, x[:, 0:T], x[:, 1:T + 1], SUB))
                            link(v.scalar_tensor_tensor(out=x[:, 1:T + 1], in0=rw_kf, scalar=mu, in1=x[:, 1:T + 1], op0=MUL, op1=ADD))
                        link(v.tensor_scalar(rw_kk, k, col("rw_k_k", hp), None, MUL))
                        v.tensor_tensor(rw_sq, rw_kk, rw_kk, MUL).then_inc(s_rw_kk_sq, 1)
                        dve.wait_ge(s_rw_sig_tanh, hp + 1)
                        decay, rate, mix = rw_t[:, 0, :], rw_t[:, 1, :], rw_t[:, 2, :]
                        link(v.tensor_scalar(decay, decay, -0.5 * math.exp(-0.5), -0.5 * math.exp(-0.5), MUL, ADD))
                        link(v.tensor_tensor_scan(rw_c, reset, decay, 0.0, MUL, ADD))
                        v.tensor_tensor(rw_cm, rw_c, decay, SUB).then_inc(s_rw_decay, 1)
                        dve.wait_ge(s_rw_decay, hp + 1)
                        link(v.tensor_tensor(decay, v_first[:, hp, :], vv, SUB))
                        link(v.scalar_tensor_tensor(out=decay, in0=mix, scalar=1.0, in1=decay, op0=ADD, op1=MUL))
                        link(v.scalar_tensor_tensor(out=vv, in0=decay, scalar=half_flag, in1=vv, op0=MUL, op1=ADD))
                        link(v.tensor_copy(v_first[:, hp, :], vv))
                        link(v.tensor_scalar(rw_kf, rate, half_ka[:, hp:hp + 1], one_m_half_ka[:, hp:hp + 1], MUL, ADD))
                        link(v.tensor_tensor(rw_kf, rw_kf, k, MUL))
                        dve.wait_ge(s_rw_kk_root, hp + 1)
                        link(v.tensor_scalar(rw_nr, rw_nr, 1e-12, None, MAX))
                        link(v.reciprocal(rw_nr, rw_nr))
                        link(v.tensor_tensor(rw_kk, rw_kk, rw_nr, MUL))
                        link(v.scalar_tensor_tensor(out=rw_sq, in0=r, scalar=col("rw_r_k", hp), in1=rw_kf, op0=MUL, op1=MUL))
                        dve.wait_ge(s_rw_decay_exp, hp + 1)
                        by_tile = "p (i t) -> p i t"
                        link(v.tensor_tensor(rw_ar[:, :, 0, :], rw_wm.rearrange(by_tile, i=NT), rw_kk.rearrange(by_tile, i=NT), MUL))
                        link(v.tensor_tensor(rw_ar[:, :, 1, :], rw_w.rearrange(by_tile, i=NT), r.rearrange(by_tile, i=NT), MUL))
                        link(v.scalar_tensor_tensor(out=rw_beta, in0=rate, scalar=1.0, in1=rw_kk, op0=ADD, op1=MUL))
                        link(v.scalar_tensor_tensor(out=rw_beta, in0=rw_beta, scalar=0.5, in1=rw_wi, op0=MUL, op1=MUL))
                        link(v.tensor_tensor(rw_kappa, rw_kf, rw_wi, MUL))
                        by_chunk = "p (c t) -> p c t"
                        link(v.tensor_copy(rw_wl, rw_w.rearrange(by_chunk, c=NCH)[:, :, 63]))
                        last_w = rw_wl[:, :, None].to_broadcast([P, NCH, 64])
                        link(v.scalar_tensor_tensor(out=rw_bn.rearrange(by_chunk, c=NCH), in0=rw_beta.rearrange(by_chunk, c=NCH), scalar=-1.0, in1=last_w, op0=MUL, op1=MUL))
                        v.tensor_tensor(rw_kt.rearrange(by_chunk, c=NCH), rw_kappa.rearrange(by_chunk, c=NCH), last_w, MUL).then_inc(s_rw_factors, 1)
                        dve.wait_ge(s_rw_turned, hp + 1)
                        v.tensor_tensor(rw_bonus, ps[:, 3, :], vv, MUL).then_inc(s_rw_bonus_ready, 1)
                        for ip in range(2):
                            dve.wait_ge(s_rw_gram, 2 * hp + ip + 1)
                            for f, (dst, mask) in enumerate(((rw_gb, mask_b), (rw_gk, mask_k))):
                                for h in range(2):
                                    ins = v.tensor_tensor(dst[:, 4 * h + 2 * ip:4 * h + 2 * ip + 2, :], ps[:, 2 * f + h, :].rearrange("p (i c) -> p i c", i=2), mask[:, None, :].to_broadcast([P, 2, 256]), MUL)
                                    if f and h:
                                        ins.then_inc(s_rw_gram_masked, 1)
                                    else:
                                        link(ins)
                        for h in range(2):
                            j = slice(4 * h, 4 * h + 4)
                            link(v.tensor_tensor(rw_xt[:, j, :], rw_gb[:, j, 0:P], level1[:, None, :].to_broadcast([P, NT, P]), MUL))
                            ins = v.tensor_tensor(rw_xt[:, j, :], ident[:, None, :].to_broadcast([P, NT, P]), rw_xt[:, j, :], SUB)
                            if h:
                                ins.then_inc(s_rw_xt_first, 1)
                            else:
                                link(ins)
                        for lv in range(len(LEVELS)):
                            level_mask = levels[:, lv * P:(lv + 1) * P][:, None, :].to_broadcast([P, NT, P])
                            for h in range(2):
                                dve.wait_ge(s_rw_levelled, 10 * hp + 2 * lv + h + 1)
                                v.tensor_tensor(rw_y[:, 4 * h:4 * h + 4, :], ps[:, 2 * h, :].rearrange("p (i c) -> p i c", i=NT), level_mask, MUL).then_inc(s_rw_level_masked, 1)
                            for h in range(2):
                                dve.wait_ge(s_rw_level_mm, 10 * hp + 2 * lv + h + 1)
                                j = slice(4 * h, 4 * h + 4)
                                if lv < len(LEVELS) - 1:
                                    link(v.tensor_tensor(rw_x[:, j, :], rw_x[:, j, :], ps[:, 2 * h, :].rearrange("p (i c) -> p i c", i=NT), SUB))
                                v.tensor_tensor(rw_xt[:, j, :], rw_xt[:, j, :], ps[:, 2 * h + 1, :].rearrange("p (i c) -> p i c", i=NT), SUB).then_inc(s_rw_level_done, 1)
                        dve.wait_ge(s_rw_local, hp + 1)
                        link(v.tensor_tensor(rw_ar[:, :, 1, :], rw_ar[:, :, 1, :], ps[:, 2, :].rearrange(by_tile, i=NT), ADD))
                        link(v.tensor_copy(rw_yl, ps[:, 3, :]))
                        link(v.tensor_tensor(rw_wli, eye64[:, None, :].to_broadcast([P, NCH, 64]), last_w, MUL))
                        dve.wait_ge(s_rw_h_copied, 2 * hp + 2)
                        for q in range(2):
                            link(v.tensor_tensor(rw_gt[:, q:NCH:2, :], rw_wli[:, q:NCH:2, :], ps[:, q, :].rearrange("p (i s c) -> p i s c", i=NT, s=2)[:, :, 0, :], ADD))
                        v.memset(rw_st[:, 0, :], 0.0).then_inc(s_rw_local_ready, 1)
                        for c in range(1, NCH - 1):
                            dve.wait_ge(s_rw_state_mm, (NCH - 2) * hp + c)
                            for h in range(2):
                                half = slice(64 * h, 64 * h + 64)
                                ins = v.tensor_tensor(rw_st[half, c + 1, :], rw_st[half, c + 1, :], ps[half, h, c * 64:(c + 1) * 64], ADD)
                                if h:
                                    ins.then_inc(s_rw_state_ready, 1)
                                else:
                                    link(ins)
                        dve.wait_ge(s_rw_carried, hp + 1)
                        for h in range(2):
                            half = slice(64 * h, 64 * h + 64)
                            ins = v.tensor_tensor(rw_yl[half, :], rw_yl[half, :], ps[half, 2 + h, :], ADD)
                            if h:
                                ins.then_inc(s_rw_y_whole, 1)
                            else:
                                link(ins)
                        dve.wait_ge(s_rw_mean, hp + 1)
                        link(v.scalar_tensor_tensor(out=rw_yl, in0=ps[:, 0, :], scalar=-1.0 / 64, in1=rw_yl, op0=MUL, op1=ADD))
                        v.tensor_tensor(rw_sq, rw_yl, rw_yl, MUL).then_inc(s_rw_centred, 1)
                        dve.wait_ge(s_rw_rstd, hp + 1)
                        link(v.tensor_tensor(rw_yl, rw_yl, rw_nr, MUL))
                        link(v.tensor_scalar(rw_yl, rw_yl, col("rw_ln_w", hp), col("rw_ln_b", hp), MUL, ADD))
                        link(v.tensor_tensor(rw_yl, rw_yl, rw_bonus, ADD))
                        gate(hp, 0, rw_z, rw_e, rw_yo, rw_yl)

                    dve.wait_ge(s_la_loaded, 16 * 6)
                    link(v.tensor_tensor(la_sq, la_in, la_in, MUL))
                    pe64 = slice(0, 64)
                    link(v.tensor_scalar(la_peg[pe64, :], la_pe[pe64, :], col("mla_k_g", 1)[pe64, :], None, MUL))
                    v.tensor_tensor(la_pesq[pe64, :], la_pe[pe64, :], la_pe[pe64, :], MUL).then_inc(s_la_squared, 1)
                    dve.wait_ge(s_la_rs_ready, 1)
                    for j in range(5):
                        gain = col("mla_q_norm_g", j) if j < 3 else col("mla_kv_norm_g", j - 3)
                        link(v.scalar_tensor_tensor(out=la_in[:, j, :], in0=la_in[:, j, :], scalar=gain, in1=la_rs[:, int(j > 2), :], op0=MUL, op1=MUL))
                    link(v.tensor_tensor(la_tmp[pe64, :], ps[pe64, 2, :], sin_mla[pe64, :], MUL))
                    link(v.tensor_tensor(la_per[pe64, :], la_peg[pe64, :], cos_mla[pe64, :], MUL))
                    v.tensor_tensor(la_per[pe64, :], la_per[pe64, :], la_tmp[pe64, :], ADD).then_inc(s_la_latents, 1)

                    def row_maxima(mx, banks, scale):
                        for b, i in banks:
                            link(v.tensor_reduce(mx[:, b:b + 1], ps[:, b, 0:(i + 1) * P], AX, MAX))
                        return v.tensor_scalar(mx, mx, -scale, None, MUL)

                    for h in range(HEADS):
                        dve.wait_ge(s_la_heads_sums, h + 1)
                        link(v.tensor_tensor(la_tmp[pe64, :], ps[pe64, 1, :], sin_mla[pe64, :], MUL))
                        link(v.tensor_tensor(la_qp[pe64, :], la_qp[pe64, :], cos_mla[pe64, :], MUL))
                        link(v.tensor_tensor(la_qp[pe64, :], la_qp[pe64, :], la_tmp[pe64, :], ADD))
                        dve.wait_ge(s_la_heads_rs, h + 1)
                        link(v.tensor_tensor(la_qp[pe64, :], la_qp[pe64, :], la_rs[pe64, 0, :], MUL))
                        link(v.tensor_tensor(la_kp[pe64, :], la_per[pe64, :], la_rs[pe64, 1, :], MUL))
                        link(v.tensor_tensor(la_q, la_q, la_rs[:, 0, :], MUL))
                        v.tensor_tensor(la_k, la_k, la_rs[:, 1, :], MUL).then_inc(s_la_qk_ready, 1)
                        dve.wait_ge(s_scores_mm, NT * (h + 1))
                        row_maxima(la_mx, [(i, i) for i in range(NT)], 192.0 ** -0.5).then_inc(s_row_max, 1)
                        dve.wait_ge(s_probs_exp, NT * (h + 1))
                        link(v.reciprocal(la_sum, la_sum))
                        for i in range(NT):
                            ins = v.tensor_scalar(la_p[:, i, 0:(i + 1) * P], la_p[:, i, 0:(i + 1) * P], la_sum[:, i:i + 1], None, MUL)
                            if i == NT - 1:
                                ins.then_inc(s_probs_ready, 1)
                            else:
                                link(ins)
                        dve.wait_ge(s_pv_done, h + 1)
                        gate(4 + h, 2, la_z, la_e, la_yo, ps[:, 0, :])

                    link(v.memset(ml_gate, 0.0))
                    v.memset(ml_in[:, :, 0:3], 0.0).then_inc(s_ml_cleared, 1)
                    dve.wait_ge(s_ml_first_loaded, 16 * 4)
                    gates, forget = slice(0, 36), slice(32, 36)
                    link(v.tensor_scalar(ml_gt[gates, :], ml_gate[gates, :], gate_bias[gates, :], None, ADD))
                    v.scalar_tensor_tensor(out=ml_sg[forget, :], in0=ml_gt[forget, :], scalar=-1.0, in1=ml_gt[forget, :], op0=MUL, op1=MAX).then_inc(s_ml_gate_abs, 1)
                    dve.wait_ge(s_ml_gate_log, 1)
                    link(v.scalar_tensor_tensor(out=ml_sg[forget, :], in0=ml_gt[forget, :], scalar=0.0, in1=ml_sg[forget, :], op0=MIN, op1=SUB))
                    v.tensor_tensor_scan(ml_gt[forget, :], carry[forget, :], ml_sg[forget, :], 0.0, MUL, ADD).then_inc(s_ml_gates, 1)
                    dve.wait_ge(s_ml_ucol_mm, 1)
                    v.tensor_copy(ml_ucol, ps[:, 3, 0:4 * NT].rearrange("p (i h) -> p i h", i=NT)).then_inc(s_ml_ucol_ready, 1)

                    def convolve(h):
                        dve.wait_ge(s_ml_qk_loaded, 32 * (h + 1))
                        for s, n in ((0, h), (1, 4 + h)):
                            link(v.tensor_scalar(ml_acc[:, s, :], ml_in[:, s, 3:T + 3], col("ml_conv_w", 24 + n), col("ml_conv_b", n), MUL, ADD))
                            for tap in (2, 1, 0):
                                ins = v.scalar_tensor_tensor(out=ml_acc[:, s, :], in0=ml_in[:, s, tap:tap + T], scalar=col("ml_conv_w", 8 * tap + n), in1=ml_acc[:, s, :], op0=MUL, op1=ADD)
                                if s and not tap:
                                    ins.then_inc(s_ml_conv, 1)
                                else:
                                    link(ins)

                    convolve(0)
                    for h in range(HEADS):
                        dve.wait_ge(s_ml_u_mm, h + 1)
                        link(v.tensor_tensor_scan(ml_m, carry, ps[:, 0, :], 0.0, MUL, MAX))
                        link(v.scalar_tensor_tensor(out=ml_nf, in0=ps[:, 1, :], scalar=-1.0, in1=ml_m, op0=MUL, op1=SUB))
                        for i in range(NT):
                            ins = v.tensor_scalar(ml_w[:, i, i * P:T], ml_m[:, i * P:T], ml_ucol[:, i, h:h + 1], 0.0, SUB, MAX)
                            if i == NT - 1:
                                ins.then_inc(s_ml_max, 1)
                            else:
                                link(ins)
                        dve.wait_ge(s_ml_conv_tanh, h + 1)
                        v.scalar_tensor_tensor(out=ml_acc, in0=ml_sil, scalar=1.0, in1=ml_acc, op0=ADD, op1=MUL).then_inc(s_ml_qk_ready, 1)
                        dve.wait_ge(s_ml_scores_mm, h + 1)
                        dve.wait_ge(s_ml_w_exp, NT * (h + 1))
                        for i in range(NT):
                            link(v.scalar_tensor_tensor(out=ml_s[:, i, i * P:T], in0=ps[:, i, i * P:T], scalar=0.25 * float(P) ** -0.5, in1=ml_w[:, i, i * P:T], op0=MUL, op1=MUL))
                            ins = v.tensor_tensor(ml_s[:, i, i * P:(i + 1) * P], ml_s[:, i, i * P:(i + 1) * P], causal, MUL)
                            if i == NT - 1:
                                ins.then_inc(s_ml_s_ready, 1)
                            else:
                                link(ins)
                        if h < HEADS - 1:
                            convolve(h + 1)
                        dve.wait_ge(s_ml_num_mm, h + 1)
                        link(v.scalar_tensor_tensor(out=ml_den, in0=ps[:, 1, :], scalar=-1.0, in1=ml_nf, op0=MUL, op1=MAX))
                        link(v.tensor_tensor(ml_den, ps[:, 1, :], ml_den, MAX))
                        link(v.reciprocal(ml_den, ml_den))
                        link(v.tensor_tensor(ml_h, ps[:, 0, :], ml_den, MUL))
                        v.tensor_tensor(ml_sq, ml_h, ml_h, MUL).then_inc(s_ml_h_sq, 1)
                        dve.wait_ge(s_ml_o_tanh, h + 1)
                        dve.wait_ge(s_ml_h_rs, h + 1)
                        link(v.scalar_tensor_tensor(out=ml_h, in0=ml_h, scalar=half_ml_g[:, h:h + 1], in1=ml_rs, op0=MUL, op1=MUL))
                        link(v.scalar_tensor_tensor(out=ml_h, in0=ml_oe, scalar=1.0, in1=ml_h, op0=ADD, op1=MUL))
                        gate(8 + h, 1, ml_z, ml_e, ml_yo, ml_h)

                    def split_y(k, y):
                        dve.wait_ge(s_y_hi_ready, y_count(k))
                        v.tensor_tensor(h_lo[:, k, :], y, h_hi[:, k, :].bitcast(F32), SUB).then_inc(s_y_split, 1)

                    def add_out(c, bank, steps):
                        for i in range(NT):
                            if i < 3:
                                dve.wait_ge(s_out_done, 3 * taken[0] + i + 1)
                            else:
                                dve.wait_ge(s_split_used, steps)
                            part = x_tok[:, i, c * G:(c + 1) * G]
                            v.tensor_tensor(part, part, bank[:, i, :], ADD).then_inc(s_out_added, 1)
                        taken[0] += 1

                    def fill_out(n=1):
                        for c in early_ended(early.ahead(n)):
                            if c == 0:
                                dve.wait_ge(s_x_prefetched, 16)
                            add_out(c, ps_proj, STEPS + EARLY_K * (c + 1))

                    early, taken = Progress(STEPS, STEPS + EARLY), [0]
                    dve.wait_ge(s_da_first_loaded, 32)
                    for h in range(HEADS):
                        if h == 1:
                            for k in range(EARLY_K):
                                split_y(k, stage[:, k % 4, :])
                        dve.wait_ge(s_da_sums, h + 1)
                        wide_sin, wide_cos = (t[:, None, :].to_broadcast([P, 2, T]) for t in (sin_da, cos_da))
                        link(v.tensor_tensor(da_qk, ps[:, 2:4, :], wide_sin, MUL))
                        link(v.tensor_tensor(da_g, da_g, wide_cos, MUL))
                        link(v.tensor_tensor(da_g, da_g, da_qk, ADD))
                        dve.wait_ge(s_da_rs_ready, h + 1)
                        v.tensor_tensor(da_g, da_g, da_rs, MUL).then_inc(s_da_qk_ready, 1)
                        fill_out(FILL["da_sums"][h] if h else 0)
                        for f in range(2):
                            if f:
                                fill_out(FILL["da_scores"][h] if h else 0)
                            dve.wait_ge(s_da_scores_mm, 2 * h + f + 1)
                            row_maxima(da_mx, [(b, 2 * f + b // 2) for b in range(4)], 64.0 ** -0.5).then_inc(s_da_row_max, 1)
                            dve.wait_ge(s_da_probs_exp, 8 * h + 4 * f + 4)
                            link(v.reciprocal(da_sum, da_sum))
                            link(v.tensor_scalar(da_sum[:, 1:4:2], da_sum[:, 1:4:2], neg_lam, None, MUL))
                            for i in (2 * f, 2 * f + 1):
                                b, ks = 2 * (i % 2), slice(0, (i + 1) * P)
                                link(v.tensor_scalar(da_a[:, i, ks], da_p[:, b, ks], da_sum[:, b:b + 1], None, MUL))
                                ins = v.scalar_tensor_tensor(out=da_a[:, i, ks], in0=da_p[:, b + 1, ks], scalar=da_sum[:, b + 1:b + 2], in1=da_a[:, i, ks], op0=MUL, op1=ADD)
                                if i % 2:
                                    ins.then_inc(s_da_half, 1)
                                else:
                                    link(ins)
                        fill_out(FILL["da_half"][h] if h else 0)
                        fill_out(FILL["da_turned"][h] if h else 0)
                        dve.wait_ge(s_da_ors_ready, h + 1)
                        link(v.scalar_tensor_tensor(out=da_o, in0=ps[:, 0, :], scalar=sub_gain, in1=da_ors, op0=MUL, op1=MUL))
                        gate(12 + h, 3, da_z, da_e, da_yo, da_o)
                        split_y(EARLY_K + h, da_yo)
                        fill_out(FILL["da_osq"][h] if h else 0)
                        fill_out((0, FILL["da_gate"][h], FILL["da_gate"][h], EARLY)[h])

                    link(v.memset(half_flag, 0.5))
                    link(v.memset(lam_init, 0.8 - 0.6 * math.exp(-0.3)))
                    link(v.memset(one_m_lam_init, 1.0 - (0.8 - 0.6 * math.exp(-0.3))))

                    for c in range(4):
                        add_out(c, (ps, ps_proj)[c % 2], STEPS + EARLY + LATE_K * (c + 1))

            nc.all_engine_barrier(sems_to_clear=of_layer)


_INS = ["x", "w_in", "w_out", "rw_w_up", "rw_a_up", "rw_v_dn", "rw_v_up", "mla_w_q_b", "mla_w_kv_b"]
_OUT = ((1, T, D), "float32")


def kernel(**inputs):
    import concourse.bacc as _bacc
    from concourse.bass_utils import run_bass_kernel_spmd as _run

    nc = _bacc.Bacc("TRN2", target_bir_lowering=False, num_devices=1)
    arrays, args = {}, {}
    given = {name: np.ascontiguousarray(inputs[name]) for name in _INS}
    given["params"] = parameters(inputs)
    given["const"] = constants()
    for name, a in given.items():
        arrays[f"in_{name}_dram"] = a
        args[name] = nc.dram_tensor(f"in_{name}_dram", a.shape, mybir.dt.from_np(a.dtype), kind="ExternalInput").ap()
    out = nc.dram_tensor("out_0_dram", _OUT[0], mybir.dt.from_np(np.dtype(_OUT[1])), kind="ExternalOutput").ap()
    build(nc, args, out)
    r = _run(nc, [arrays], core_ids=[0])
    return r.results[0]["out_0_dram"]
```
